# Optimizing a Trainium2 kernel written in Bass

```python
import jax
import jax.numpy as jnp
from jax import lax
import numpy as np

D_MODEL = 1024
BATCH = 1
SEQ = 1024
DEPTH = 2
DEC_BATCH = 8
DEC_SEQ = 16
PAST_LEN = 1024

CHUNK = 64
N_META = 16
Q_BLOCK = 128
ROPE_THETA = 10000.0
MIX_WIDTH = D_MODEL
MLA_HEADS = 8
MLA_Q_LORA = 256
MLA_KV_LORA = 128
MLA_NOPE = 64
MLA_ROPE = 32
MLA_V = 64
MLA_OUT = MLA_HEADS * MLA_V
SWA_HEADS = 8
SWA_KV_HEADS = 2
SWA_HEAD_DIM = 64
SWA_GROUP = SWA_HEADS // SWA_KV_HEADS
SWA_OUT = SWA_HEADS * SWA_HEAD_DIM
WINDOW = 128
BAND_CHUNKS = WINDOW // CHUNK
D_FF = ((8 * D_MODEL + 3 * 256 - 1) // (3 * 256)) * 256
IN_SPLITS = (MLA_Q_LORA,
             MLA_Q_LORA + MLA_KV_LORA,
             MLA_Q_LORA + MLA_KV_LORA + MLA_ROPE,
             MLA_Q_LORA + MLA_KV_LORA + MLA_ROPE + SWA_OUT,
             MLA_Q_LORA + MLA_KV_LORA + MLA_ROPE + SWA_OUT + SWA_KV_HEADS * SWA_HEAD_DIM)
IN_WIDTH = IN_SPLITS[-1] + SWA_KV_HEADS * SWA_HEAD_DIM
ALPHA = (2.0 * DEPTH) ** 0.25
BETA = (8.0 * DEPTH) ** -0.25
MLA_SCALE = (MLA_NOPE + MLA_ROPE) ** -0.5
SWA_SCALE = SWA_HEAD_DIM ** -0.5
NEG_INF = -1e30
LN_EPS = 1e-5
RMS_EPS = 1e-6

kernel_name = 'hymba_mla_swa_sink_streaming_encoder'

def layer_norm(x, g, b):
    xf = x.astype(jnp.float32)
    mu = jnp.mean(xf, axis=-1, keepdims=True)
    var = jnp.mean(jnp.square(xf - mu), axis=-1, keepdims=True)
    return ((xf - mu) * lax.rsqrt(var + LN_EPS) * g.astype(jnp.float32) + b.astype(jnp.float32)).astype(x.dtype)

def rms_norm(x, g):
    xf = x.astype(jnp.float32)
    ms = jnp.mean(jnp.square(xf), axis=-1, keepdims=True)
    return (xf * lax.rsqrt(ms + RMS_EPS) * g.astype(jnp.float32)).astype(x.dtype)

def rope(x, pos):
    d = x.shape[-1]
    half = d // 2
    inv = jnp.power(ROPE_THETA, -(jnp.arange(half, dtype=jnp.float32) * (2.0 / d)))
    ang = pos.astype(jnp.float32)[:, None] * inv[None, :]
    ang = ang.reshape((pos.shape[0],) + (1,) * (x.ndim - 3) + (half,))
    cos, sin = jnp.cos(ang), jnp.sin(ang)
    xf = x.astype(jnp.float32)
    x1, x2 = xf[..., :half], xf[..., half:]
    return jnp.concatenate([x1 * cos - x2 * sin, x2 * cos + x1 * sin], axis=-1).astype(x.dtype)

def _project(h, pos, w_in, q_g, w_uq, w_uk, kv_g):
    b, t, _ = h.shape
    z = jnp.einsum('btd,de->bte', h, w_in)
    cq, ckv, kr, sq, sk, sv = jnp.split(z, IN_SPLITS, axis=-1)
    q = jnp.einsum('btr,rhe->bthe', rms_norm(cq, q_g), w_uq)
    q_lat = jnp.einsum('bthn,lhn->bthl', q[..., :MLA_NOPE], w_uk)
    q_rope = rope(q[..., MLA_NOPE:], pos)
    ckv = rms_norm(ckv, kv_g)
    kr = rope(kr, pos)
    sq = rope(sq.reshape(b, t, SWA_KV_HEADS, SWA_GROUP, SWA_HEAD_DIM), pos)
    sk = rope(sk.reshape(b, t, SWA_KV_HEADS, SWA_HEAD_DIM), pos)
    sv = sv.reshape(b, t, SWA_KV_HEADS, SWA_HEAD_DIM)
    return q_lat, q_rope, ckv, kr, sq, sk, sv

def _mla_attend(q_lat, q_rope, ckv, kr, mask):
    s = (jnp.einsum('bqhl,bkl->bhqk', q_lat, ckv).astype(jnp.float32)
         + jnp.einsum('bqhr,bkr->bhqk', q_rope, kr).astype(jnp.float32)) * MLA_SCALE
    if mask is not None:
        s = jnp.where(mask, s, NEG_INF)
    p = jax.nn.softmax(s, axis=-1).astype(ckv.dtype)
    return jnp.einsum('bhqk,bkl->bqhl', p, ckv)

def _swa_attend(q, k, v, sinks, key_mask):
    s = jnp.einsum('...qkgd,...skd->...kgqs', q, k).astype(jnp.float32) * SWA_SCALE
    if key_mask is not None:
        s = jnp.where(key_mask[..., None, None, None, :], s, NEG_INF)
    sink = jnp.broadcast_to(sinks.astype(jnp.float32).reshape(SWA_KV_HEADS, SWA_GROUP, 1, 1),
                            s.shape[:-1] + (1,))
    p = jax.nn.softmax(jnp.concatenate([s, sink], axis=-1), axis=-1)[..., :-1].astype(v.dtype)
    o = jnp.einsum('...kgqs,...skd->...qkgd', p, v)
    return o.reshape(o.shape[:-3] + (SWA_OUT,))

def _block_out(x, o_lat, o_swa, p):
    (_, _, _, _, _, w_uv, _, g_a, g_b, w_out, ln1_g, ln1_b, wg, wu, wd, ln2_g, ln2_b) = p
    b, t, _ = x.shape
    o_a = jnp.einsum('bthl,lhv->bthv', o_lat, w_uv).reshape(b, t, MLA_OUT)
    mix = jnp.concatenate([rms_norm(o_a, g_a), rms_norm(o_swa, g_b)], axis=-1)
    x = layer_norm(ALPHA * x + jnp.einsum('btm,md->btd', mix, w_out), ln1_g, ln1_b)
    hid = jax.nn.silu(jnp.einsum('btd,df->btf', x, wg)) * jnp.einsum('btd,df->btf', x, wu)
    return layer_norm(ALPHA * x + jnp.einsum('btf,fd->btd', hid, wd), ln2_g, ln2_b)

def _prompt_layer(x, p):
    (w_in, q_g, w_uq, kv_g, w_uk, _, sinks) = p[:7]
    b, t, _ = x.shape
    seq = t - N_META
    pos = jnp.arange(t, dtype=jnp.int32)
    q_lat, q_rope, ckv, kr, sq, sk, sv = _project(x, pos, w_in, q_g, w_uq, w_uk, kv_g)
    o_meta = _mla_attend(q_lat[:, :N_META], q_rope[:, :N_META], ckv[:, :N_META], kr[:, :N_META], None)
    nb = seq // Q_BLOCK
    ql = jnp.moveaxis(q_lat[:, N_META:].reshape(b, nb, Q_BLOCK, MLA_HEADS, MLA_KV_LORA), 1, 0)
    qr = jnp.moveaxis(q_rope[:, N_META:].reshape(b, nb, Q_BLOCK, MLA_HEADS, MLA_ROPE), 1, 0)
    key_chunk = (jnp.arange(t, dtype=jnp.int32) - N_META) // CHUNK

    def mla_block(args):
        i, ql_i, qr_i = args
        q_chunk = (i * Q_BLOCK + jnp.arange(Q_BLOCK, dtype=jnp.int32)) // CHUNK
        mask = key_chunk[None, :] <= q_chunk[:, None]
        return _mla_attend(ql_i, qr_i, ckv, kr, mask)

    o_frames = lax.map(mla_block, (jnp.arange(nb, dtype=jnp.int32), ql, qr))
    o_frames = jnp.moveaxis(o_frames, 0, 1).reshape(b, seq, MLA_HEADS, MLA_KV_LORA)
    o_lat = jnp.concatenate([o_meta, o_frames], axis=1)
    nc = seq // CHUNK
    qc = sq[:, N_META:].reshape(b, nc, CHUNK, SWA_KV_HEADS, SWA_GROUP, SWA_HEAD_DIM)
    kc = sk[:, N_META:].reshape(b, nc, CHUNK, SWA_KV_HEADS, SWA_HEAD_DIM)
    vc = sv[:, N_META:].reshape(b, nc, CHUNK, SWA_KV_HEADS, SWA_HEAD_DIM)
    pad = ((0, 0), (BAND_CHUNKS, 0), (0, 0), (0, 0), (0, 0))
    kp, vp = jnp.pad(kc, pad), jnp.pad(vc, pad)
    meta_shape = (b, nc, N_META, SWA_KV_HEADS, SWA_HEAD_DIM)
    k_band = jnp.concatenate([jnp.broadcast_to(sk[:, None, :N_META], meta_shape)]
                             + [kp[:, r:r + nc] for r in range(BAND_CHUNKS + 1)], axis=2)
    v_band = jnp.concatenate([jnp.broadcast_to(sv[:, None, :N_META], meta_shape)]
                             + [vp[:, r:r + nc] for r in range(BAND_CHUNKS + 1)], axis=2)
    slot_ok = (jnp.arange(nc)[:, None] + jnp.arange(BAND_CHUNKS + 1)[None, :]) >= BAND_CHUNKS
    key_mask = jnp.concatenate([jnp.ones((nc, N_META), dtype=bool),
                                jnp.repeat(slot_ok, CHUNK, axis=1)], axis=1)
    o_band = _swa_attend(qc, k_band, v_band, sinks, key_mask).reshape(b, seq, SWA_OUT)
    o_swa_meta = _swa_attend(sq[:, :N_META], sk[:, :N_META], sv[:, :N_META], sinks, None)
    o_swa = jnp.concatenate([o_swa_meta, o_band], axis=1)
    y = _block_out(x, o_lat, o_swa, p)
    buf = min(WINDOW, seq)
    k_buf = jnp.concatenate([sk[:, :N_META], sk[:, t - buf:]], axis=1)
    v_buf = jnp.concatenate([sv[:, :N_META], sv[:, t - buf:]], axis=1)
    return y, (ckv, kr, k_buf, v_buf)

def _sample_layer(x, ckv_c, kr_c, k_c, v_c, p):
    (w_in, q_g, w_uq, kv_g, w_uk, _, sinks) = p[:7]
    b, t, _ = x.shape
    past = ckv_c.shape[1] - N_META
    pos = N_META + past + jnp.arange(t, dtype=jnp.int32)
    q_lat, q_rope, ckv, kr, sq, sk, sv = _project(x, pos, w_in, q_g, w_uq, w_uk, kv_g)
    o_lat = _mla_attend(q_lat, q_rope, jnp.concatenate([ckv_c, ckv], axis=1),
                        jnp.concatenate([kr_c, kr], axis=1), None)
    o_swa = _swa_attend(sq, jnp.concatenate([k_c, sk], axis=1),
                        jnp.concatenate([v_c, sv], axis=1), sinks, None)
    y = _block_out(x, o_lat, o_swa, p)
    buf = k_c.shape[1] - N_META
    k_rows = jnp.concatenate([k_c[:, N_META:], sk], axis=1)
    v_rows = jnp.concatenate([v_c[:, N_META:], sv], axis=1)
    k_new = jnp.concatenate([k_c[:, :N_META], k_rows[:, k_rows.shape[1] - buf:]], axis=1)
    v_new = jnp.concatenate([v_c[:, :N_META], v_rows[:, v_rows.shape[1] - buf:]], axis=1)
    return y, (ckv, kr, k_new, v_new)

def setup_inputs(seed: int = 0) -> dict:
    key = jax.random.key(seed)
    ks = jax.random.split(key, 26)
    f32 = jnp.float32

    def nrm(k, shape, scale=1.0):
        return jax.random.normal(k, shape, f32) * scale

    def gain(k, shape):
        return 1.0 + 0.05 * jax.random.normal(k, shape, f32)

    past_rows = N_META + PAST_LEN
    buf_rows = N_META + min(WINDOW, PAST_LEN)
    return {
        'x_prompt': nrm(ks[0], (BATCH, SEQ, D_MODEL)),
        'x_sample': nrm(ks[1], (DEC_BATCH, DEC_SEQ, D_MODEL)),
        'cache_mla_ckv': nrm(ks[2], (DEPTH, DEC_BATCH, past_rows, MLA_KV_LORA)),
        'cache_mla_krope': nrm(ks[3], (DEPTH, DEC_BATCH, past_rows, MLA_ROPE)),
        'cache_swa_k': nrm(ks[4], (DEPTH, DEC_BATCH, buf_rows, SWA_KV_HEADS, SWA_HEAD_DIM)),
        'cache_swa_v': nrm(ks[5], (DEPTH, DEC_BATCH, buf_rows, SWA_KV_HEADS, SWA_HEAD_DIM)),
        'meta_tokens': nrm(ks[6], (N_META, D_MODEL)),
        'in_ln_g': gain(ks[7], (D_MODEL,)),
        'in_ln_b': nrm(ks[8], (D_MODEL,), 0.02),
        'w_in': nrm(ks[9], (DEPTH, D_MODEL, IN_WIDTH), D_MODEL ** -0.5),
        'mla_q_norm_g': gain(ks[10], (DEPTH, MLA_Q_LORA)),
        'mla_w_uq': nrm(ks[11], (DEPTH, MLA_Q_LORA, MLA_HEADS, MLA_NOPE + MLA_ROPE), MLA_Q_LORA ** -0.5),
        'mla_kv_norm_g': gain(ks[12], (DEPTH, MLA_KV_LORA)),
        'mla_w_uk': nrm(ks[13], (DEPTH, MLA_KV_LORA, MLA_HEADS, MLA_NOPE), MLA_KV_LORA ** -0.5),
        'mla_w_uv': nrm(ks[14], (DEPTH, MLA_KV_LORA, MLA_HEADS, MLA_V), MLA_KV_LORA ** -0.5),
        'swa_sinks': nrm(ks[15], (DEPTH, SWA_HEADS), 0.5),
        'out_norm_mla_g': gain(ks[16], (DEPTH, MLA_OUT)),
        'out_norm_swa_g': gain(ks[17], (DEPTH, SWA_OUT)),
        'w_out': nrm(ks[18], (DEPTH, MIX_WIDTH, D_MODEL), BETA * MIX_WIDTH ** -0.5),
        'ln1_g': gain(ks[19], (DEPTH, D_MODEL)),
        'ln1_b': nrm(ks[20], (DEPTH, D_MODEL), 0.02),
        'ffn_w_gate': nrm(ks[21], (DEPTH, D_MODEL, D_FF), D_MODEL ** -0.5),
        'ffn_w_up': nrm(ks[22], (DEPTH, D_MODEL, D_FF), D_MODEL ** -0.5),
        'ffn_w_down': nrm(ks[23], (DEPTH, D_FF, D_MODEL), BETA * D_FF ** -0.5),
        'ln2_g': gain(ks[24], (DEPTH, D_MODEL)),
        'ln2_b': nrm(ks[25], (DEPTH, D_MODEL), 0.02),
    }

def reference(x_prompt, x_sample, cache_mla_ckv, cache_mla_krope, cache_swa_k, cache_swa_v,
              meta_tokens, in_ln_g, in_ln_b, w_in, mla_q_norm_g, mla_w_uq, mla_kv_norm_g,
              mla_w_uk, mla_w_uv, swa_sinks, out_norm_mla_g, out_norm_swa_g, w_out,
              ln1_g, ln1_b, ffn_w_gate, ffn_w_up, ffn_w_down, ln2_g, ln2_b):
    b = x_prompt.shape[0]
    meta = jnp.broadcast_to(meta_tokens[None].astype(x_prompt.dtype), (b, N_META, D_MODEL))
    hp = layer_norm(jnp.concatenate([meta, x_prompt], axis=1), in_ln_g, in_ln_b)
    hs = layer_norm(x_sample, in_ln_g, in_ln_b)
    p_ckv, p_kr, p_k, p_v = [], [], [], []
    s_ckv, s_kr, s_k, s_v = [], [], [], []
    for l in range(DEPTH):
        p = (w_in[l], mla_q_norm_g[l], mla_w_uq[l], mla_kv_norm_g[l], mla_w_uk[l], mla_w_uv[l],
             swa_sinks[l], out_norm_mla_g[l], out_norm_swa_g[l], w_out[l], ln1_g[l], ln1_b[l],
             ffn_w_gate[l], ffn_w_up[l], ffn_w_down[l], ln2_g[l], ln2_b[l])
        hp, (c1, c2, c3, c4) = _prompt_layer(hp, p)
        hs, (d1, d2, d3, d4) = _sample_layer(hs, cache_mla_ckv[l], cache_mla_krope[l],
                                             cache_swa_k[l], cache_swa_v[l], p)
        p_ckv.append(c1); p_kr.append(c2); p_k.append(c3); p_v.append(c4)
        s_ckv.append(d1); s_kr.append(d2); s_k.append(d3); s_v.append(d4)
    y_prompt = hp[:, N_META:]
    return (y_prompt, hs,
            jnp.stack(p_ckv), jnp.stack(p_kr), jnp.stack(p_k), jnp.stack(p_v),
            jnp.stack(s_ckv), jnp.stack(s_kr), jnp.stack(s_k), jnp.stack(s_v))


_drawn_inputs = setup_inputs


def setup_inputs(seed=0):
    import zlib

    import numpy as np

    out = dict(_drawn_inputs(seed))
    spreads = {}
    factors = {'mla_q_norm_g': 3.195, 'swa_sinks': 8.0, 'out_norm_mla_g': 3.065, 'out_norm_swa_g': 2.922}
    for name, (base, spread) in spreads.items():
        noise = np.random.default_rng([zlib.crc32(name.encode()), seed]).standard_normal(out[name].shape)
        drawn = base * np.exp(spread * noise) if base else spread * noise
        out[name] = jnp.asarray(drawn.astype(out[name].dtype))
    for name, factor in factors.items():
        out[name] = (out[name] * factor).astype(out[name].dtype)
    return out
```

```python
from contextlib import ExitStack

import numpy as np

import concourse.bass as bass
from concourse import mybir

F32 = mybir.dt.float32
F32R = mybir.dt.float32r
ALU = mybir.AluOpType
ACT = mybir.ActivationFunctionType
AX = mybir.AxisListType

P = 128
L = 2
D = 1024
KD = D // P
SEQ = 1024
NB = 8
NS = 16
META = 16
CH = 64
PAST = 1024
WIN = 128
HEADS = 8
QL = 256
LAT = 128
ROPE = 32
HD = 64
KVH = 2
SWA_H = 8
FF = 2816
FC = FF // P
TILES = 10
TOK = SEQ + NB * NS + META
SAMPLE = SEQ
METAROW = SEQ + NB * NS
INW = 1184
KR0 = QL + LAT
SQ0 = KR0 + ROPE
SK0 = SQ0 + SWA_H * HD
SV0 = SK0 + KVH * HD
KVW = LAT + ROPE + 2 * KVH * HD
CKEYS = META + PAST
WKEYS = META + WIN
NCH = SEQ // CH
TURNS = FC // 2
TURN_ITEMS = [(1, 0, 0), (0, 0, 2), (0, 1, 2), (1, 0, 1), (1, 1, 0), (1, 1, 1)]
LAST_ITEMS = [(0, 0, 2), (0, 1, 2)]
W_ITEMS = 4 + 6 * (TURNS - 1) + 2
NT = (390, 390, 388)
N0 = (0, 390, 780)
ALPHA = (2.0 * L) ** 0.25
MLA_SCALE = (64 + ROPE) ** -0.5
SWA_SCALE = HD ** -0.5
LN_EPS = 1e-5
RMS_EPS = 1e-6
MASKED = -1e30
BANK = 512


def rows(t):
    return META if t == TILES - 1 else P


def cols(t):
    return slice(t * P, t * P + rows(t))


def place_of(h):
    return (h % 2) * (HEADS // 2) + h // 2


def head_at(place):
    return (place % (HEADS // 2)) * 2 + place // (HEADS // 2)


def plan_units():
    prompt = [("qa", 9), ("qb", 9), ("qc", 9), ("mla_m", 9), ("qa", 0), ("swa_m", 9), ("qb", 0), ("oa", 9), ("qc", 0)]
    for t in range(8):
        nxt = t + 1
        body = [("mla", t, h) for h in range(HEADS)]
        body = body[:2] + [("qa", nxt)] + body[2:4] + [("qb", nxt)] + body[4:6] + [("qc", nxt)] + body[6:]
        prompt += body + [("swa", 2 * t), ("swa", 2 * t + 1), ("oa", t)]
    decode = []
    for b in range(NB):
        decode += [("mla_d", b), ("swa_d", b)]
    decode += [("oa", 8)]
    units, att, groups, swa = [], 0, 0, 0
    nq = {"qa": 0, "qb": 0, "qc": 0, "oa": 0}
    for n, what in enumerate(prompt + decode):
        u = {"n": n, "kind": what[0], "arg": what[1], "h": what[2] if len(what) > 2 else 0, "buf": n % 2,
             "before": units[n - 2] if n >= 2 else None}
        k = u["kind"]
        if k in nq:
            u["i"] = nq[k]
            nq[k] += 1
        else:
            u["out_before"] = next((v for v in reversed(units) if "a" in v), None)
            u["tail"] = {"mla": META if u["arg"] == 7 else 0, "mla_d": META + NS}.get(k, 0)
            u["tail_before"] = next((v for v in reversed(units) if v.get("tail")), None)
            u["a"] = att
            att += 1
            if k == "mla":
                nblk = u["arg"] + 2
            elif k == "mla_m":
                nblk = 1
            elif k == "mla_d":
                nblk = 9
            if k.startswith("mla"):
                u["sizes"] = [min(4, nblk - g) for g in range(0, nblk, 4)]
                u["oa"] = nq["oa"]
            elif k == "swa":
                u["sizes"] = [4, 4] if u["arg"] else [4]
            elif k == "swa_d":
                u["sizes"] = [2]
            else:
                u["sizes"] = [1]
            if k.startswith("swa"):
                u["w"] = swa
                swa += 1
            u["g0"] = groups
            groups += len(u["sizes"])
        units.append(u)
    return units[:len(prompt)], units[len(prompt):], att, groups, swa, nq


UB, UE, N_ATT, N_GRP, N_SWA, N_Q = plan_units()


def program(nc, X, LNP, ROT, W_IN, QKVG, W_UQ, W_UK, W_UV, SINKS, MIXG, W_OUT, LN1, W_FF,
            CKVT, CKV, KRT, SKT, SK, SV, H, KVS, NSK, NSV):
    MIX = nc.dram_tensor("mix_scratch", [TOK, D], F32).ap()
    CQT = nc.dram_tensor("cqt_scratch", [TILES, P, 4 * P], F32).ap()
    SQT = nc.dram_tensor("sqt_scratch", [TILES, P, SWA_H * P], F32).ap()

    with ExitStack() as ctx:
        names = {}

        def S(name):
            if name not in names:
                names[name] = ctx.enter_context(nc.semaphore(name))
            return names[name]

        base = nc.sbuf_base
        top = nc.sbuf_usable_end
        start = ((base + 31) // 32) * 32

        class Map:
            def __init__(self, at):
                self.at = at

            def __call__(self, name, shape, dt=F32):
                free = int(np.prod(shape[1:])) * 4
                t = nc.alloc_sbuf_tensor_at(name, shape, dt, offset=self.at)
                self.at += (free + 31) // 32 * 32
                assert self.at <= top, (name, self.at, top)
                return t

        m = Map(start)
        ident = m("ident", [P, P])
        half = m("half", [P, 1])
        stats = [m(f"stats{i}", [P, 12]) for i in range(2)]
        mv = [m(f"mv{i}", [P, 2]) for i in range(2)]
        veps = [m(f"veps{i}", [P, 1]) for i in range(2)]
        rstd = [m(f"rstd{i}", [P, 1]) for i in range(2)]
        ms = [m(f"ms{i}", [P, 2]) for i in range(2)]
        mse = [m(f"mse{i}", [P, 2]) for i in range(2)]
        mrs = [m(f"mrs{i}", [P, 2]) for i in range(2)]
        raw = [m(f"raw{i}", [P, INW]) for i in range(2)]
        common = m.at

        ckvTh = m("ckvTh", [P, TOK], F32R)
        ckvTl = m("ckvTl", [P, TOK], F32R)
        krT = m("krT", [P, TOK], F32R)
        skT = m("skT", [P, KVH, 2, TOK], F32R)
        vh = m("vh", [P, TILES, P], F32R)
        vl = m("vl", [P, TILES, P], F32R)
        after_kv = m.at

        winh = m("winh", [P, KD, INW], F32R)
        winl = m("winl", [P, KD, INW], F32R)
        ht = [m(f"ht{i}", [P, D]) for i in range(2)]
        xTh = [m(f"xTh{i}", [P, KD, P], F32R) for i in range(2)]
        xTl = [m(f"xTl{i}", [P, KD, P], F32R) for i in range(2)]
        zs = m("zs", [P, INW])
        cqn = m("cqn", [P, QL])
        kv1 = m("kv1", [P, LAT + ROPE])
        zr = m("zr", [P, 10, HD])
        rta = m("rta", [P, 10, HD])
        rot = [m(f"rot{i}", [P, 192]) for i in range(2)]
        qkvg = m("qkvg", [P, QL + LAT])
        krs = m("krs", [P, 4, ROPE], F32R)
        kss = m("kss", [P, KVH, 2, 2, HD], F32R)
        sqs = m("sqs", [P, SWA_H, 2, HD], F32R)
        cqTs = m("cqTs", [P, 2, 2, P], F32R)
        sqTs = m("sqTs", [P, SWA_H * P], F32R)
        junkA = m("junkA", [P, QL + LAT])
        rtb = m("rtb", [P, 10, HD])

        m = Map(after_kv)
        x0 = [m(f"x0_{i}", [P, D]) for i in range(2)]
        y0 = [m(f"y0_{i}", [P, D]) for i in range(2)]
        lnp = m("lnp", [P, 2 * D])

        m = Map(after_kv)
        wuvh = m("wuvh", [P, 512], F32R)
        wuvl = m("wuvl", [P, 512], F32R)
        only_b = m.at
        wuqh = m("wuqh", [P, 2, 768], F32R)
        wuql = m("wuql", [P, 2, 768], F32R)
        wukh = m("wukh", [P, 4, P], F32R)
        wukl = m("wukl", [P, 4, P], F32R)
        cq = [m(f"cq{i}", [P, 2, 2, P], F32R) for i in range(2)]
        qnh = m("qnh", [P, 4, P], F32R)
        qnl = m("qnl", [P, 4, P], F32R)
        qr_raw = m("qr_raw", [P, HEADS, ROPE])
        qra = m("qra", [P, HEADS, ROPE])
        qrb = m("qrb", [P, HEADS, ROPE])
        qrs = m("qrs", [P, HEADS, 4, ROPE], F32R)
        rotB = [m(f"rotB{i}", [P, 192]) for i in range(2)]
        only_b_end = m.at
        qrT = [m(f"qrT{i}", [P, HEADS * P], F32R) for i in range(2)]
        qlh = [m(f"qlh{i}", [P, HEADS * P], F32R) for i in range(2)]
        qll = [m(f"qll{i}", [P, HEADS * P], F32R) for i in range(2)]
        sqT = [m(f"sqT{i}", [P, SWA_H * P], F32R) for i in range(2)]
        olh = m("olh", [P, HEADS, P], F32R)
        oll = m("oll", [P, HEADS, P], F32R)
        Pb = [m(f"Pb{i}", [P, 1056]) for i in range(2)]
        PTh = [m(f"PTh{i}", [P, 9 * P], F32R) for i in range(2)]
        PTl = [m(f"PTl{i}", [P, 9 * P], F32R) for i in range(2)]
        mixo = m("mixo", [P, 512])
        mixs = [m(f"mixs{i}", [P, 4, HD]) for i in range(2)]
        mx = [m(f"mx{i}", [P, 4]) for i in range(2)]
        nb = [m(f"nb{i}", [P, 4]) for i in range(2)]
        sm = [m(f"sm{i}", [P, 4]) for i in range(2)]
        es = [m(f"es{i}", [P, 4]) for i in range(2)]
        ee = [m(f"ee{i}", [P, 4]) for i in range(2)]
        den = [m(f"den{i}", [P, 4]) for i in range(2)]
        rin = [m(f"rin{i}", [P, 4]) for i in range(4)]
        ri = [m(f"ri{i}", [P, HEADS]) for i in range(2)]
        sinkT = m("sinkT", [P, 5])
        nsink = m("nsink", [P, 5])
        maskq = m("maskq", [1, P], F32R)
        maskk = m("maskk", [1, CH], F32R)
        after_b = m.at
        VFh = m("VFh", [P, NCH, P], F32R)
        VFl = m("VFl", [P, NCH, P], F32R)
        VXh = m("VXh", [P, NCH, P], F32R)
        VXl = m("VXl", [P, NCH, P], F32R)
        svmh = m("svmh", [META, P], F32R)
        svml = m("svml", [META, P], F32R)

        m = Map(only_b)
        dkraw = m("dkraw", [P, CKEYS])
        drraw = m("drraw", [P, CKEYS])
        dvraw = m("dvraw", [P, 9, P])
        dsraw = m("dsraw", [P, KVH, WKEYS])
        duraw = m("duraw", [P, 2, P])
        drs = [m(f"drs{i}", [P, CKEYS], F32R) for i in range(2)]
        assert m.at <= only_b_end
        m = Map(after_b)
        dkh = [m(f"dkh{i}", [P, CKEYS], F32R) for i in range(2)]
        dkl = [m(f"dkl{i}", [P, CKEYS], F32R) for i in range(2)]
        dvh = [m(f"dvh{i}", [P, 9, P], F32R) for i in range(2)]
        dvl = [m(f"dvl{i}", [P, 9, P], F32R) for i in range(2)]
        dsh = [m(f"dsh{i}", [P, KVH, 2, WKEYS], F32R) for i in range(2)]
        duh = [m(f"duh{i}", [P, 2, P], F32R) for i in range(2)]
        dul = [m(f"dul{i}", [P, 2, P], F32R) for i in range(2)]

        m = Map(common)
        xh = m("xh", [P, KD, TOK], F32R)
        xl = m("xl", [P, KD, TOK], F32R)
        after_x = m.at
        wouth = m("wouth", [P, KD, D], F32R)
        woutl = m("woutl", [P, KD, D], F32R)
        mt = m("mt", [P, D])
        mn = m("mn", [P, D])
        hc = m("hc", [P, D])
        mTh = m("mTh", [P, KD, P], F32R)
        mTl = m("mTl", [P, KD, P], F32R)
        x1 = m("x1", [P, D])
        h1 = m("h1", [P, D])
        ln1 = m("ln1", [P, 2 * D])
        mixg = m("mixg", [P, D])
        junkC = m("junkC", [P, D])

        m = Map(common)
        m.at = after_x
        acc = m("acc", [P, KD, TOK])
        after_acc = m.at
        hidh = [m(f"hidh{i}", [P, TOK], F32R) for i in range(2)]
        hidl = [m(f"hidl{i}", [P, TOK], F32R) for i in range(2)]
        gate = m("gate", [P, TOK])
        fwh = [m(f"fwh{i}", [P, KD, P], F32R) for i in range(6)]
        fwl = [m(f"fwl{i}", [P, KD, P], F32R) for i in range(6)]
        fraw = [raw[0][:, 0:D].rearrange("p (k f) -> p k f", f=P), raw[1][:, 0:D].rearrange("p (k f) -> p k f", f=P),
                m("fraw2", [P, KD, P])[:, :, :]]

        m = Map(common)
        xo = [m(f"xo{i}", [P, D]) for i in range(2)]
        yo = [m(f"yo{i}", [P, D]) for i in range(2)]
        lnd = m("lnd", [P, 2 * D])

        PS = ctx.enter_context(nc.psum_tensor("PS", [P, 8 * BANK], F32))
        Sb = [PS[:, 3 * BANK * i:3 * BANK * (i + 1)] for i in range(2)]
        Tb = [PS[:, (6 + i) * BANK:(7 + i) * BANK] for i in range(2)]
        OB = PS[:, 5 * BANK:6 * BANK]
        block = ctx.enter_context(nc.Block())

        def f(ap):
            return ap.bitcast(F32)

        def barrier(eng, k):
            eng.drain().then_inc(S("phase_done"), 1)
            eng.wait_ge(S("phase_done"), 5 * k)

        def phase_no(l, which):
            return 1 + 1 + 6 * l + "ABECFD".index(which)

        def split_items(l, which):
            if which == "A":
                w = W_IN[l].rearrange("(k p) n -> p k n", p=P)
                return [([(lambda r, k=k: r[:, 0:INW], w[:, k, :])], lambda r: r[:, 0:INW],
                         winh[:, k, :], winl[:, k, :]) for k in range(KD)]
            if which == "C":
                w = W_OUT[l].rearrange("(k p) n -> p k n", p=P)
                return [([(lambda r: r[:, 0:D], w[:, k, :])], lambda r: r[:, 0:D],
                         wouth[:, k, :], woutl[:, k, :]) for k in range(KD)]
            w = W_UQ[l].rearrange("(k p) n -> p k n", p=P)
            items = [([(lambda r: r[:, 0:768], w[:, k, :])], lambda r: r[:, 0:768], wuqh[:, k, :], wuql[:, k, :])
                     for k in range(2)]
            cut = lambda r: r[:, 0:512]
            cut3 = lambda r: r[:, 0:512].rearrange("p (j n) -> p j n", n=P)
            items += [([(cut3, W_UK[l].rearrange("(j p) n -> p j n", p=P))], cut3, wukh[:, :, :], wukl[:, :, :]),
                      ([(cut, W_UV[l])], cut, wuvh[:, :], wuvl[:, :])]
            v = KVS[l][:, LAT + ROPE + KVH * HD:KVW]
            cut7 = lambda r: r[:, 0:7 * P].rearrange("p (j n) -> p j n", n=P)
            for odd in range(2):
                items.append(([(cut7, v[CH * odd:CH * odd + 7 * P, :].rearrange("(j p) n -> p j n", p=P))], cut7,
                              VFh[:, 2 + odd:NCH:2, :], VFl[:, 2 + odd:NCH:2, :]))
            c1 = lambda r: r[0:CH, 0:P]
            items.append(([(c1, v[0:CH, :])], c1, VFh[0:CH, 1, :], VFl[0:CH, 1, :]))
            for part in range(2):
                a = lambda r: r[0:CH, 0:D].rearrange("p (c n) -> p c n", n=P)
                full = lambda r: r[0:CH + META, 0:D].rearrange("p (c n) -> p c n", n=P)
                src = v[SEQ // 2 * part:SEQ // 2 * (part + 1), :].rearrange("(c p) n -> p c n", p=CH)
                dm = [(a, src)] + [(lambda r, c=c: r[CH:CH + META, c * P:(c + 1) * P], v[METAROW:TOK, :])
                                   for c in range(8)]
                items.append((dm, full, VXh[0:CH + META, 8 * part:8 * part + 8, :],
                              VXl[0:CH + META, 8 * part:8 * part + 8, :]))
            c2 = lambda r: r[0:META, 0:P]
            items.append(([(c2, v[METAROW:TOK, :])], c2, svmh[:, :], svml[:, :]))
            return items

        first, n_dma, n_item = {}, [0, 0], 0
        landed = []
        for l in range(L):
            for which in "ABC":
                first[l, which] = n_item
                for it in split_items(l, which):
                    n_dma[n_item % 2] += len(it[0])
                    landed.append(n_dma[n_item % 2])
                    n_item += 1

        def load_split(sp, l, which):
            for i, it in enumerate(split_items(l, which)):
                q = first[l, which] + i
                if q >= 2:
                    sp.wait_ge(S("split_lo"), q - 1)
                for place, src in it[0]:
                    sp.dma_start(place(raw[q % 2]), src).then_inc(S(f"raw{q % 2}_in"), 16)

        def split_hi(act, l, which):
            for i, it in enumerate(split_items(l, which)):
                q = first[l, which] + i
                act.wait_ge(S(f"raw{q % 2}_in"), 16 * landed[q])
                act.activation(it[2], it[1](raw[q % 2]), ACT.Copy).then_inc(S("split_hi"), 1)

        def split_lo(dve, l, which):
            for i, it in enumerate(split_items(l, which)):
                q = first[l, which] + i
                dve.wait_ge(S("split_hi"), q + 1)
                dve.tensor_tensor(it[3], it[1](raw[q % 2]), f(it[2]), ALU.subtract).then_inc(S("split_lo"), 1)

        def all_split(pe, l, which):
            pe.wait_ge(S("split_lo"), first[l, which] + len(split_items(l, which)))

        def ln_stats(dve, q, x, r):
            if q >= 2:
                dve.wait_ge(S("ln_norm"), q - 1)
            dve.bn_stats(stats[q % 2][0:r, 0:6], x[0:r, 0:512])
            dve.bn_stats(stats[q % 2][0:r, 6:12], x[0:r, 512:D]).then_inc(S("ln_stats"), 1)
            dve.wait_ge(S("ln_stats"), q + 1)
            dve.bn_aggr(mv[q % 2][0:r, :], stats[q % 2][0:r, :]).then_inc(S("ln_mv"), 1)
            dve.wait_ge(S("ln_mv"), q + 1)
            dve.tensor_scalar(veps[q % 2][0:r, :], mv[q % 2][0:r, 1:2], LN_EPS, None, ALU.add).then_inc(S("ln_eps"), 1)

        def ln_root(pool, q, r):
            pool.wait_ge(S("ln_eps"), q + 1)
            pool.wait_ge(S("half_set"), 1)
            pool.tensor_tensor(rstd[q % 2][0:r, :], veps[q % 2][0:r, :], half[0:r, :], ALU.pow).then_inc(S("ln_root"), 1)

        def ln_apply(dve, q, x, y, gb, r):
            dve.wait_ge(S("ln_root"), q + 1)
            dve.tensor_scalar(y[0:r, :], x[0:r, :], mv[q % 2][0:r, 0:1], rstd[q % 2][0:r, 0:1],
                              ALU.subtract, ALU.mult).then_inc(S("ln_norm"), 1)
            dve.wait_ge(S("ln_norm"), q + 1)
            dve.tensor_tensor(y[0:r, :], y[0:r, :], gb[0:r, 0:D], ALU.mult).then_inc(S("ln_gain"), 1)
            dve.wait_ge(S("ln_gain"), q + 1)
            dve.tensor_tensor(y[0:r, :], y[0:r, :], gb[0:r, D:2 * D], ALU.add).then_inc(S("ln_out"), 1)

        def q0(t):
            return t

        def qC(l, t):
            return TILES + 2 * TILES * l + t

        def qD(l, t):
            return 2 * TILES + 2 * TILES * l + t

        def small_loads(l, which):
            if which == "0":
                return [(lnp[:, :], LNP[0:1, :].to_broadcast([P, 2 * D]))]
            if which == "A":
                return [(qkvg[:, :], QKVG[l:l + 1, :].to_broadcast([P, QL + LAT]))]
            if which == "B":
                return [(sinkT[:, :], SINKS[l])]
            if which == "C":
                return [(ln1[:, :], LN1[l:l + 1, :].to_broadcast([P, 2 * D])),
                        (mixg[:, :], MIXG[l:l + 1, :].to_broadcast([P, D]))]
            return [(lnd[:, :], LNP[l + 1:l + 2, :].to_broadcast([P, 2 * D]))]

        param_count, total = {}, 0
        for key in ["0"] + [(l, w) for l in range(L) for w in "ABCD"]:
            total += len(small_loads(0, key) if key == "0" else small_loads(*key))
            param_count[key] = total

        def load_params(sp, l, which):
            for dst, src in small_loads(l, which):
                sp.dma_start(dst, src).then_inc(S("params_in"), 16)

        def params(eng, key):
            eng.wait_ge(S("params_in"), 16 * param_count[key])

        def A(l, t):
            return l * TILES + t

        def AT(l, a):
            return l * N_ATT + a

        def G(l, g):
            return l * N_GRP + g

        def QN(l, kind, i):
            return l * N_Q[kind] + i

        q_order = [u["arg"] for u in UB if u["kind"] == "qa"]
        q_slot = {t: i % 2 for i, t in enumerate(q_order)}
        q_index = {t: i for i, t in enumerate(q_order)}
        oa_order = [u["arg"] for u in UB + UE if u["kind"] == "oa"]
        oa_index = {t: i for i, t in enumerate(oa_order)}
        att_units = [u for u in UB + UE if "a" in u]
        mlas = [u for u in att_units if u["kind"].startswith("mla")]
        normed = [u for u in mlas if u["kind"] != "mla"]
        for i, u in enumerate(mlas):
            u["mla_i"] = i
        for i, u in enumerate(normed):
            u["norm_i"] = i
        for u in UB + UE:
            if u["kind"] == "oa":
                u["last_mla"] = max(v["a"] for v in mlas if v["oa"] == u["i"])

        def mla_ord(l, u):
            return len(mlas) * l + u["mla_i"]

        def norm_ord(l, u):
            return len(normed) * l + u["norm_i"]

        dec = {(u["kind"], u["arg"]): u["a"] for u in UE if "a" in u}
        per_slot = [0, 0]
        for u in att_units:
            if "w" in u:
                u["before_dmas"] = per_slot[u["w"] % 2]
                per_slot[u["w"] % 2] += 2 if u["kind"] == "swa" else 1

        def group_shape(u, g):
            k = u["kind"]
            if k in ("mla", "mla_d"):
                return P, u["sizes"][g] * P, 512 * g
            if k == "swa":
                if len(u["sizes"]) == 2 and g == 0:
                    return min(u["arg"], 2) * CH, 512, 0
                return CH + META, 512, 512
            if k == "swa_d":
                return P, 2 * P, 0
            return META, P, 0

        def key_count(u):
            return {"mla": (u["arg"] + 1) * P + META, "mla_m": META, "mla_d": CKEYS + NS}[u["kind"]]

        def score_view(u):
            c0 = 0 if u["buf"] == 0 else 3 * BANK - u["tail"]
            return PS[:, c0:c0 + key_count(u)]

        def tail_view(u):
            c0 = 2 * BANK if u["buf"] == 0 else 3 * BANK - u["tail"]
            return PS[:, c0:c0 + u["tail"]]

        def o_view(u):
            o = OB[:, 0:P]
            return o if u["kind"] == "mla" else o.rearrange("p (h t) -> p h t", t=NS)

        def out_view(ol, u):
            if u["kind"] == "mla":
                return ol[:, u["h"], :]
            at = 0 if u["kind"] == "mla_m" else NS * u["arg"]
            return ol[:, :, at:at + NS]

        def q_to(flat, t, chunks=False):
            if t == 9:
                return flat[:, 0:P].rearrange("p (h n) -> p h n", n=META)
            n = NB if t == 8 else 2
            if t < 8 and not chunks:
                return flat[:, :].rearrange("p (h n) -> p h n", n=P)
            return flat[:, :].rearrange("p (c h n) -> p h c n", c=n, h=HEADS)

        def q_from(ap, t, chunks=False):
            v = ap.rearrange("p (h n) -> p h n", n=P)
            if t == 9:
                return v[:, :, 0:META]
            if t < 8 and not chunks:
                return v
            return v.rearrange("p h (c n) -> p h c n", c=NB if t == 8 else 2)

        def heads(ap, r):
            return ap.rearrange("p (k n) -> p k n", n=P)[:, :, 0:r]

        def free_scores(eng, l, u):
            b = u["before"]
            if b is None:
                return
            if "a" in b:
                eng.wait_ge(S("probs"), AT(l, b["a"]) + 1)
            elif b["kind"] == "oa":
                eng.wait_ge(S("oa_out"), QN(l, "oa", b["i"]) + 1)
            else:
                done = {"qa": "qa_rope", "qb": "qb_lo", "qc": "qc_out"}[b["kind"]]
                eng.wait_ge(S(done), QN(l, b["kind"], b["i"]) + 1)

        last_swa = {}
        for u in UB:
            if u["kind"] == "swa":
                last_swa[u["arg"] // 2] = u["a"]
            if u["kind"] == "swa_m":
                last_swa[9] = u["a"]

        @block.sync
        def _(sp):
            load_params(sp, 0, "0")
            for t in range(TILES):
                if t >= 2:
                    sp.wait_ge(S("ln_norm"), q0(t - 2) + 1)
                sp.dma_start(x0[t % 2][0:rows(t), :], X[cols(t), :]).then_inc(S(f"x0_in{t % 2}"), 16)
            barrier(sp, 1)
            for l in range(L):
                load_params(sp, l, "A")
                for t in range(2):
                    sp.dma_start(ht[t][0:rows(t), :], H[l, cols(t), :]).then_inc(S(f"ht_in{t}"), 16)
                    sp.dma_start(rot[t][0:rows(t), :], ROT[cols(t), :]).then_inc(S(f"ht_in{t}"), 16)
                load_split(sp, l, "A")
                for t in range(2, TILES):
                    sp.wait_ge(S("a_xT"), A(l, t - 2) + 1)
                    sp.dma_start(ht[t % 2][0:rows(t), :], H[l, cols(t), :]).then_inc(S(f"ht_in{t % 2}"), 16)
                    sp.wait_ge(S("a_rope"), A(l, t - 2) + 1)
                    sp.dma_start(rot[t % 2][0:rows(t), :], ROT[cols(t), :]).then_inc(S(f"ht_in{t % 2}"), 16)
                barrier(sp, phase_no(l, "A"))
                load_params(sp, l, "B")
                load_split(sp, l, "B")
                for i, t in enumerate(q_order):
                    r = rows(t)
                    if i >= 2:
                        sp.wait_ge(S("qa"), QN(l, "qa", i - 2) + 1)
                        sp.wait_ge(S("qa_rope"), QN(l, "qa", i - 2) + 1)
                    for a in range(2):
                        sp.dma_start(f(cq[i % 2][:, a, :, 0:r]),
                                     CQT[t].rearrange("p (a k n) -> p a k n", a=2, k=2)[:, a, :, 0:r])\
                          .then_inc(S(f"q_in{i % 2}"), 16)
                    sp.dma_start(rotB[i % 2][0:r, :], ROT[cols(t), :]).then_inc(S(f"q_in{i % 2}"), 16)
                    if i >= 2:
                        sp.wait_ge(S("pv"), AT(l, last_swa[q_order[i - 2]]) + 1)
                    sp.dma_start(f(sqT[i % 2][:, 0:SWA_H * r]), SQT[t, :, 0:SWA_H * r]).then_inc(S(f"sq_in{i % 2}"), 16)
                barrier(sp, phase_no(l, "B"))
                for b in range(NB):
                    s = l * NB + b
                    r0 = SAMPLE + NS * b
                    if s >= 1:
                        sp.wait_ge(S("dm_lo"), s)
                    sp.dma_start(dkraw[:, :], CKVT[l, b]).then_inc(S("dm_in"), 16)
                    for i in range(4):
                        sp.dma_start(drraw[ROPE * i:ROPE * (i + 1), :], KRT[l, b]).then_inc(S("dm_in"), 16)
                    sp.dma_start(dvraw[:, 0:8, :], CKV[l, b, 0:PAST, :].rearrange("(j p) n -> p j n", p=P))\
                      .then_inc(S("dm_in"), 16)
                    sp.dma_start(dvraw[0:META, 8, :], CKV[l, b, PAST:CKEYS, :]).then_inc(S("dm_in"), 16)
                    sp.dma_start(dvraw[META:META + NS, 8, :], KVS[l, r0:r0 + NS, 0:LAT]).then_inc(S("dm_in"), 16)
                    if s >= 1:
                        sp.wait_ge(S("ds_lo"), s)
                    for i in range(2):
                        sp.dma_start(dsraw[HD * i:HD * (i + 1), :, :], SKT[l, b].rearrange("(g d) n -> d g n", d=HD))\
                          .then_inc(S("ds_in"), 16)
                    sp.dma_start(duraw[:, 0, :], SV[l, b, 0:P, :]).then_inc(S("ds_in"), 16)
                    sp.dma_start(duraw[0:META, 1, :], SV[l, b, P:WKEYS, :]).then_inc(S("ds_in"), 16)
                    sp.dma_start(duraw[META:META + NS, 1, :], KVS[l, r0:r0 + NS, LAT + ROPE + KVH * HD:KVW])\
                      .then_inc(S("ds_in"), 16)
                barrier(sp, phase_no(l, "E"))
                load_params(sp, l, "C")
                sp.dma_start(mt[:, :], MIX[cols(0), :]).then_inc(S("mt_in"), 16)
                sp.dma_start(hc[:, :], H[l, cols(0), :]).then_inc(S("hc_in"), 16)
                load_split(sp, l, "C")
                for t in range(1, TILES):
                    sp.wait_ge(S("c_mixn"), A(l, t - 1) + 1)
                    sp.dma_start(mt[0:rows(t), :], MIX[cols(t), :]).then_inc(S("mt_in"), 16)
                    sp.wait_ge(S("c_res"), A(l, t - 1) + 1)
                    sp.dma_start(hc[0:rows(t), :], H[l, cols(t), :]).then_inc(S("hc_in"), 16)
                barrier(sp, phase_no(l, "C"))
                def w_load(n, c, which, slot):
                    sp.dma_start(fraw[slot], W_FF[l, c, which].rearrange("p (k f) -> p k f", f=P))\
                      .then_inc(S(f"fraw_in{slot}"), 16)

                for k in range(4):
                    if W_ITEMS * l + k >= 3:
                        sp.wait_ge(S("f_lo"), W_ITEMS * l + k - 2)
                    w_load(k, k // 2, k % 2, k % 3)

                def turn(j, items):
                    for k, (ahead, c, which) in enumerate(items):
                        sp.wait_ge(S("f_lo"), j * 6 + (W_ITEMS * l + 4 + k - 3 + 1))
                        w_load(None, (j + ahead) * 2 + c, which, (4 + k) % 3)

                with sp.Fori(0, TURNS - 1) as j:
                    turn(j, TURN_ITEMS)
                turn(TURNS - 1, LAST_ITEMS)
                barrier(sp, phase_no(l, "F"))
                load_params(sp, l, "D")
                barrier(sp, phase_no(l, "D"))

        def store_q(pool, l, t):
            r = rows(t)
            pool.wait_ge(S("a_post_lo"), A(l, t) + 1)
            for a in range(2):
                pool.dma_start(CQT[t].rearrange("p (a k n) -> p a k n", a=2, k=2)[:, a, :, 0:r],
                               f(cqTs[:, a, :, 0:r])).then_inc(S("cqT_out"), 16)
            pool.wait_ge(S("a_sqT"), A(l, t) + 1)
            w = SWA_H * r
            pool.dma_start(SQT[t, :, 0:w], f(sqTs[:, 0:w])).then_inc(S("sqT_out"), 16)

        def store_swa(pool, l, u):
            src = mixs[u["w"] % 2]
            pool.wait_ge(S("out_read"), AT(l, u["a"]) + 1)
            name = f"mixs_out{u['w'] % 2}"
            if u["kind"] == "swa":
                c = u["arg"]
                for hh in range(2):
                    dst = MIX[CH * c:CH * c + CH, 512:1024].rearrange("q (j h d) -> q j h d", h=2, d=HD)[:, :, hh, :]
                    pool.dma_start(dst, src[CH * hh:CH * hh + CH, :, :]).then_inc(S(name), 16)
            else:
                r0 = METAROW if u["kind"] == "swa_m" else SAMPLE + NS * u["arg"]
                dst = MIX[r0:r0 + NS, 512:1024].rearrange("t (h d) -> h t d", d=HD)
                pool.dma_start(dst, src[:, 0, :]).then_inc(S(name), 16)

        @block.gpsimd
        def _(pool):
            pool.memset(half[:, :], -0.5).then_inc(S("half_set"), 1)
            pool.memset(ident[:, :], 0.0).then_inc(S("ident_zero"), 1)
            pool.wait_ge(S("ident_zero"), 1)
            pool.affine_select(out=ident[:, :], in_=ident[:, :], compare_op=ALU.not_equal, fill=1.0,
                               base=0, pattern=[[-1, P]], channel_multiplier=1).then_inc(S("ident"), 1)
            for t in range(TILES):
                ln_root(pool, q0(t), rows(t))
                pool.wait_ge(S("ln_out"), q0(t) + 1)
                pool.dma_start(H[0, cols(t), :], y0[t % 2][0:rows(t), :]).then_inc(S(f"y0_out{t % 2}"), 16)
            pool.wait_ge(S("y0_out0"), 16 * (TILES // 2))
            pool.wait_ge(S("y0_out1"), 16 * (TILES // 2))
            barrier(pool, 1)
            for l in range(L):
                for t in range(TILES):
                    r = rows(t)
                    pool.wait_ge(S("a_mse"), A(l, t) + 1)
                    pool.tensor_tensor(mrs[t % 2][0:r, :], mse[t % 2][0:r, :], half[0:r, 0:1].to_broadcast([r, 2]),
                                       ALU.pow).then_inc(S("a_root"), 1)
                    pool.wait_ge(S("a_rope"), A(l, t) + 1)
                    pool.dma_start(KVS[l, cols(t), 0:LAT + ROPE], kv1[0:r, :]).then_inc(S("kv_out"), 16)
                    pool.dma_start(KVS[l, cols(t), LAT + ROPE:LAT + ROPE + KVH * HD],
                                   zr[0:r, 8:10, :]).then_inc(S("kv_out"), 16)
                    pool.dma_start(KVS[l, cols(t), LAT + ROPE + KVH * HD:KVW],
                                   zs[0:r, SV0:INW]).then_inc(S("kv_out"), 16)
                    if t >= 1:
                        store_q(pool, l, t - 1)
                store_q(pool, l, TILES - 1)
                pool.wait_ge(S("cqT_out"), 16 * (2 * TILES * (l + 1)))
                pool.wait_ge(S("sqT_out"), 16 * (TILES * (l + 1)))
                pool.wait_ge(S("kv_out"), 16 * (3 * TILES * (l + 1)))
                barrier(pool, phase_no(l, "A"))
                for part, units in (("B", UB), ("E", UE)):
                    prev = None
                    for u in units + [None]:
                        if prev is not None and (prev["kind"].startswith("swa")):
                            store_swa(pool, l, prev)
                        if u is not None and u["kind"] == "oa":
                            t = u["arg"]
                            pool.wait_ge(S("oa_out"), QN(l, "oa", u["i"]) + 1)
                            pool.dma_start(MIX[cols(t), 0:512], mixo[0:rows(t), :]).then_inc(S("mixo_out"), 16)
                        prev = u
                    if part == "B":
                        pool.wait_ge(S("mixo_out"), 16 * (10 * l + 9))
                    else:
                        pool.wait_ge(S("mixo_out"), 16 * (10 * l + 10))
                        for i in range(2):
                            pool.wait_ge(S(f"mixs_out{i}"), 16 * (per_slot[i] * (l + 1)))
                        for src, dst, c0 in ((SK, NSK, LAT + ROPE), (SV, NSV, LAT + ROPE + KVH * HD)):
                            pool.dma_start(dst[l, :, 0:META, :], src[l, :, 0:META, :]).then_inc(S("cache_out"), 16)
                            pool.dma_start(dst[l, :, META:WIN, :], src[l, :, META + NS:WKEYS, :])\
                                .then_inc(S("cache_out"), 16)
                            pool.dma_start(dst[l, :, WIN:WKEYS, :],
                                           KVS[l, SAMPLE:METAROW, c0:c0 + KVH * HD].rearrange("(b t) n -> b t n", t=NS))\
                                .then_inc(S("cache_out"), 16)
                    barrier(pool, phase_no(l, part))
                for t in range(TILES):
                    r = rows(t)
                    pool.wait_ge(S("c_mse"), A(l, t) + 1)
                    pool.tensor_tensor(mrs[t % 2][0:r, :], mse[t % 2][0:r, :], half[0:r, 0:1].to_broadcast([r, 2]),
                                       ALU.pow).then_inc(S("c_root"), 1)
                    if t >= 1:
                        ln_root(pool, qC(l, t - 1), rows(t - 1))
                ln_root(pool, qC(l, TILES - 1), rows(TILES - 1))
                barrier(pool, phase_no(l, "C"))

                def w_lo(n_wait, slot, dst):
                    pool.wait_ge(S("f_hi"), n_wait)
                    pool.tensor_tensor(fwl[dst][:, :, :], fraw[slot], f(fwh[dst][:, :, :]), ALU.subtract)\
                        .then_inc(S("f_lo"), 1)

                for k in range(4):
                    w_lo(W_ITEMS * l + k + 1, k % 3, k)

                def turn(j, items):
                    for k, (ahead, c, which) in enumerate(items):
                        w_lo(j * 6 + (W_ITEMS * l + 4 + k + 1), (4 + k) % 3, 4 + c if which == 2 else 2 * c + which)

                with pool.Fori(0, TURNS - 1) as j:
                    turn(j, TURN_ITEMS)
                turn(TURNS - 1, LAST_ITEMS)
                barrier(pool, phase_no(l, "F"))
                for t in range(TILES):
                    ln_root(pool, qD(l, t), rows(t))
                    pool.wait_ge(S("ln_out"), qD(l, t) + 1)
                    pool.dma_start(H[l + 1, cols(t), :], yo[t % 2][0:rows(t), :]).then_inc(S(f"yo_out{t % 2}"), 16)
                for i in range(2):
                    pool.wait_ge(S(f"yo_out{i}"), 16 * ((l + 1) * TILES // 2))
                barrier(pool, phase_no(l, "D"))
            pool.wait_ge(S("cache_out"), 16 * (6 * L))

        def w_hi(act, l, item, slot, dst, total):
            act.wait_ge(S(f"fraw_in{slot}"), 16 * (total // 3 + 1))
            act.activation(fwh[dst][:, :, :], fraw[slot], ACT.Copy).then_inc(S("f_hi"), 1)

        def g_bank(i):
            return Sb[0][:, 512 * i:512 * i + NT[i]]

        def u_bank(i):
            return Sb[1][:, 512 * i:512 * i + NT[i]]

        @block.scalar
        def _(act):
            barrier(act, 1)
            for l in range(L):
                split_hi(act, l, "A")

                def x_hi(t):
                    r = rows(t)
                    act.wait_ge(S("a_xT"), A(l, t) + 1)
                    if t >= 2:
                        act.wait_ge(S("a_z"), A(l, t - 2) + 1)
                    act.activation(xTh[t % 2][:, :, 0:r],
                                   Sb[1][:, 0:1024].rearrange("p (k n) -> p k n", n=P)[:, :, 0:r], ACT.Copy)\
                       .then_inc(S("a_xh"), 1)

                def z_out(t):
                    r = rows(t)
                    act.wait_ge(S("a_z"), A(l, t) + 1)
                    if t >= 1:
                        act.wait_ge(S("a_rope"), A(l, t - 1) + 1)
                        act.wait_ge(S("kv_out"), 16 * (3 * A(l, t)))
                    act.activation(zs[0:r, :], Sb[0][0:r, 0:INW], ACT.Copy)
                    act.activation(junkA[0:r, 0:QL], Sb[0][0:r, 0:QL], ACT.Square, scale=QL ** -0.5,
                                   accum_out=ms[t % 2][0:r, 0:1])
                    act.activation(junkA[0:r, QL:QL + LAT], Sb[0][0:r, QL:QL + LAT], ACT.Square, scale=LAT ** -0.5,
                                   accum_out=ms[t % 2][0:r, 1:2]).then_inc(S("a_zs"), 1)

                def stack_hi(t):
                    r = rows(t)
                    act.wait_ge(S("a_rope"), A(l, t) + 1)
                    if t >= 1:
                        act.wait_ge(S("a_post"), A(l, t - 1) + 1)
                    act.activation(vh[0:r, t, :], kv1[0:r, 0:LAT], ACT.Copy)
                    kr = kv1[0:r, LAT:LAT + ROPE]
                    for i in (0, 2):
                        act.activation(krs[0:r, i, :], kr, ACT.Copy)
                    for i in range(2):
                        act.activation(kss[0:r, :, 0, i, :], zr[0:r, 8:10, :], ACT.Copy)
                    act.activation(sqs[0:r, :, 0, :], zr[0:r, 0:8, :], ACT.Copy).then_inc(S("a_stack_hi"), 1)

                def post_hi(t):
                    r = rows(t)
                    act.wait_ge(S("a_post"), A(l, t) + 1)
                    if t >= 1:
                        act.wait_ge(S("cqT_out"), 16 * (2 * A(l, t)))
                        act.wait_ge(S("sqT_out"), 16 * (A(l, t)))
                    b5 = Sb[1][:, 1024:1536].rearrange("p (k n) -> p k n", n=P)
                    act.activation(cqTs[:, 0, :, 0:r], b5[:, 0:2, 0:r], ACT.Copy)
                    act.activation(ckvTh[:, cols(t)], b5[:, 2, 0:r], ACT.Copy)
                    act.activation(krT[:, cols(t)], b5[:, 3, 0:r], ACT.Copy).then_inc(S("a_post_hi"), 1)
                    act.activation(q_to(sqTs, t, True), q_from(Sb[1][:, 0:1024], t, True), ACT.Copy).then_inc(S("a_sqT"), 1)

                x_hi(0)
                for n in range(TILES + 1):
                    if n + 1 < TILES:
                        x_hi(n + 1)
                    if n < TILES:
                        z_out(n)
                    if n >= 1:
                        post_hi(n - 1)
                    if n < TILES:
                        stack_hi(n)
                barrier(act, phase_no(l, "A"))

                split_hi(act, l, "B")

                def soft(u):
                    a = u["a"]
                    i = a % 2
                    act.wait_ge(S("bias"), AT(l, a) + 1)
                    if a >= 2:
                        act.wait_ge(S("rinv"), AT(l, a - 2) + 1)
                    if a >= 2:
                        pu = att_units[a - 2]
                        act.wait_ge(S("probsT"), G(l, pu["g0"] + len(pu["sizes"]) - 1) + 1)
                    k, sbuf = u["kind"], Sb[u["buf"]]
                    if k.startswith("mla"):
                        act.activation(Pb[i][:, 0:key_count(u)], score_view(u), ACT.Exp, bias=nb[i][:, 0:1], scale=MLA_SCALE,
                                       accum_out=sm[i][:, 0:1]).then_inc(S("probs"), 1)
                        return
                    if k == "swa":
                        n = min(u["arg"], 2) * CH + CH + META
                        act.activation(ee[i][:, 0:4], es[i][:, 0:4], ACT.Exp)
                        for j in range(4):
                            ins = act.activation(Pb[i][:, 256 * j:256 * j + n], sbuf[:, 256 * j:256 * j + n], ACT.Exp,
                                                 bias=nb[i][:, j:j + 1], scale=SWA_SCALE, accum_out=sm[i][:, j:j + 1])
                    else:
                        n = WKEYS + NS if k == "swa_d" else META
                        act.activation(ee[i][:, 0:1], es[i][:, 0:1], ACT.Exp)
                        for g in range(KVH):
                            p = slice(CH * g, CH * g + CH)
                            ins = act.activation(Pb[i][p, 0:n], sbuf[p, 256 * g:256 * g + n], ACT.Exp,
                                                 bias=nb[i][p, 0:1], scale=SWA_SCALE, accum_out=sm[i][p, 0:1])
                    ins.then_inc(S("probs"), 1)

                def unit_hi(u, groups):
                    a = u["a"]
                    i = a % 2
                    for g in groups:
                        gg = G(l, u["g0"] + g)
                        act.wait_ge(S("probsT"), gg + 1)
                        if g == 0 and a >= 2:
                            act.wait_ge(S("pv"), AT(l, a - 2) + 1)
                        kk, w, at = group_shape(u, g)
                        act.activation(PTh[i][0:kk, at:at + w], Tb[gg % 2][0:kk, 0:w], ACT.Copy)\
                           .then_inc(S("probsT_hi"), 1)

                def out_hi(u):
                    if not u["kind"].startswith("mla"):
                        return
                    act.wait_ge(S("pv"), AT(l, u["a"]) + 1)
                    if u["oa"]:
                        act.wait_ge(S("oa"), QN(l, "oa", u["oa"] - 1) + 1)
                    act.activation(out_view(olh, u), o_view(u), ACT.Copy).then_inc(S("ol_hi"), 1)

                def q_unit(u):
                    k, i, t = u["kind"], QN(l, u["kind"], u["i"]), u["arg"]
                    r, s, sbuf = rows(t), u["i"] % 2, Sb[u["buf"]]
                    act.wait_ge(S(k), i + 1)
                    if k == "qa":
                        if u["i"] >= 1:
                            act.wait_ge(S("qb"), QN(l, "qb", u["i"] - 1) + 1)
                        act.activation(qnh[:, :, 0:r], sbuf[:, 0:512].rearrange("p (k n) -> p k n", n=P)[:, :, 0:r],
                                       ACT.Copy).then_inc(S("qa_hi"), 1)
                    elif k == "qb":
                        act.activation(q_to(qlh[s], t), q_from(sbuf[:, 0:1024], t), ACT.Copy).then_inc(S("qb_hi"), 1)
                    else:
                        act.activation(q_to(qrT[s], t), q_from(sbuf[:, 0:1024], t), ACT.Copy).then_inc(S("qc_out"), 1)

                def rope_hi(u):
                    r = rows(u["arg"])
                    act.wait_ge(S("qa_rope"), QN(l, "qa", u["i"]) + 1)
                    if u["i"] >= 1:
                        act.wait_ge(S("qc"), QN(l, "qc", u["i"] - 1) + 1)
                    for i in range(2):
                        ins = act.activation(qrs[0:r, :, i, :], qr_raw[0:r, :, :], ACT.Copy)
                    ins.then_inc(S("qrs_hi"), 1)

                def attend(units):
                    for n in range(len(units) + 2):
                        u = units[n] if n < len(units) else None
                        v = units[n - 1] if 1 <= n <= len(units) else None
                        w = units[n - 2] if n >= 2 else None
                        if v is not None and "a" in v:
                            unit_hi(v, range(1))
                        if u is not None:
                            if "a" in u:
                                soft(u)
                            elif u["kind"] != "oa":
                                q_unit(u)
                        if v is not None and "a" in v:
                            unit_hi(v, range(1, len(v["sizes"])))
                        if w is not None and "a" in w:
                            out_hi(w)
                        if u is not None:
                            if u["kind"] == "mla_d" and u["arg"] + 1 < NB:
                                latents_hi(u["arg"] + 1)
                            if u["kind"] == "swa_d" and u["arg"] + 1 < NB:
                                window_hi(u["arg"] + 1)
                            if u["kind"] == "qa":
                                rope_hi(u)

                def latents_hi(b):
                    act.wait_ge(S("dm_in"), 16 * (8 * (l * NB + b + 1)))
                    if b >= 2:
                        act.wait_ge(S("pv"), AT(l, dec["mla_d", b - 2]) + 1)
                    s = b % 2
                    act.activation(dkh[s][:, :], dkraw[:, :], ACT.Copy)
                    act.activation(drs[s][:, :], drraw[:, :], ACT.Copy)
                    act.activation(dvh[s][:, 0:8, :], dvraw[:, 0:8, :], ACT.Copy)
                    act.activation(dvh[s][0:32, 8, :], dvraw[0:32, 8, :], ACT.Copy).then_inc(S("dm_hi"), 1)

                def window_hi(b):
                    act.wait_ge(S("ds_in"), 16 * (5 * (l * NB + b + 1)))
                    if b >= 2:
                        act.wait_ge(S("pv"), AT(l, dec["swa_d", b - 2]) + 1)
                    s = b % 2
                    act.activation(dsh[s][:, :, 0, :], dsraw[:, :, :], ACT.Copy)
                    act.activation(duh[s][:, 0, :], duraw[:, 0, :], ACT.Copy)
                    act.activation(duh[s][0:32, 1, :], duraw[0:32, 1, :], ACT.Copy).then_inc(S("ds_hi"), 1)

                attend(UB)
                barrier(act, phase_no(l, "B"))
                latents_hi(0)
                window_hi(0)
                attend(UE)
                barrier(act, phase_no(l, "E"))

                split_hi(act, l, "C")

                def mix_sq(t):
                    r = rows(t)
                    act.wait_ge(S("mt_in"), 16 * (A(l, t) + 1))
                    for i in range(2):
                        ins = act.activation(junkC[0:r, 512 * i:512 * i + 512], mt[0:r, 512 * i:512 * i + 512], ACT.Square,
                                             scale=512 ** -0.5, accum_out=ms[t % 2][0:r, i:i + 1])
                    ins.then_inc(S("c_ms"), 1)

                def mix_hi(t):
                    r = rows(t)
                    act.wait_ge(S("c_mT"), A(l, t) + 1)
                    if t >= 1:
                        act.wait_ge(S("c_y"), A(l, t - 1) + 1)
                    act.activation(mTh[:, :, 0:r], Sb[0][:, 0:1024].rearrange("p (k n) -> p k n", n=P)[:, :, 0:r],
                                   ACT.Copy).then_inc(S("c_mh"), 1)

                def h1_hi(t):
                    r = rows(t)
                    act.wait_ge(S("c_hT"), A(l, t) + 1)
                    for i in range(2):
                        ins = act.activation(xh[:, 4 * i:4 * i + 4, cols(t)],
                                             Tb[i][:, :].rearrange("p (k n) -> p k n", n=P)[:, :, 0:r], ACT.Copy)
                    ins.then_inc(S("c_xh"), 1)

                mix_sq(0)
                mix_hi(0)
                for n in range(TILES + 1):
                    if n + 1 < TILES:
                        mix_sq(n + 1)
                    if n >= 1:
                        h1_hi(n - 1)
                    if n + 1 < TILES:
                        mix_hi(n + 1)
                barrier(act, phase_no(l, "C"))

                for k in range(KD):
                    act.activation(acc[:, k, :], f(xh[:, k, :]), ACT.Copy, scale=ALPHA).then_inc(S("f_acc0"), 1)
                    if k < 4:
                        w_hi(act, l, k, k % 3, k, W_ITEMS * l + k)

                def silu(j, c, first_turn):
                    for i in range(3):
                        act.wait_ge(S("f_gate"), j * 6 + (6 * TURNS * l + 3 * c + i + 1))
                        if not (first_turn and c == 0):
                            act.wait_ge(S("f_hidl"), j * 6 + (6 * TURNS * l + 3 * c - 3 + i + 1))
                        act.activation(gate[:, N0[i]:N0[i] + NT[i]], g_bank(i), ACT.Silu).then_inc(S("f_silu"), 1)

                def hid_hi(j, c):
                    for i in range(3):
                        act.wait_ge(S("f_hid"), j * 6 + (6 * TURNS * l + 3 * c + i + 1))
                        act.activation(hidh[c][:, N0[i]:N0[i] + NT[i]], gate[:, N0[i]:N0[i] + NT[i]], ACT.Copy)\
                           .then_inc(S("f_hidh"), 1)

                def weights_hi(j, items, k, first_turn):
                    _, c, which = items[k]
                    slot = (4 + k) % 3
                    item = W_ITEMS * l + 4 + k
                    act.wait_ge(S(f"fraw_in{slot}"), j * 32 + 16 * (item // 3 + 1))
                    if which < 2:
                        act.wait_ge(S("f_up" if which else "f_gate"), j * 6 + (6 * TURNS * l + 3 * c + 3))
                        act.activation(fwh[2 * c + which][:, :, :], fraw[slot], ACT.Copy).then_inc(S("f_hi"), 1)
                    else:
                        if not first_turn:
                            act.wait_ge(S("f_down"), j * 24 + 24 * TURNS * l)
                        act.activation(fwh[4 + c][:, :, :], fraw[slot], ACT.Copy).then_inc(S("f_hi"), 1)

                def turn(j, first_turn):
                    silu(j, 0, first_turn)
                    weights_hi(j, TURN_ITEMS, 0, first_turn)
                    hid_hi(j, 0)
                    for k in range(1, 4):
                        weights_hi(j, TURN_ITEMS, k, first_turn)
                    silu(j, 1, first_turn)
                    weights_hi(j, TURN_ITEMS, 4, first_turn)
                    hid_hi(j, 1)
                    weights_hi(j, TURN_ITEMS, 5, first_turn)

                turn(0, True)
                with act.Fori(1, TURNS - 1) as j:
                    turn(j, False)
                j = TURNS - 1
                silu(j, 0, False)
                hid_hi(j, 0)
                weights_hi(j, LAST_ITEMS, 0, False)
                weights_hi(j, LAST_ITEMS, 1, False)
                silu(j, 1, False)
                hid_hi(j, 1)
                barrier(act, phase_no(l, "F"))
                for t in range(TILES):
                    r = rows(t)
                    q = A(l, t)
                    act.wait_ge(S("d_T"), q + 1)
                    if t >= 2:
                        act.wait_ge(S("ln_norm"), qD(l, t - 2) + 1)
                    act.activation(xo[t % 2][0:r, :], Sb[t % 2][0:r, 0:1024], ACT.Copy).then_inc(S("d_xo"), 1)
                barrier(act, phase_no(l, "D"))

        @block.vector
        def _(dve):
            for i in range(2):
                dve.memset(Tb[i][:, :], 0.0).then_inc(S("t_zero"), 1)
            params(dve, "0")
            for t in range(TILES + 1):
                if t < TILES:
                    dve.wait_ge(S(f"x0_in{t % 2}"), 16 * (t // 2 + 1))
                    ln_stats(dve, q0(t), x0[t % 2], rows(t))
                if t >= 1:
                    if t >= 3:
                        dve.wait_ge(S(f"y0_out{(t - 1) % 2}"), 16 * ((t - 1) // 2))
                    ln_apply(dve, q0(t - 1), x0[(t - 1) % 2], y0[(t - 1) % 2], lnp, rows(t - 1))
            barrier(dve, 1)
            for l in range(L):
                split_lo(dve, l, "A")
                params(dve, (l, "A"))

                def x_lo(t):
                    r = rows(t)
                    dve.wait_ge(S("a_xh"), A(l, t) + 1)
                    dve.tensor_tensor(xTl[t % 2][:, :, 0:r], heads(Sb[1][:, 0:1024], r), f(xTh[t % 2][:, :, 0:r]),
                                      ALU.subtract).then_inc(S("a_xl"), 1)

                def rotate(out, x, ta, tb, cs, sn, r, n, half_n, sems, items):
                    w = 2 * half_n
                    c = cs.rearrange("p (a w) -> p a w", a=1).to_broadcast([r, n, w])
                    s1 = sn[:, 0:half_n].rearrange("p (a w) -> p a w", a=1).to_broadcast([r, n, half_n])
                    s2 = sn[:, half_n:w].rearrange("p (a w) -> p a w", a=1).to_broadcast([r, n, half_n])
                    dve.tensor_tensor(ta, x, c, ALU.mult)
                    dve.tensor_tensor(tb[:, :, 0:half_n], x[:, :, half_n:w], s1, ALU.mult)
                    dve.tensor_tensor(tb[:, :, half_n:w], x[:, :, 0:half_n], s2, ALU.mult).then_inc(S(sems[0]), 1)
                    dve.wait_ge(S(sems[0]), items + 1)
                    dve.tensor_tensor(out, ta, tb, ALU.add).then_inc(S(sems[1]), 1)

                def norm_rope(t):
                    r, q = rows(t), A(l, t)
                    dve.wait_ge(S("a_zs"), q + 1)
                    if t >= 2:
                        dve.wait_ge(S("a_root"), q - 1)
                    dve.tensor_scalar(mse[t % 2][0:r, :], ms[t % 2][0:r, :], RMS_EPS, None, ALU.add)\
                       .then_inc(S("a_mse"), 1)
                    if t >= 1:
                        dve.wait_ge(S("kv_out"), 16 * (3 * q))
                        dve.wait_ge(S("a_stack_hi"), q)
                        dve.wait_ge(S("a_stack_lo"), q)
                        dve.wait_ge(S("a_post"), q)
                    dve.wait_ge(S(f"ht_in{t % 2}"), 16 * (2 * (5 * l + t // 2 + 1)))
                    ro = rot[t % 2]
                    z10 = zs[0:r, SQ0:SV0].rearrange("p (h d) -> p h d", d=HD)
                    rotate(zr[0:r, :, :], z10, rta[0:r, :, :], rtb[0:r, :, :], ro[0:r, 0:64], ro[0:r, 64:128],
                           r, 10, HD // 2, ("a_rot1", "a_rot2"), q)
                    k1 = zs[0:r, KR0:SQ0].rearrange("p (h d) -> p h d", h=1)
                    dve.wait_ge(S("a_rot2"), q + 1)
                    rotate(kv1[0:r, LAT:LAT + ROPE].rearrange("p (h d) -> p h d", h=1), k1,
                           rta[0:r, 0:1, 0:ROPE], rtb[0:r, 0:1, 0:ROPE], ro[0:r, 128:160], ro[0:r, 160:192],
                           r, 1, ROPE // 2, ("a_rot3", "a_rot4"), q)
                    dve.wait_ge(S("a_root"), q + 1)
                    dve.scalar_tensor_tensor(out=cqn[0:r, :], in0=zs[0:r, 0:QL], scalar=mrs[t % 2][0:r, 0:1],
                                             in1=qkvg[0:r, 0:QL], op0=ALU.mult, op1=ALU.mult)
                    dve.scalar_tensor_tensor(out=kv1[0:r, 0:LAT], in0=zs[0:r, QL:KR0], scalar=mrs[t % 2][0:r, 1:2],
                                             in1=qkvg[0:r, QL:QL + LAT], op0=ALU.mult, op1=ALU.mult)\
                       .then_inc(S("a_rope"), 1)

                def stack_lo(t):
                    r = rows(t)
                    dve.wait_ge(S("a_stack_hi"), A(l, t) + 1)
                    dve.tensor_tensor(vl[0:r, t, :], kv1[0:r, 0:LAT], f(vh[0:r, t, :]), ALU.subtract)
                    for i in (1, 3):
                        dve.tensor_tensor(krs[0:r, i, :], kv1[0:r, LAT:LAT + ROPE], f(krs[0:r, 0, :]), ALU.subtract)
                    for i in range(2):
                        dve.tensor_tensor(kss[0:r, :, 1, i, :], zr[0:r, 8:10, :], f(kss[0:r, :, 0, 0, :]), ALU.subtract)
                    dve.tensor_tensor(sqs[0:r, :, 1, :], zr[0:r, 0:8, :], f(sqs[0:r, :, 0, :]), ALU.subtract)\
                       .then_inc(S("a_stack_lo"), 1)

                def post_lo(t):
                    r = rows(t)
                    dve.wait_ge(S("a_post_hi"), A(l, t) + 1)
                    b5 = Sb[1][:, 1024:1536].rearrange("p (k n) -> p k n", n=P)
                    dve.tensor_tensor(cqTs[:, 1, :, 0:r], b5[:, 0:2, 0:r], f(cqTs[:, 0, :, 0:r]), ALU.subtract)
                    dve.tensor_tensor(ckvTl[:, cols(t)], b5[:, 2, 0:r], f(ckvTh[:, cols(t)]), ALU.subtract)
                    dve.tensor_copy(skT[:, :, :, cols(t)].rearrange("p g a n -> p (g a) n"), heads(Tb[0][:, :], r))\
                       .then_inc(S("a_post_lo"), 1)

                x_lo(0)
                for n in range(TILES + 1):
                    if n + 1 < TILES:
                        x_lo(n + 1)
                    if n < TILES:
                        norm_rope(n)
                    if n >= 1:
                        post_lo(n - 1)
                    if n < TILES:
                        stack_lo(n)
                barrier(dve, phase_no(l, "A"))

                split_lo(dve, l, "B")
                params(dve, (l, "B"))
                dve.tensor_scalar(nsink[:, :], sinkT[:, :], -1.0, None, ALU.mult)
                dve.memset(f(maskq[:, :]), 0.0)
                dve.memset(f(maskk[:, :]), MASKED).then_inc(S("mask_zero"), 1)
                dve.wait_ge(S("mask_zero"), l + 1)
                dve.memset(f(maskq[0:1, 0:CH]), 1.0).then_inc(S("mask"), 1)

                def bias(u):
                    a = u["a"]
                    i, q = a % 2, AT(l, a)
                    dve.wait_ge(S("s_done"), q + 1)
                    if a >= 2:
                        dve.wait_ge(S("probs"), q - 1)
                    k, sbuf = u["kind"], Sb[u["buf"]]
                    if k.startswith("mla"):
                        dve.tensor_reduce(mx[i][:, 0:1], score_view(u), AX.X, ALU.max, negate=True).then_inc(S("mx"), 1)
                        dve.wait_ge(S("mx"), q + 1)
                        dve.tensor_scalar(nb[i][:, 0:1], mx[i][:, 0:1], MLA_SCALE, None, ALU.mult)\
                           .then_inc(S("bias"), 1)
                        return
                    if k == "swa":
                        n, js, sk = min(u["arg"], 2) * CH + CH + META, 4, slice(0, 4)
                        dve.tensor_reduce(mx[i][:, 0:4], sbuf[:, 0:1024].rearrange("p (j n) -> p j n", n=256)[:, :, 0:n],
                                          AX.X, ALU.max, negate=True).then_inc(S("mx"), 1)
                    else:
                        n, js, sk = (WKEYS + NS if k == "swa_d" else META), 1, slice(4, 5)
                        for g in range(KVH):
                            p = slice(CH * g, CH * g + CH)
                            ins = dve.tensor_reduce(mx[i][p, 0:1], sbuf[p, 256 * g:256 * g + n], AX.X, ALU.max,
                                                    negate=True)
                        ins.then_inc(S("mx"), 1)
                    dve.wait_ge(S("mx"), q + 1)
                    dve.scalar_tensor_tensor(out=nb[i][:, 0:js], in0=mx[i][:, 0:js], scalar=SWA_SCALE,
                                             in1=nsink[:, sk], op0=ALU.mult, op1=ALU.min).then_inc(S("nbs"), 1)
                    dve.wait_ge(S("nbs"), l * N_SWA + u["w"] + 1)
                    dve.tensor_tensor(es[i][:, 0:js], nb[i][:, 0:js], sinkT[:, sk], ALU.add).then_inc(S("bias"), 1)

                def inverse(u):
                    a = u["a"]
                    i, q = a % 2, AT(l, a)
                    dve.wait_ge(S("probs"), q + 1)
                    k = u["kind"]
                    if k == "mla":
                        if u["oa"] >= 2:
                            dve.wait_ge(S("oa_out"), QN(l, "oa", u["oa"] - 2) + 1)
                        h = head_at(u["h"])
                        dve.reciprocal(ri[u["oa"] % 2][:, h:h + 1], sm[i][:, 0:1]).then_inc(S("rinv"), 1)
                        return
                    if k.startswith("mla"):
                        n = META if k == "mla_m" else CKEYS + NS
                        dve.reciprocal(rin[u["a"] % 4][:, 0:1], sm[i][:, 0:1]).then_inc(S("rinv"), 1)
                        dve.wait_ge(S("rinv"), q + 1)
                        dve.tensor_scalar(Pb[i][:, 0:n], Pb[i][:, 0:n], rin[u["a"] % 4][:, 0:1], None, ALU.mult)\
                           .then_inc(S("pnorm"), 1)
                        return
                    js = 4 if k == "swa" else 1
                    dve.tensor_tensor(den[i][:, 0:js], sm[i][:, 0:js], ee[i][:, 0:js], ALU.add).then_inc(S("den"), 1)
                    dve.wait_ge(S("den"), l * N_SWA + u["w"] + 1)
                    dve.reciprocal(rin[u["a"] % 4][:, 0:js], den[i][:, 0:js]).then_inc(S("rinv"), 1)

                def unit_lo(u):
                    i = u["a"] % 2
                    for g in range(len(u["sizes"])):
                        gg = G(l, u["g0"] + g)
                        dve.wait_ge(S("probsT_hi"), gg + 1)
                        kk, w, at = group_shape(u, g)
                        dve.tensor_tensor(PTl[i][0:kk, at:at + w], Tb[gg % 2][0:kk, 0:w], f(PTh[i][0:kk, at:at + w]),
                                          ALU.subtract).then_inc(S("probsT_lo"), 1)

                def out_lo(u):
                    i, q = u["a"] % 2, AT(l, u["a"])
                    if u["kind"].startswith("mla"):
                        dve.wait_ge(S("ol_hi"), mla_ord(l, u) + 1)
                        dve.tensor_tensor(out_view(oll, u), o_view(u), f(out_view(olh, u)), ALU.subtract)\
                           .then_inc(S("out_read"), 1)
                        return
                    dve.wait_ge(S("pv"), q + 1)
                    if per_slot[u["w"] % 2] * l + u["before_dmas"] > 0:
                        dve.wait_ge(S(f"mixs_out{u['w'] % 2}"), 16 * (per_slot[u["w"] % 2] * l + u["before_dmas"]))
                    dve.wait_ge(S("rinv"), q + 1)
                    dst = mixs[u["w"] % 2]
                    if u["kind"] == "swa":
                        dve.tensor_tensor(dst[:, :, :], OB[:, 0:4 * HD].rearrange("p (j d) -> p j d", d=HD),
                                          rin[u["a"] % 4][:, 0:4].rearrange("p (j d) -> p j d", d=1).to_broadcast([P, 4, HD]),
                                          ALU.mult).then_inc(S("out_read"), 1)
                        return
                    for g in range(KVH):
                        p = slice(CH * g, CH * g + CH)
                        ins = dve.tensor_scalar(dst[p, 0, :], OB[p, HD * g:HD * g + HD], rin[u["a"] % 4][p, 0:1],
                                                None, ALU.mult)
                    ins.then_inc(S("out_read"), 1)

                def q_unit(u):
                    k, q, t = u["kind"], QN(l, u["kind"], u["i"]), u["arg"]
                    r, s, sbuf = rows(t), u["i"] % 2, Sb[u["buf"]]
                    if k == "qa":
                        dve.wait_ge(S("qa_hi"), q + 1)
                        if u["i"] >= 1:
                            dve.wait_ge(S("qb"), q)
                        dve.tensor_tensor(qnl[:, :, 0:r], heads(sbuf[:, 0:512], r), f(qnh[:, :, 0:r]), ALU.subtract)\
                           .then_inc(S("qa_lo"), 1)
                        dve.wait_ge(S(f"q_in{s}"), 16 * (3 * (l * N_Q["qa"] // 2 + u["i"] // 2 + 1)))
                        if u["i"] >= 1:
                            dve.wait_ge(S("qrs_hi"), q)
                            dve.wait_ge(S("qrs_lo"), q)
                        x = sbuf[0:r, 512:768].rearrange("p (h d) -> p h d", d=ROPE)
                        ro = rotB[s]
                        rotate(qr_raw[0:r, :, :], x, qra[0:r, :, :], qrb[0:r, :, :], ro[0:r, 128:160],
                               ro[0:r, 160:192], r, HEADS, ROPE // 2, ("qa_rot", "qa_rope"), q)
                    elif k == "qb":
                        dve.wait_ge(S("qb_hi"), q + 1)
                        dve.tensor_tensor(q_to(qll[s], t), q_from(sbuf[:, 0:1024], t), q_to(f(qlh[s][:, :]), t),
                                          ALU.subtract).then_inc(S("qb_lo"), 1)
                    elif k == "oa":
                        dve.wait_ge(S("oa"), q + 1)
                        if q >= 1:
                            dve.wait_ge(S("mixo_out"), 16 * q)
                        if t < 8:
                            dve.tensor_tensor(mixo[:, :].rearrange("p (h d) -> p h d", d=HD),
                                              sbuf[:, 0:512].rearrange("p (h d) -> p h d", d=HD),
                                              ri[u["i"] % 2][:, :].rearrange("p (h d) -> p h d", d=1)
                                              .to_broadcast([P, HEADS, HD]), ALU.mult).then_inc(S("oa_out"), 1)
                        else:
                            dve.tensor_copy(mixo[0:r, :], sbuf[0:r, 0:512]).then_inc(S("oa_out"), 1)

                def rope_lo(u):
                    r, q = rows(u["arg"]), QN(l, "qa", u["i"])
                    dve.wait_ge(S("qrs_hi"), q + 1)
                    for i in range(2):
                        ins = dve.tensor_tensor(qrs[0:r, :, 2 + i, :], qr_raw[0:r, :, :], f(qrs[0:r, :, 0, :]),
                                                ALU.subtract)
                    ins.then_inc(S("qrs_lo"), 1)

                def attend(units):
                    for n in range(len(units) + 2):
                        u = units[n] if n < len(units) else None
                        v = units[n - 1] if 1 <= n <= len(units) else None
                        w = units[n - 2] if n >= 2 else None
                        if u is not None:
                            if "a" in u:
                                bias(u)
                            elif u["kind"] != "oa":
                                q_unit(u)
                        if v is not None and "a" in v:
                            unit_lo(v)
                        if w is not None and "a" in w:
                            out_lo(w)
                        if u is not None:
                            if "a" in u:
                                inverse(u)
                            if u["kind"] == "mla_d" and u["arg"] + 1 < NB:
                                latents_lo(u["arg"] + 1)
                            if u["kind"] == "swa_d" and u["arg"] + 1 < NB:
                                window_lo(u["arg"] + 1)
                            if u["kind"] == "qa":
                                rope_lo(u)
                            if u["kind"] == "oa":
                                q_unit(u)

                def latents_lo(b):
                    s = b % 2
                    dve.wait_ge(S("dm_hi"), l * NB + b + 1)
                    dve.tensor_tensor(dkl[s][:, :], dkraw[:, :], f(dkh[s][:, :]), ALU.subtract)
                    for i in (1, 3):
                        p = slice(ROPE * i, ROPE * i + ROPE)
                        dve.tensor_tensor(drs[s][p, :], drraw[p, :], f(drs[s][p, :]), ALU.subtract)
                    dve.tensor_tensor(dvl[s][:, 0:8, :], dvraw[:, 0:8, :], f(dvh[s][:, 0:8, :]), ALU.subtract)
                    dve.tensor_tensor(dvl[s][0:32, 8, :], dvraw[0:32, 8, :], f(dvh[s][0:32, 8, :]), ALU.subtract)\
                       .then_inc(S("dm_lo"), 1)

                def window_lo(b):
                    s = b % 2
                    dve.wait_ge(S("ds_hi"), l * NB + b + 1)
                    dve.tensor_tensor(dsh[s][:, :, 1, :], dsraw[:, :, :], f(dsh[s][:, :, 0, :]), ALU.subtract)
                    dve.tensor_tensor(dul[s][:, 0, :], duraw[:, 0, :], f(duh[s][:, 0, :]), ALU.subtract)
                    dve.tensor_tensor(dul[s][0:32, 1, :], duraw[0:32, 1, :], f(duh[s][0:32, 1, :]), ALU.subtract)\
                       .then_inc(S("ds_lo"), 1)

                attend(UB)
                barrier(dve, phase_no(l, "B"))
                latents_lo(0)
                window_lo(0)
                attend(UE)
                barrier(dve, phase_no(l, "E"))

                split_lo(dve, l, "C")
                params(dve, (l, "C"))

                def mix_norm(t):
                    r, q = rows(t), A(l, t)
                    dve.wait_ge(S("c_ms"), q + 1)
                    if t >= 2:
                        dve.wait_ge(S("c_root"), q - 1)
                    dve.tensor_scalar(mse[t % 2][0:r, :], ms[t % 2][0:r, :], RMS_EPS, None, ALU.add)\
                       .then_inc(S("c_mse"), 1)
                    dve.wait_ge(S("c_root"), q + 1)
                    if t >= 1:
                        dve.wait_ge(S("c_mT"), q)
                    for i in range(2):
                        ins = dve.scalar_tensor_tensor(out=mn[0:r, 512 * i:512 * i + 512],
                                                       in0=mt[0:r, 512 * i:512 * i + 512],
                                                       scalar=mrs[t % 2][0:r, i:i + 1],
                                                       in1=mixg[0:r, 512 * i:512 * i + 512],
                                                       op0=ALU.mult, op1=ALU.mult)
                    ins.then_inc(S("c_mixn"), 1)

                def mix_lo(t):
                    r = rows(t)
                    dve.wait_ge(S("c_mh"), A(l, t) + 1)
                    dve.tensor_tensor(mTl[:, :, 0:r], heads(Sb[0][:, 0:1024], r), f(mTh[:, :, 0:r]),
                                      ALU.subtract).then_inc(S("c_ml"), 1)

                def residual(t):
                    r, q = rows(t), A(l, t)
                    dve.wait_ge(S("c_y"), q + 1)
                    dve.wait_ge(S("hc_in"), 16 * (q + 1))
                    dve.scalar_tensor_tensor(out=x1[0:r, :], in0=hc[0:r, :], scalar=ALPHA, in1=Sb[1][0:r, 0:1024],
                                             op0=ALU.mult, op1=ALU.add).then_inc(S("c_res"), 1)
                    dve.wait_ge(S("c_res"), q + 1)
                    ln_stats(dve, qC(l, t), x1, r)
                    if t >= 1:
                        dve.wait_ge(S("c_hT"), q)
                    ln_apply(dve, qC(l, t), x1, h1, ln1, r)

                def h1_lo(t):
                    r = rows(t)
                    dve.wait_ge(S("c_xh"), A(l, t) + 1)
                    for i in range(2):
                        ins = dve.tensor_tensor(xl[:, 4 * i:4 * i + 4, cols(t)], heads(Tb[i][:, :], r),
                                                f(xh[:, 4 * i:4 * i + 4, cols(t)]), ALU.subtract)
                    ins.then_inc(S("c_xl"), 1)

                mix_norm(0)
                mix_lo(0)
                for n in range(TILES + 1):
                    if n + 1 < TILES:
                        mix_norm(n + 1)
                    if n >= 1:
                        h1_lo(n - 1)
                    if n + 1 < TILES:
                        mix_lo(n + 1)
                    if n < TILES:
                        residual(n)
                barrier(dve, phase_no(l, "C"))

                for k in range(KD):
                    dve.wait_ge(S("f_acc0"), KD * l + k + 1)
                    dve.scalar_tensor_tensor(out=acc[:, k, :], in0=f(xl[:, k, :]), scalar=ALPHA, in1=acc[:, k, :],
                                             op0=ALU.mult, op1=ALU.add).then_inc(S("f_acc"), 1)

                def hidden(j, c):
                    for i in range(3):
                        g = gate[:, N0[i]:N0[i] + NT[i]]
                        dve.wait_ge(S("f_silu"), j * 6 + (6 * TURNS * l + 3 * c + i + 1))
                        dve.wait_ge(S("f_up"), j * 6 + (6 * TURNS * l + 3 * c + i + 1))
                        dve.tensor_tensor(g, u_bank(i), g, ALU.mult).then_inc(S("f_hid"), 1)
                    for i in range(3):
                        g = gate[:, N0[i]:N0[i] + NT[i]]
                        dve.wait_ge(S("f_hidh"), j * 6 + (6 * TURNS * l + 3 * c + i + 1))
                        dve.tensor_tensor(hidl[c][:, N0[i]:N0[i] + NT[i]], g, f(hidh[c][:, N0[i]:N0[i] + NT[i]]),
                                          ALU.subtract).then_inc(S("f_hidl"), 1)

                def add_down(j):
                    for e in range(24):
                        k, i = e // 3, e % 3
                        a = acc[:, k, N0[i]:N0[i] + NT[i]]
                        dve.wait_ge(S("f_down"), j * 24 + (24 * TURNS * l + e + 1))
                        dve.tensor_tensor(a, a, Tb[e % 2][:, 0:NT[i]], ALU.add).then_inc(S("f_y"), 1)

                dve.wait_ge(S("f_acc"), KD * l + KD)
                hidden(0, 0)
                hidden(0, 1)
                with dve.Fori(1, TURNS) as j:
                    add_down(j - 1)
                    hidden(j, 0)
                    hidden(j, 1)
                add_down(TURNS - 1)
                barrier(dve, phase_no(l, "F"))

                params(dve, (l, "D"))
                for t in range(TILES + 1):
                    if t < TILES:
                        dve.wait_ge(S("d_xo"), A(l, t) + 1)
                        ln_stats(dve, qD(l, t), xo[t % 2], rows(t))
                    if t >= 1:
                        v = t - 1
                        if 5 * l + v // 2 >= 1:
                            dve.wait_ge(S(f"yo_out{v % 2}"), 16 * (5 * l + v // 2))
                        ln_apply(dve, qD(l, v), xo[v % 2], yo[v % 2], lnd, rows(v))
                barrier(dve, phase_no(l, "D"))

        @block.tensor
        def _(pe):
            def three(out, wh, wl, mh, ml, start, stop):
                pe.matmul(out, wh, mh, start=start, stop=False)
                pe.matmul(out, wh, ml, start=False, stop=False)
                return pe.matmul(out, wl, mh, start=False, stop=stop)

            pe.wait_ge(S("ident"), 1)
            pe.wait_ge(S("t_zero"), 2)
            barrier(pe, 1)
            for l in range(L):
                def x_T(t):
                    r = rows(t)
                    pe.wait_ge(S(f"ht_in{t % 2}"), 16 * (2 * (5 * l + t // 2 + 1)))
                    if t >= 1:
                        pe.wait_ge(S("a_xl"), A(l, t - 1) + 1)
                    if t >= 3:
                        pe.wait_ge(S("a_sqT"), A(l, t - 3) + 1)
                    for k in range(KD):
                        ins = pe.transpose(Sb[1][:, k * P:k * P + r], ht[t % 2][0:r, k * P:k * P + P], ident[0:r, 0:r])
                    ins.then_inc(S("a_xT"), 1)

                def z(t):
                    r = rows(t)
                    pe.wait_ge(S("a_xl"), A(l, t) + 1)
                    if t >= 1:
                        pe.wait_ge(S("a_zs"), A(l, t - 1) + 1)
                    for k in range(KD):
                        for c0, c1 in ((0, 512), (512, 1024), (1024, INW)):
                            ins = three(Sb[0][0:r, c0:c1], xTh[t % 2][:, k, 0:r], xTl[t % 2][:, k, 0:r],
                                        winh[:, k, c0:c1], winl[:, k, c0:c1], k == 0, k == KD - 1)
                    ins.then_inc(S("a_z"), 1)

                def post(t):
                    r = rows(t)
                    i = ident[0:r, 0:r]
                    pe.wait_ge(S("a_rope"), A(l, t) + 1)
                    pe.wait_ge(S("a_stack_lo"), A(l, t) + 1)
                    if t >= 1:
                        pe.wait_ge(S("a_post_lo"), A(l, t - 1) + 1)
                    for k in range(2):
                        pe.transpose(Sb[1][:, 1024 + k * P:1024 + k * P + r], cqn[0:r, k * P:k * P + P], i)
                    pe.transpose(Sb[1][:, 1280:1280 + r], kv1[0:r, 0:LAT], i)
                    pe.transpose(Sb[1][:, 1408:1408 + r], f(krs[0:r, :, :]).rearrange("p a d -> p (a d)"), i)
                    for k in range(4):
                        pe.transpose(Tb[0][:, k * P:k * P + r],
                                     f(kss[0:r, k // 2, k % 2, :, :]).rearrange("p a d -> p (a d)"), i)
                    pe.wait_ge(S("a_xl"), A(l, min(t + 2, TILES - 1)) + 1)
                    for k in range(SWA_H):
                        ins = pe.transpose(Sb[1][:, k * P:k * P + r],
                                           f(sqs[0:r, k, :, :]).rearrange("p a d -> p (a d)"), i)
                    ins.then_inc(S("a_post"), 1)

                x_T(0)
                all_split(pe, l, "A")
                for n in range(TILES + 1):
                    if n + 1 < TILES:
                        x_T(n + 1)
                    if n < TILES:
                        z(n)
                    if n >= 1:
                        post(n - 1)
                barrier(pe, phase_no(l, "A"))

                all_split(pe, l, "B")
                pe.wait_ge(S("mask"), l + 1)

                def scores(u):
                    k, n, t = u["kind"], u["n"], u["arg"]
                    sbuf = Sb[u["buf"]]
                    free_scores(pe, l, u)
                    if k in ("qa", "qb", "qc", "oa"):
                        q_scores(u, sbuf)
                        return
                    tt = t if k == "mla" else (9 if k.endswith("_m") else (8 if k.endswith("_d") else t // 2))
                    i = q_index[tt]
                    s = i % 2
                    if k.startswith("mla"):
                        pe.wait_ge(S("qb_lo"), QN(l, "qb", i) + 1)
                        pe.wait_ge(S("qc_out"), QN(l, "qc", i) + 1)
                        if k == "mla":
                            at = P * u["h"]
                        else:
                            at = 0 if k == "mla_m" else P * t
                        a, b, c = (x[s][:, at:at + P] for x in (qlh, qll, qrT))

                        def keys(out, kh, kl, kr, more=False):
                            pe.matmul(out, a, kh, start=True, stop=False)
                            pe.matmul(out, a, kl, start=False, stop=False)
                            pe.matmul(out, b, kh, start=False, stop=False)
                            return pe.matmul(out, c, kr, start=False, stop=not more)

                        if k == "mla":
                            for c0 in range(0, (t + 1) * P, 512):
                                c1 = min(c0 + 512, (t + 1) * P)
                                keys(sbuf[:, c0:c1], ckvTh[:, c0:c1], ckvTl[:, c0:c1], krT[:, c0:c1], more=c1 == (t + 1) * P)
                            pe.matmul(sbuf[:, c1 - CH:c1], maskq[:, :], maskk[:, :], start=False, stop=True)
                            last = sbuf[:, c1:c1 + META] if t < 7 else tail_view(u)
                        elif k == "mla_d":
                            pe.wait_ge(S("dm_lo"), l * NB + t + 1)
                            for c0, c1 in ((0, 512), (512, 1024), (1024, CKEYS)):
                                if c0 == 1024 and u["tail_before"] is not None:
                                    pe.wait_ge(S("probs"), AT(l, u["tail_before"]["a"]) + 1)
                                keys(sbuf[:, c0:c1] if c0 < 1024 else tail_view(u)[:, 0:META],
                                     dkh[t % 2][:, c0:c1], dkl[t % 2][:, c0:c1], drs[t % 2][:, c0:c1])
                            last = tail_view(u)[:, META:META + NS]
                        else:
                            last = sbuf[:, 0:META]
                        o = SAMPLE + NS * t if k == "mla_d" else METAROW
                        if k == "mla" and u["tail"] and u["tail_before"] is not None:
                            pe.wait_ge(S("probs"), AT(l, u["tail_before"]["a"]) + 1)
                        ins = keys(last, ckvTh[:, o:o + NS], ckvTl[:, o:o + NS], krT[:, o:o + NS])
                    elif k == "swa":
                        pe.wait_ge(S(f"sq_in{s}"), 16 * (l * N_Q["qa"] // 2 + i // 2 + 1))
                        q0_ = SWA_H * CH * (t % 2)
                        k0, k1 = CH * max(t - 2, 0), CH * (t + 1)
                        for j in range(4):
                            q = sqT[s][:, q0_ + P * j:q0_ + P * j + P]
                            c0 = 256 * j
                            for (s0, s1), at in (((k0, k1), c0), ((METAROW, TOK), c0 + k1 - k0)):
                                for a in range(2):
                                    ins = pe.matmul(sbuf[:, at:at + s1 - s0], q, skT[:, j // 2, a, s0:s1],
                                                    start=a == 0, stop=a == 1)
                    else:
                        pe.wait_ge(S(f"sq_in{s}"), 16 * (l * N_Q["qa"] // 2 + i // 2 + 1))
                        at = 0 if k == "swa_m" else P * t
                        q = sqT[s][:, at:at + P]
                        if k == "swa_d":
                            pe.wait_ge(S("ds_lo"), l * NB + t + 1)
                        for g in range(KVH):
                            c0, o = 256 * g, METAROW
                            if k == "swa_d":
                                for a in range(2):
                                    pe.matmul(sbuf[:, c0:c0 + WKEYS], q, dsh[t % 2][:, g, a, :], start=a == 0, stop=a == 1)
                                c0, o = c0 + WKEYS, SAMPLE + NS * t
                            for a in range(2):
                                ins = pe.matmul(sbuf[:, c0:c0 + NS], q, skT[:, g, a, o:o + NS],
                                                start=a == 0, stop=a == 1)
                    ins.then_inc(S("s_done"), 1)

                def q_scores(u, sbuf):
                    k, t, i = u["kind"], u["arg"], u["i"]
                    r, s, q = rows(t), i % 2, QN(l, k, i)
                    if k == "qa":
                        pe.wait_ge(S(f"q_in{s}"), 16 * (3 * (l * N_Q["qa"] // 2 + i // 2 + 1)))
                        for m in range(4):
                            for kk in range(2):
                                three(sbuf[:, m * P:m * P + r], wuqh[:, kk, m * P:m * P + P], wuql[:, kk, m * P:m * P + P],
                                      cq[s][:, 0, kk, 0:r], cq[s][:, 1, kk, 0:r], kk == 0, kk == 1)
                        for kk in range(2):
                            ins = three(sbuf[0:r, 512:768], cq[s][:, 0, kk, 0:r], cq[s][:, 1, kk, 0:r],
                                        wuqh[:, kk, 512:768], wuql[:, kk, 512:768], kk == 0, kk == 1)
                    elif k == "qb":
                        pe.wait_ge(S("qa_lo"), q + 1)
                        for h in range(HEADS):
                            p = slice(64 * (h % 2), 64 * (h % 2) + 64)
                            c0 = P * place_of(h)
                            ins = three(sbuf[:, c0:c0 + r], wukh[p, h // 2, :], wukl[p, h // 2, :],
                                        qnh[p, h // 2, 0:r], qnl[p, h // 2, 0:r], True, True)
                    elif k == "qc":
                        pe.wait_ge(S("qrs_lo"), q + 1)
                        for h in range(HEADS):
                            c0 = P * place_of(h)
                            ins = pe.transpose(sbuf[:, c0:c0 + r],
                                               f(qrs[0:r, h, :, :]).rearrange("p a d -> p (a d)"), ident[0:r, 0:r])
                    else:
                        last = u["last_mla"]
                        pe.wait_ge(S("out_read"), AT(l, last) + 1)
                        for h in range(HEADS):
                            ins = three(sbuf[0:r, h * HD:h * HD + HD], olh[:, place_of(h), 0:r], oll[:, place_of(h), 0:r],
                                        wuvh[:, h * HD:h * HD + HD], wuvl[:, h * HD:h * HD + HD], True, True)
                    ins.then_inc(S(k), 1)

                def blocks_of(u):
                    k, t = u["kind"], u["arg"]
                    if k == "mla":
                        at = u["tail"] * u["buf"]
                        return [(at + P * j, P) for j in range(t + 1)] + [(0 if at else (t + 1) * P, META)]
                    if k == "mla_d":
                        at = u["tail"] * u["buf"]
                        return [(at + P * j, P) for j in range(8)] + [(0 if at else PAST, META + NS)]
                    if k == "swa":
                        w = min(t, 2) * CH
                        return [(256 * j, w) for j in range(4 if w else 0)] + \
                            [(256 * j + w, CH + META) for j in range(4)]
                    if k == "swa_d":
                        return [(0, P), (P, META + NS)]
                    return [(0, META)]

                def turn_probs(u, groups):
                    for g in groups:
                        if g == 0:
                            if u["kind"] in ("mla_m", "mla_d"):
                                pe.wait_ge(S("pnorm"), norm_ord(l, u) + 1)
                            else:
                                pe.wait_ge(S("probs"), AT(l, u["a"]) + 1)
                        gg = G(l, u["g0"] + g)
                        if gg >= 2:
                            pe.wait_ge(S("probsT_lo"), gg - 1)
                        for b in range(u["sizes"][g]):
                            c0, w = blocks_of(u)[sum(u["sizes"][:g]) + b]
                            ins = pe.transpose(Tb[gg % 2][0:w, b * P:b * P + P], Pb[u["a"] % 2][:, c0:c0 + w],
                                               ident[:, :])
                        ins.then_inc(S("probsT"), 1)

                def values(u):
                    k, a, t = u["kind"], u["a"], u["arg"]
                    i = a % 2
                    blocks = blocks_of(u)
                    pe.wait_ge(S("probsT_lo"), G(l, u["g0"] + len(u["sizes"]) - 1) + 1)
                    if u["out_before"] is not None:
                        pe.wait_ge(S("out_read"), AT(l, u["out_before"]["a"]) + 1)
                    th, tl = PTh[i], PTl[i]
                    if k.startswith("mla"):
                        out = OB[:, 0:P]
                        for b, (c0, w) in enumerate(blocks):
                            if k == "mla_d":
                                v1, v2 = dvh[t % 2][0:w, b, :], dvl[t % 2][0:w, b, :]
                            else:
                                tile = b if (k == "mla" and b <= t) else 9
                                v1, v2 = vh[0:w, tile, :], vl[0:w, tile, :]
                            ins = three(out, v1, v2, th[0:w, b * P:b * P + P], tl[0:w, b * P:b * P + P],
                                        b == 0, b == len(blocks) - 1)
                    elif k == "swa":
                        w = min(t, 2) * CH
                        for j in range(4):
                            out, d = OB[:, HD * j:HD * j + HD], slice(HD * (j // 2), HD * (j // 2) + HD)
                            if w:
                                three(out, th[0:w, j * P:j * P + P], tl[0:w, j * P:j * P + P],
                                      VFh[0:w, t, d], VFl[0:w, t, d], True, False)
                            e = 512 + j * P
                            ins = three(out, th[0:CH + META, e:e + P], tl[0:CH + META, e:e + P],
                                        VXh[0:CH + META, t, d], VXl[0:CH + META, t, d], not w, True)
                    else:
                        out = OB[:, 0:P]
                        for b, (c0, w) in enumerate(blocks):
                            v1, v2 = (duh[t % 2][0:w, b, :], dul[t % 2][0:w, b, :]) if k == "swa_d" else (svmh[:, :], svml[:, :])
                            ins = three(out, th[0:w, b * P:b * P + P], tl[0:w, b * P:b * P + P], v1, v2,
                                        b == 0, b == len(blocks) - 1)
                    ins.then_inc(S("pv"), 1)

                def attend(units):
                    for n in range(len(units) + 2):
                        u = units[n] if n < len(units) else None
                        v = units[n - 1] if 1 <= n <= len(units) else None
                        w = units[n - 2] if n >= 2 else None
                        if u is not None and u["kind"] != "oa":
                            scores(u)
                        if v is not None and "a" in v:
                            turn_probs(v, range(min(2, len(v["sizes"]))))
                        if w is not None and "a" in w:
                            values(w)
                        if v is not None and "a" in v:
                            turn_probs(v, range(2, len(v["sizes"])))
                        if u is not None and u["kind"] == "oa":
                            scores(u)

                attend(UB)
                barrier(pe, phase_no(l, "B"))
                attend(UE)
                barrier(pe, phase_no(l, "E"))

                def mix_T(t):
                    r = rows(t)
                    pe.wait_ge(S("c_mixn"), A(l, t) + 1)
                    if t >= 1:
                        pe.wait_ge(S("c_ml"), A(l, t - 1) + 1)
                    for k in range(KD):
                        ins = pe.transpose(Sb[0][:, k * P:k * P + r], mn[0:r, k * P:k * P + P], ident[0:r, 0:r])
                    ins.then_inc(S("c_mT"), 1)

                def w_out(t):
                    r = rows(t)
                    pe.wait_ge(S("c_ml"), A(l, t) + 1)
                    if t >= 1:
                        pe.wait_ge(S("c_res"), A(l, t - 1) + 1)
                    for k in range(KD):
                        for c0 in (0, 512):
                            ins = three(Sb[1][0:r, c0:c0 + 512], mTh[:, k, 0:r], mTl[:, k, 0:r],
                                        wouth[:, k, c0:c0 + 512], woutl[:, k, c0:c0 + 512], k == 0, k == KD - 1)
                    ins.then_inc(S("c_y"), 1)

                def h1_T(t):
                    r = rows(t)
                    pe.wait_ge(S("ln_out"), qC(l, t) + 1)
                    if t >= 1:
                        pe.wait_ge(S("c_xl"), A(l, t - 1) + 1)
                    for k in range(KD):
                        ins = pe.transpose(Tb[k // 4][:, (k % 4) * P:(k % 4) * P + r], h1[0:r, k * P:k * P + P],
                                           ident[0:r, 0:r])
                    ins.then_inc(S("c_hT"), 1)

                mix_T(0)
                all_split(pe, l, "C")
                for n in range(TILES + 1):
                    if n + 1 < TILES:
                        mix_T(n + 1)
                    if n < TILES:
                        w_out(n)
                    if n >= 1:
                        h1_T(n - 1)
                barrier(pe, phase_no(l, "C"))

                def up_or_gate(j, c, which, first_turn):
                    k0 = TURN_ITEMS.index((1, c, which)) if not first_turn else None
                    slot = 2 * c + which
                    if first_turn:
                        pe.wait_ge(S("f_lo"), W_ITEMS * l + slot + 1)
                    else:
                        pe.wait_ge(S("f_lo"), j * 6 + (W_ITEMS * l + 4 - 6 + k0 + 1))
                    bank = u_bank if which else g_bank
                    for i in range(3):
                        if not (first_turn and c == 0):
                            pe.wait_ge(S("f_hid" if which else "f_silu"),
                                       j * 6 + (6 * TURNS * l + 3 * c + i - 3 + 1))
                        for k in range(KD):
                            ins = three(bank(i), fwh[slot][:, k, :], fwl[slot][:, k, :],
                                        xh[:, k, N0[i]:N0[i] + NT[i]], xl[:, k, N0[i]:N0[i] + NT[i]],
                                        k == 0, k == KD - 1)
                        ins.then_inc(S("f_up" if which else "f_gate"), 1)

                def down(j, last):
                    items = LAST_ITEMS if last else TURN_ITEMS
                    pe.wait_ge(S("f_lo"), j * 6 + (W_ITEMS * l + 4 + items.index((0, 1, 2)) + 1))
                    pe.wait_ge(S("f_hidl"), j * 6 + (6 * TURNS * l + 6))
                    for e in range(24):
                        k, i = e // 3, e % 3
                        if e >= 2:
                            pe.wait_ge(S("f_y"), j * 24 + (24 * TURNS * l + e - 1))
                        for c in range(2):
                            ins = three(Tb[e % 2][:, 0:NT[i]], fwh[4 + c][:, k, :], fwl[4 + c][:, k, :],
                                        hidh[c][:, N0[i]:N0[i] + NT[i]], hidl[c][:, N0[i]:N0[i] + NT[i]],
                                        c == 0, c == 1)
                        ins.then_inc(S("f_down"), 1)

                for c in range(2):
                    for which in range(2):
                        up_or_gate(0, c, which, True)
                with pe.Fori(1, TURNS) as j:
                    up_or_gate(j, 0, 0, False)
                    down(j - 1, False)
                    up_or_gate(j, 0, 1, False)
                    up_or_gate(j, 1, 0, False)
                    up_or_gate(j, 1, 1, False)
                down(TURNS - 1, True)
                barrier(pe, phase_no(l, "F"))

                for t in range(TILES):
                    r = rows(t)
                    if t >= 2:
                        pe.wait_ge(S("d_xo"), A(l, t - 2) + 1)
                    for k in range(KD):
                        ins = pe.transpose(Sb[t % 2][0:r, k * P:k * P + P], acc[:, k, cols(t)], ident[:, :])
                    ins.then_inc(S("d_T"), 1)
                barrier(pe, phase_no(l, "D"))


def kernel(x_prompt, x_sample, cache_mla_ckv, cache_mla_krope, cache_swa_k, cache_swa_v,
           meta_tokens, in_ln_g, in_ln_b, w_in, mla_q_norm_g, mla_w_uq, mla_kv_norm_g,
           mla_w_uk, mla_w_uv, swa_sinks, out_norm_mla_g, out_norm_swa_g, w_out,
           ln1_g, ln1_b, ffn_w_gate, ffn_w_up, ffn_w_down, ln2_g, ln2_b):
    import concourse.bacc as bacc
    from concourse.bass_utils import run_bass_kernel_spmd

    def C(a):
        return np.ascontiguousarray(a)

    def pair(g, b):
        return np.concatenate([g, b], axis=-1)

    pos = np.concatenate([META + np.arange(SEQ), np.tile(META + PAST + np.arange(NS), NB), np.arange(META)])
    parts = []
    for d in (HD, ROPE):
        inv = np.power(np.float32(10000.0), -(np.arange(d // 2, dtype=np.float32) * np.float32(2.0 / d)))
        ang = pos.astype(np.float32)[:, None] * inv[None, :].astype(np.float32)
        c, s = np.cos(ang), np.sin(ang)
        parts += [c, c, -s, s]
    rot = C(np.concatenate(parts, axis=1).astype(np.float32))

    sk = np.asarray(cache_swa_k).reshape(L, NB, WKEYS, KVH * HD)
    sinks = np.asarray(swa_sinks)
    lanes = np.arange(P)
    sink_rows = np.stack([sinks[:, 2 * j + lanes // CH] for j in range(4)] + [sinks[:, lanes // NS]], axis=-1)
    uq = np.asarray(mla_w_uq)
    gu = [np.asarray(w).reshape(L, KD, P, FC, P).transpose(0, 3, 2, 1, 4).reshape(L, FC, P, D)
          for w in (ffn_w_gate, ffn_w_up)]
    w_ff = np.stack(gu + [np.asarray(ffn_w_down).reshape(L, FC, P, D)], axis=2)
    arrays = {
        "X": np.concatenate([np.asarray(x_prompt)[0], np.asarray(x_sample).reshape(NB * NS, D),
                             np.asarray(meta_tokens)], axis=0),
        "LNP": np.concatenate([pair(in_ln_g, in_ln_b)[None], pair(ln2_g, ln2_b)], axis=0),
        "ROT": rot,
        "W_IN": np.asarray(w_in),
        "QKVG": pair(mla_q_norm_g, mla_kv_norm_g),
        "W_UQ": np.concatenate([uq[..., 0:64].reshape(L, QL, 512), uq[..., 64:96].reshape(L, QL, 256)], axis=-1),
        "W_UK": np.asarray(mla_w_uk).transpose(0, 2, 3, 1).reshape(L, HEADS * 64, LAT),
        "W_UV": np.asarray(mla_w_uv).reshape(L, LAT, HEADS * 64),
        "SINKS": sink_rows,
        "MIXG": pair(out_norm_mla_g, out_norm_swa_g),
        "W_OUT": np.asarray(w_out),
        "LN1": pair(ln1_g, ln1_b),
        "W_FF": w_ff,
        "CKVT": np.asarray(cache_mla_ckv).transpose(0, 1, 3, 2),
        "CKV": np.asarray(cache_mla_ckv),
        "KRT": np.asarray(cache_mla_krope).transpose(0, 1, 3, 2),
        "SKT": sk.transpose(0, 1, 3, 2),
        "SK": sk,
        "SV": np.asarray(cache_swa_v).reshape(L, NB, WKEYS, KVH * HD),
    }
    outs = {"H": (L + 1, TOK, D), "KVS": (L, TOK, KVW), "NSK": (L, NB, WKEYS, KVH * HD), "NSV": (L, NB, WKEYS, KVH * HD)}
    nc = bacc.Bacc("TRN2", target_bir_lowering=False, num_devices=1)
    feed, args = {}, []
    for name, a in arrays.items():
        feed[f"in_{name}"] = C(a)
        args.append(nc.dram_tensor(f"in_{name}", a.shape, F32, kind="ExternalInput").ap())
    for name, shape in outs.items():
        args.append(nc.dram_tensor(f"out_{name}", shape, F32, kind="ExternalOutput").ap())
    program(nc, *args)
    got = run_bass_kernel_spmd(nc, [feed], core_ids=[0]).results[0]
    h, kv, nk, nv = (np.asarray(got[f"out_{n}"]) for n in outs)

    meta, seq, smp = slice(METAROW, TOK), slice(0, SEQ), slice(SAMPLE, METAROW)
    k0, v0 = LAT + ROPE, LAT + ROPE + KVH * HD

    def prompt(c0, c1, n):
        return np.concatenate([kv[:, meta, c0:c1], kv[:, SEQ - n:SEQ, c0:c1]], axis=1)[:, None]

    def sample(c0, c1):
        return kv[:, smp, c0:c1].reshape(L, NB, NS, c1 - c0)

    def kvh(a):
        return a.reshape(a.shape[:-1] + (KVH, HD))

    return (h[L, seq][None], h[L, smp].reshape(NB, NS, D),
            prompt(0, LAT, SEQ), prompt(LAT, k0, SEQ), kvh(prompt(k0, v0, WIN)), kvh(prompt(v0, KVW, WIN)),
            sample(0, LAT), sample(LAT, k0), kvh(nk), kvh(nv))
```

```python
from contextlib import ExitStack

import numpy as np

import concourse.bass as bass
from concourse import mybir

F32 = mybir.dt.float32
F32R = mybir.dt.float32r
ALU = mybir.AluOpType
ACT = mybir.ActivationFunctionType
AX = mybir.AxisListType

P = 128
L = 2
D = 1024
KD = D // P
SEQ = 1024
NB = 8
NS = 16
META = 16
CH = 64
PAST = 1024
WIN = 128
HEADS = 8
QL = 256
LAT = 128
ROPE = 32
HD = 64
KVH = 2
SWA_H = 8
FF = 2816
FC = FF // P
TILES = 10
TOK = SEQ + NB * NS + META
SAMPLE = SEQ
METAROW = SEQ + NB * NS
INW = 1184
KR0 = QL + LAT
SQ0 = KR0 + ROPE
SK0 = SQ0 + SWA_H * HD
SV0 = SK0 + KVH * HD
KVW = LAT + ROPE + 2 * KVH * HD
CKEYS = META + PAST
WKEYS = META + WIN
NCH = SEQ // CH
TURNS = FC // 2
TURN_ITEMS = [(1, 0, 0), (0, 0, 2), (0, 1, 2), (1, 0, 1), (1, 1, 0), (1, 1, 1)]
LAST_ITEMS = [(0, 0, 2), (0, 1, 2)]
W_ITEMS = 4 + 6 * (TURNS - 1) + 2
NT = (390, 390, 388)
N0 = (0, 390, 780)
Z_BLOCKS = ((0, 396), (396, 790), (790, INW))
B_FIRST = 5
B_ITEMS = 16
ALPHA = (2.0 * L) ** 0.25
MLA_SCALE = (64 + ROPE) ** -0.5
SWA_SCALE = HD ** -0.5
LN_EPS = 1e-5
RMS_EPS = 1e-6
MASKED = -1e30
BANK = 512


def rows(t):
    return META if t == TILES - 1 else P


def cols(t):
    return slice(t * P, t * P + rows(t))


def place_of(h):
    return (h % 2) * (HEADS // 2) + h // 2


def head_at(place):
    return (place % (HEADS // 2)) * 2 + place // (HEADS // 2)


def key_cols(t):
    c0 = 0 if t == TILES - 1 else META + t * P
    return slice(c0, c0 + rows(t))


def plan_units():
    prompt = [("qa", 9), ("qb", 9), ("qc", 9), ("mla_m", 9), ("qa", 0), ("swa_m", 9), ("qb", 0), ("oa", 9), ("qc", 0)]
    for t in range(8):
        nxt = t + 1
        if (t + 1) * P + META <= BANK:
            pairs = [[("mla2", t, h)] for h in range(0, HEADS, 2)]
        else:
            pairs = [[("mla", t, h), ("mla", t, h + 1)] for h in range(0, HEADS, 2)]
        prompt += pairs[0] + [("qa", nxt)] + pairs[1] + [("swa", 2 * t), ("qb", nxt)] + pairs[2] + pairs[3] + \
            [("qc", nxt), ("swa", 2 * t + 1), ("oa", t)]
    decode = []
    for b in range(NB):
        decode += [("mla_d", b), ("swa_d", b)]
    decode += [("oa", 8)]
    units, att, groups, swa, vals = [], 0, 0, 0, 0
    nq = {"qa": 0, "qb": 0, "qc": 0, "oa": 0}
    for n, what in enumerate(prompt + decode):
        u = {"n": n, "kind": what[0], "arg": what[1], "h": what[2] if len(what) > 2 else 0, "buf": n % 2,
             "before": units[n - 2] if n >= 2 else None}
        k = u["kind"]
        if k in nq:
            u["i"] = nq[k]
            nq[k] += 1
        else:
            u["v"], u["opens"] = vals, k != "mla" or u["h"] % 2 == 0
            u["closes"] = k != "mla" or u["h"] % 2 == 1
            vals += u["closes"]
            u["tail"] = {"mla": META if u["arg"] == 7 else 0, "mla_d": META + NS}.get(k, 0)
            u["tail_before"] = next((v for v in reversed(units) if v.get("tail")), None)
            u["a"] = att
            att += 1
            if k == "mla":
                nblk = u["arg"] + 2
            elif k == "mla2":
                nblk = 2 * (u["arg"] + 2)
            elif k == "mla_m":
                nblk = 1
            elif k == "mla_d":
                nblk = 9
            if k.startswith("mla"):
                u["sizes"] = [min(4, nblk - g) for g in range(0, nblk, 4)]
                u["oa"] = nq["oa"]
            elif k == "swa":
                u["sizes"] = [4, 4] if u["arg"] else [4]
            elif k == "swa_d":
                u["sizes"] = [2]
            else:
                u["sizes"] = [1]
            if k.startswith("swa"):
                u["w"] = swa
                swa += 1
            u["g0"] = groups
            groups += len(u["sizes"])
        units.append(u)
    return units[:len(prompt)], units[len(prompt):], att, groups, swa, vals, nq


UB, UE, N_ATT, N_GRP, N_SWA, N_VAL, N_Q = plan_units()


def program(nc, X, LNP, ROT, W_IN, QKVG, W_UQ, W_UK, W_UV, SINKS, MIXG, W_OUT, LN1, W_FF,
            CKVT, CKV, KRT, SKT, SK, SV, H, KVS, NSK, NSV):
    MIX = nc.dram_tensor("mix_scratch", [TOK, D], F32).ap()
    CQT = nc.dram_tensor("cqt_scratch", [TILES, P, 4 * P], F32).ap()
    SQT = nc.dram_tensor("sqt_scratch", [TILES, P, SWA_H * P], F32).ap()

    with ExitStack() as ctx:
        names = {}

        def S(name):
            if name not in names:
                names[name] = ctx.enter_context(nc.semaphore(name))
            return names[name]

        base = nc.sbuf_base
        top = nc.sbuf_usable_end
        start = ((base + 31) // 32) * 32

        class Map:
            def __init__(self, at):
                self.at = at

            def __call__(self, name, shape, dt=F32):
                free = int(np.prod(shape[1:])) * 4
                t = nc.alloc_sbuf_tensor_at(name, shape, dt, offset=self.at)
                self.at += (free + 31) // 32 * 32
                assert self.at <= top, (name, self.at, top)
                return t

        m = Map(start)
        ident = m("ident", [P, P])
        half = m("half", [P, 1])
        stats = [m(f"stats{i}", [P, 12]) for i in range(2)]
        mv = [m(f"mv{i}", [P, 2]) for i in range(2)]
        veps = [m(f"veps{i}", [P, 1]) for i in range(2)]
        rstd = [m(f"rstd{i}", [P, 1]) for i in range(2)]
        ms = [m(f"ms{i}", [P, 2]) for i in range(2)]
        mse = [m(f"mse{i}", [P, 2]) for i in range(2)]
        mrs = [m(f"mrs{i}", [P, 2]) for i in range(2)]
        raw_at = m.at
        raw = [m(f"raw{i}", [P, INW]) for i in range(2)]
        common = m.at

        ckvTh = m("ckvTh", [P, TOK], F32R)
        ckvTl = m("ckvTl", [P, TOK], F32R)
        krT = m("krT", [P, TOK], F32R)
        skT_at = m.at
        skT = m("skT", [P, KVH, 2, TOK], F32R)
        vh_at = m.at
        vh = m("vh", [P, TILES, P], F32R)
        vl = m("vl", [P, TILES, P], F32R)
        after_kv = m.at

        ht = [m(f"ht{i}", [P, D]) for i in range(2)]
        xTh = [m(f"xTh{i}", [P, KD, P], F32R) for i in range(2)]
        xTl = [m(f"xTl{i}", [P, KD, P], F32R) for i in range(2)]
        zs = m("zs", [P, INW])
        cqn = m("cqn", [P, QL])
        kv1 = m("kv1", [P, LAT + ROPE])
        zr = m("zr", [P, 10, HD])
        rta = m("rta", [P, 10, HD])
        rot = [m(f"rot{i}", [P, 192]) for i in range(2)]
        qkvg = m("qkvg", [P, QL + LAT])
        krs = m("krs", [P, 4, ROPE], F32R)
        kss = m("kss", [P, KVH, 2, 2, HD], F32R)
        sqs = m("sqs", [P, SWA_H, 2, HD], F32R)
        cqTs = m("cqTs", [P, 2, 2, P], F32R)
        sqTs = m("sqTs", [P, SWA_H * P], F32R)
        junkA = m("junkA", [P, QL + LAT])
        rtb = m("rtb", [P, 10, HD])
        m.at = max(m.at, common + 3 * KD * TOK * 4)
        winh = m("winh", [P, KD, INW], F32R)
        winl = m("winl", [P, KD, INW], F32R)

        m = Map(after_kv)
        x0 = [m(f"x0_{i}", [P, D]) for i in range(2)]
        y0 = [m(f"y0_{i}", [P, D]) for i in range(2)]
        lnp = m("lnp", [P, 2 * D])

        m = Map(after_kv)
        wuvh = m("wuvh", [P, 512], F32R)
        wuvl = m("wuvl", [P, 512], F32R)
        only_b = m.at
        wuqh = m("wuqh", [P, 2, 768], F32R)
        wuql = m("wuql", [P, 2, 768], F32R)
        wukh = m("wukh", [P, 4, P], F32R)
        wukl = m("wukl", [P, 4, P], F32R)
        cq = [m(f"cq{i}", [P, 2, 2, P], F32R) for i in range(2)]
        qnh = m("qnh", [P, 4, P], F32R)
        qnl = m("qnl", [P, 4, P], F32R)
        qr_raw = m("qr_raw", [P, HEADS, ROPE])
        qra = m("qra", [P, HEADS, ROPE])
        qrb = m("qrb", [P, HEADS, ROPE])
        qrs = m("qrs", [P, HEADS, 4, ROPE], F32R)
        rotB = [m(f"rotB{i}", [P, 192]) for i in range(2)]
        only_b_end = m.at
        qrT = [m(f"qrT{i}", [P, HEADS * P], F32R) for i in range(2)]
        qlh = [m(f"qlh{i}", [P, HEADS * P], F32R) for i in range(2)]
        qll = [m(f"qll{i}", [P, HEADS * P], F32R) for i in range(2)]
        sqT = [m(f"sqT{i}", [P, SWA_H * P], F32R) for i in range(2)]
        olh = m("olh", [P, HEADS, P], F32R)
        oll = m("oll", [P, HEADS, P], F32R)
        Pb = [m(f"Pb{i}", [P, 1056]) for i in range(2)]
        PTh = [m(f"PTh{i}", [P, 9 * 2 * P], F32R) for i in range(2)]
        PTl = [m("PTl0", [P, 9 * 2 * P], F32R), None]
        mixo = m("mixo", [P, 512])
        mixs = [m(f"mixs{i}", [P, 4, HD]) for i in range(2)]
        mx = [m(f"mx{i}", [P, 4]) for i in range(2)]
        nb = [m(f"nb{i}", [P, 4]) for i in range(2)]
        sm = [m(f"sm{i}", [P, 4]) for i in range(2)]
        es = [m(f"es{i}", [P, 4]) for i in range(2)]
        ee = [m(f"ee{i}", [P, 4]) for i in range(2)]
        den = [m(f"den{i}", [P, 4]) for i in range(2)]
        rin = [m(f"rin{i}", [P, 4]) for i in range(4)]
        ri = [m(f"ri{i}", [P, HEADS]) for i in range(2)]
        sinkT = m("sinkT", [P, 5])
        nsink = m("nsink", [P, 5])
        maskq = m("maskq", [1, P], F32R)
        maskk = m("maskk", [1, CH], F32R)
        after_b = m.at
        PTl[1] = Map(raw_at)("PTl1", [P, 9 * 2 * P], F32R)
        VFh = m("VFh", [P, NCH, P], F32R)
        VFl = m("VFl", [P, NCH, P], F32R)
        VXh = m("VXh", [P, NCH, P], F32R)
        VXl = m("VXl", [P, NCH, P], F32R)
        svmh = m("svmh", [META, P], F32R)
        svml = m("svml", [META, P], F32R)
        rawB = [m(f"rawB{i}", [P, 512]) for i in range(2)]

        m = Map(only_b)
        keys0, keys1 = Map(skT_at), Map(skT_at + 4 * TOK)
        second = Map(vh_at)
        dkraw = [m("dkraw0", [P, CKEYS]), second("dkraw1", [P, CKEYS])]
        drraw = [m("drraw0", [P, CKEYS]), second("drraw1", [P, CKEYS])]
        assert second.at <= after_kv
        dvraw = [m("dvraw0", [P, PAST]), keys0("dvraw1", [P, PAST])]
        dtraw = [m("dtraw0", [P, P]), keys1("dtraw1", [P, P])]
        dsraw = [m("dsraw0", [P, KVH * WKEYS]), keys1("dsraw1", [P, KVH * WKEYS])]
        duraw = [m("duraw0", [P, 2 * P]), keys1("duraw1", [P, 2 * P])]
        assert keys0.at <= skT_at + 4 * SEQ and keys1.at <= skT_at + 4 * (TOK + SEQ)
        drs = [m(f"drs{i}", [P, CKEYS], F32R) for i in range(2)]
        dsh = [m(f"dsh{i}", [P, KVH, 2, WKEYS], F32R) for i in range(2)]
        duh = [m(f"duh{i}", [P, 2, P], F32R) for i in range(2)]
        dul = [m(f"dul{i}", [P, 2, P], F32R) for i in range(2)]
        assert m.at <= only_b_end
        m = Map(after_b)
        dkh = [m(f"dkh{i}", [P, CKEYS], F32R) for i in range(2)]
        dkl = [m(f"dkl{i}", [P, CKEYS], F32R) for i in range(2)]
        dvh = [m(f"dvh{i}", [P, 9, P], F32R) for i in range(2)]
        dvl = [m(f"dvl{i}", [P, 9, P], F32R) for i in range(2)]

        m = Map(common)
        xh = m("xh", [P, KD, TOK], F32R)
        xl = m("xl", [P, KD, TOK], F32R)
        after_x = m.at
        wouth = m("wouth", [P, KD, D], F32R)
        woutl = m("woutl", [P, KD, D], F32R)
        mt = m("mt", [P, D])
        mn = m("mn", [P, D])
        hc = m("hc", [P, D])
        mTh = [m(f"mTh{i}", [P, KD, P], F32R) for i in range(2)]
        mTl = [m(f"mTl{i}", [P, KD, P], F32R) for i in range(2)]
        x1 = m("x1", [P, D])
        h1 = m("h1", [P, D])
        ln1 = m("ln1", [P, 2 * D])
        mixg = m("mixg", [P, D])
        junkC = m("junkC", [P, D])
        rawC = [m(f"rawC{i}", [P, D]) for i in range(2)]

        m = Map(common)
        m.at = after_x
        acc = m("acc", [P, KD, TOK])
        hidh = [m(f"hidh{i}", [P, TOK], F32R) for i in range(2)]
        hidl = [m(f"hidl{i}", [P, TOK], F32R) for i in range(2)]
        gate = m("gate", [P, TOK])
        fwh = [m(f"fwh{i}", [P, KD, P], F32R) for i in range(6)]
        fwl = [m(f"fwl{i}", [P, KD, P], F32R) for i in range(6)]
        fraw = [raw[0][:, 0:D].rearrange("p (k f) -> p k f", f=P), raw[1][:, 0:D].rearrange("p (k f) -> p k f", f=P),
                m("fraw2", [P, KD, P])[:, :, :]]

        m = Map(common)
        xo = [m(f"xo{i}", [P, D]) for i in range(2)]
        yo = [m(f"yo{i}", [P, D]) for i in range(2)]
        lnd = m("lnd", [P, 2 * D])

        PS = ctx.enter_context(nc.psum_tensor("PS", [P, 8 * BANK], F32))
        Sb = [PS[:, 3 * BANK * i:3 * BANK * (i + 1)] for i in range(2)]
        Tb = [PS[:, (6 + i) * BANK:(7 + i) * BANK] for i in range(2)]
        OB = PS[:, 5 * BANK:6 * BANK]
        YB = [PS[:, (2 + 2 * i) * BANK:(4 + 2 * i) * BANK] for i in range(2)]
        block = ctx.enter_context(nc.Block())

        def f(ap):
            return ap.bitcast(F32)

        def barrier(eng, k):
            eng.drain().then_inc(S("phase_done"), 1)
            eng.wait_ge(S("phase_done"), 5 * k)

        def phase_no(l, which):
            return 1 + 1 + 6 * l + "ABECFD".index(which)

        def split_items(l, which):
            if which == "A":
                w = W_IN[l].rearrange("(k p) n -> p k n", p=P)
                return [([(lambda r, k=k: r[:, 0:INW], w[:, k, :])], lambda r: r[:, 0:INW],
                         winh[:, k, :], winl[:, k, :]) for k in range(KD)]
            if which == "C":
                w = W_OUT[l].rearrange("(k p) n -> p k n", p=P)
                return [([(lambda r: r[:, 0:D], w[:, k, :])], lambda r: r[:, 0:D],
                         wouth[:, k, :], woutl[:, k, :]) for k in range(KD)]
            w = W_UQ[l].rearrange("(k p) n -> p k n", p=P)
            items = [([(lambda r, n=c1 - c0: r[:, 0:n], w[:, k, c0:c1])], lambda r, n=c1 - c0: r[:, 0:n],
                      wuqh[:, k, c0:c1], wuql[:, k, c0:c1]) for k in range(2) for c0, c1 in ((0, 512), (512, 768))]
            cut = lambda r: r[:, 0:512]
            cut3 = lambda r: r[:, 0:512].rearrange("p (j n) -> p j n", n=P)
            items += [([(cut3, W_UK[l].rearrange("(j p) n -> p j n", p=P))], cut3, wukh[:, :, :], wukl[:, :, :]),
                      ([(cut, W_UV[l])], cut, wuvh[:, :], wuvl[:, :])]
            v = KVS[l][:, LAT + ROPE + KVH * HD:KVW]
            c2 = lambda r: r[0:META, 0:P]
            items.append(([(c2, v[METAROW:TOK, :])], c2, svmh[:, :], svml[:, :]))
            for odd in range(2):
                for j0, j1 in ((0, 4), (4, 7)):
                    cut = lambda r, n=j1 - j0: r[:, 0:n * P].rearrange("p (j n) -> p j n", n=P)
                    r0 = CH * odd + P * j0
                    c = slice(2 + odd + 2 * j0, 1 + odd + 2 * j1, 2)
                    items.append(([(cut, v[r0:r0 + P * (j1 - j0), :].rearrange("(j p) n -> p j n", p=P))], cut,
                                  VFh[:, c, :], VFl[:, c, :]))
            c1 = lambda r: r[0:CH, 0:P]
            items.append(([(c1, v[0:CH, :])], c1, VFh[0:CH, 1, :], VFl[0:CH, 1, :]))
            for c0 in range(0, NCH, 4):
                a = lambda r: r[0:CH, 0:4 * P].rearrange("p (c n) -> p c n", n=P)
                full = lambda r: r[0:CH + META, 0:4 * P].rearrange("p (c n) -> p c n", n=P)
                dm = [(a, v[CH * c0:CH * (c0 + 4), :].rearrange("(c p) n -> p c n", p=CH))]
                dm += [(lambda r, c=c: r[CH:CH + META, c * P:(c + 1) * P], v[METAROW:TOK, :]) for c in range(4)]
                items.append((dm, full, VXh[0:CH + META, c0:c0 + 4, :], VXl[0:CH + META, c0:c0 + 4, :]))
            return items

        def raw_slot(i, which):
            if which == "B":
                return i - 2 if i in (2, 3) else 4 + i % 2
            return i % (4 if which == "C" else 2)

        def raw_of(i, which):
            return (raw + rawC + rawB)[raw_slot(i, which)]

        def raw_before(i, which):
            return max([j for j in range(i) if raw_slot(j, which) == raw_slot(i, which)], default=None)

        first, n_dma, n_item = {}, [0] * 6, 0
        landed = []
        for l in range(L):
            for which in "ABC":
                first[l, which] = n_item
                for i, it in enumerate(split_items(l, which)):
                    slot = raw_slot(i, which)
                    n_dma[slot] += len(it[0])
                    landed.append(n_dma[slot])
                    n_item += 1

        def load_split(sp, l, which, part=slice(None)):
            for i, it in list(enumerate(split_items(l, which)))[part]:
                if raw_before(i, which) is not None:
                    sp.wait_ge(S("split_lo"), first[l, which] + raw_before(i, which) + 1)
                for place, src in it[0]:
                    sp.dma_start(place(raw_of(i, which)), src).then_inc(S(f"raw{raw_slot(i, which)}_in"), 16)

        def split_hi(act, l, which, part=slice(None)):
            for i, it in list(enumerate(split_items(l, which)))[part]:
                q = first[l, which] + i
                act.wait_ge(S(f"raw{raw_slot(i, which)}_in"), 16 * landed[q])
                act.activation(it[2], it[1](raw_of(i, which)), ACT.Copy).then_inc(S("split_hi"), 1)

        def split_lo(dve, l, which, part=slice(None)):
            for i, it in list(enumerate(split_items(l, which)))[part]:
                q = first[l, which] + i
                dve.wait_ge(S("split_hi"), q + 1)
                dve.tensor_tensor(it[3], it[1](raw_of(i, which)), f(it[2]), ALU.subtract).then_inc(S("split_lo"), 1)

        def all_split(pe, l, which):
            pe.wait_ge(S("split_lo"), first[l, which] + len(split_items(l, which)))

        def ln_stats(dve, q, x, r):
            if q >= 2:
                dve.wait_ge(S("ln_out"), q - 1)
            dve.bn_stats(stats[q % 2][0:r, 0:6], x[0:r, 0:512])
            dve.bn_stats(stats[q % 2][0:r, 6:12], x[0:r, 512:D]).then_inc(S("ln_stats"), 1)
            dve.wait_ge(S("ln_stats"), q + 1)
            dve.bn_aggr(mv[q % 2][0:r, :], stats[q % 2][0:r, :]).then_inc(S("ln_mv"), 1)
            dve.wait_ge(S("ln_mv"), q + 1)
            dve.tensor_scalar(veps[q % 2][0:r, :], mv[q % 2][0:r, 1:2], LN_EPS, None, ALU.add).then_inc(S("ln_eps"), 1)

        def ln_root(pool, q, r):
            pool.wait_ge(S("ln_eps"), q + 1)
            pool.wait_ge(S("half_set"), 1)
            pool.tensor_tensor(rstd[q % 2][0:r, :], veps[q % 2][0:r, :], half[0:r, :], ALU.pow).then_inc(S("ln_root"), 1)

        def ln_apply(dve, q, x, y, gb, r):
            dve.scalar_tensor_tensor(out=y[0:r, :], in0=x[0:r, :], scalar=mv[q % 2][0:r, 0:1], in1=gb[0:r, 0:D],
                                     op0=ALU.subtract, op1=ALU.mult).then_inc(S("ln_norm"), 1)
            dve.wait_ge(S("ln_root"), q + 1)
            dve.wait_ge(S("ln_norm"), q + 1)
            dve.scalar_tensor_tensor(out=y[0:r, :], in0=y[0:r, :], scalar=rstd[q % 2][0:r, 0:1], in1=gb[0:r, D:2 * D],
                                     op0=ALU.mult, op1=ALU.add).then_inc(S("ln_out"), 1)

        def q0(t):
            return t

        def qC(l, t):
            return TILES + 2 * TILES * l + t

        def qD(l, t):
            return 2 * TILES + 2 * TILES * l + t

        def small_loads(l, which):
            if which == "0":
                return [(lnp[:, :], LNP[0:1, :].to_broadcast([P, 2 * D]))]
            if which == "A":
                return [(qkvg[:, :], QKVG[l:l + 1, :].to_broadcast([P, QL + LAT]))]
            if which == "B":
                return [(sinkT[:, :], SINKS[l])]
            if which == "C":
                return [(ln1[:, :], LN1[l:l + 1, :].to_broadcast([P, 2 * D])),
                        (mixg[:, :], MIXG[l:l + 1, :].to_broadcast([P, D]))]
            return [(lnd[:, :], LNP[l + 1:l + 2, :].to_broadcast([P, 2 * D]))]

        param_count, total = {}, 0
        for key in ["0"] + [(l, w) for l in range(L) for w in "ABCD"]:
            total += len(small_loads(0, key) if key == "0" else small_loads(*key))
            param_count[key] = total

        def load_params(sp, l, which):
            for dst, src in small_loads(l, which):
                sp.dma_start(dst, src).then_inc(S("params_in"), 16)

        def params(eng, key):
            eng.wait_ge(S("params_in"), 16 * param_count[key])

        def A(l, t):
            return l * TILES + t

        def AT(l, a):
            return l * N_ATT + a

        def V(l, v):
            return l * N_VAL + v

        def G(l, g):
            return l * N_GRP + g

        def QN(l, kind, i):
            return l * N_Q[kind] + i

        q_order = [u["arg"] for u in UB if u["kind"] == "qa"]
        q_index = {t: i for i, t in enumerate(q_order)}
        att_units = [u for u in UB + UE if "a" in u]
        mlas = [u for u in att_units if u["kind"].startswith("mla") and u["closes"]]
        normed = [u for u in mlas if u["kind"] in ("mla_m", "mla_d")]
        for i, u in enumerate(mlas):
            u["mla_i"] = i
        for i, u in enumerate(normed):
            u["norm_i"] = i
        for u in UB + UE:
            if u["kind"] == "oa":
                u["last_mla"] = max(v["v"] for v in mlas if v["oa"] == u["i"])

        def mla_ord(l, u):
            return len(mlas) * l + u["mla_i"]

        def norm_ord(l, u):
            return len(normed) * l + u["norm_i"]

        dec = {(u["kind"], u["arg"]): u["v"] for u in UE if "a" in u}
        per_slot = [0, 0]
        for u in att_units:
            if "w" in u:
                u["before_dmas"] = per_slot[u["w"] % 2]
                per_slot[u["w"] % 2] += 2 if u["kind"] == "swa" else 1

        def turned(u, g, bank, pt):
            k, w = u["kind"], u["sizes"][g] * P
            kk, at = P, 512 * g
            if k == "mla":
                src = bank[:, 0:w].rearrange("p (b n) -> p b n", n=P)
                dst = pt.rearrange("p (b h n) -> p b h n", h=2, n=P)
                return src, dst[:, 4 * g:4 * g + u["sizes"][g], u["h"] % 2, :]
            if k == "swa":
                if len(u["sizes"]) == 2 and g == 0:
                    kk = min(u["arg"], 2) * CH
                else:
                    kk, at = CH + META, 512
            elif k == "mla_m" or k == "swa_m":
                kk = META
            return bank[0:kk, 0:w], pt[0:kk, at:at + w]

        def key_count(u):
            if u["kind"] == "mla2":
                return (u["arg"] + 1) * P + META
            return {"mla": (u["arg"] + 1) * P + META, "mla_m": META, "mla_d": CKEYS + NS}[u["kind"]]

        def score_view(u):
            c0 = 0 if u["buf"] == 0 else 3 * BANK - u["tail"]
            return PS[:, c0:c0 + key_count(u)]

        def tail_view(u):
            c0 = 2 * BANK if u["buf"] == 0 else 3 * BANK - u["tail"]
            return PS[:, c0:c0 + u["tail"]]

        def o_view(u):
            if u["kind"] in ("mla", "mla2"):
                return OB[:, 0:2 * P].rearrange("p (h t) -> p h t", t=P)
            return OB[:, 0:P].rearrange("p (h t) -> p h t", t=NS)

        def out_view(ol, u):
            if u["kind"] in ("mla", "mla2"):
                h = u["h"] // 2 * 2
                return ol[:, h:h + 2, :]
            at = 0 if u["kind"] == "mla_m" else NS * u["arg"]
            return ol[:, :, at:at + NS]

        def q_to(flat, t, chunks=False):
            if t == 9:
                return flat[:, 0:P].rearrange("p (h n) -> p h n", n=META)
            n = NB if t == 8 else 2
            if t < 8 and not chunks:
                return flat[:, :].rearrange("p (h n) -> p h n", n=P)
            return flat[:, :].rearrange("p (c h n) -> p h c n", c=n, h=HEADS)

        def q_from(ap, t, chunks=False):
            v = ap.rearrange("p (h n) -> p h n", n=P)
            if t == 9:
                return v[:, :, 0:META]
            if t < 8 and not chunks:
                return v
            return v.rearrange("p h (c n) -> p h c n", c=NB if t == 8 else 2)

        def heads(ap, r):
            return ap.rearrange("p (k n) -> p k n", n=P)[:, :, 0:r]

        def free_scores(eng, l, u):
            b = u["before"]
            if b is None:
                return
            if "a" in b:
                eng.wait_ge(S("probs"), AT(l, b["a"]) + 1)
            elif b["kind"] == "oa":
                eng.wait_ge(S("oa_out"), QN(l, "oa", b["i"]) + 1)
            else:
                done = {"qa": "qa_rope", "qb": "qb_lo", "qc": "qc_out"}[b["kind"]]
                eng.wait_ge(S(done), QN(l, b["kind"], b["i"]) + 1)

        last_swa = {}
        for u in UB:
            if u["kind"] == "swa":
                last_swa[u["arg"] // 2] = u["v"]
            if u["kind"] == "swa_m":
                last_swa[9] = u["v"]

        @block.sync
        def _(sp):
            load_params(sp, 0, "0")
            for t in range(TILES):
                if t >= 2:
                    sp.wait_ge(S("ln_norm"), q0(t - 2) + 1)
                sp.dma_start(x0[t % 2][0:rows(t), :], X[cols(t), :]).then_inc(S(f"x0_in{t % 2}"), 16)
                if t >= 1:
                    load_split(sp, 0, "A", slice(t - 1, t))
            barrier(sp, 1)
            for l in range(L):
                load_params(sp, l, "A")
                for t in range(2):
                    sp.dma_start(ht[t][0:rows(t), :], H[l, cols(t), :]).then_inc(S(f"ht_in{t}"), 16)
                    sp.dma_start(rot[t][0:rows(t), :], ROT[cols(t), :]).then_inc(S(f"rot_in{t}"), 16)
                for t in range(2, TILES):
                    sp.wait_ge(S("a_xT"), A(l, t - 2) + 1)
                    sp.dma_start(ht[t % 2][0:rows(t), :], H[l, cols(t), :]).then_inc(S(f"ht_in{t % 2}"), 16)
                    sp.wait_ge(S("a_rope"), A(l, t - 2) + 1)
                    sp.dma_start(rot[t % 2][0:rows(t), :], ROT[cols(t), :]).then_inc(S(f"rot_in{t % 2}"), 16)
                load_split(sp, l, "B", slice(0, 4))
                barrier(sp, phase_no(l, "A"))
                load_params(sp, l, "B")
                for i, t in enumerate(q_order):
                    r = rows(t)
                    if i == 2:
                        load_split(sp, l, "B", slice(4, None))
                    if i >= 2:
                        sp.wait_ge(S("qa"), QN(l, "qa", i - 2) + 1)
                        sp.wait_ge(S("qa_rope"), QN(l, "qa", i - 2) + 1)
                    for a in range(2):
                        sp.dma_start(f(cq[i % 2][:, a, :, 0:r]),
                                     CQT[t].rearrange("p (a k n) -> p a k n", a=2, k=2)[:, a, :, 0:r])\
                          .then_inc(S(f"q_in{i % 2}"), 16)
                    sp.dma_start(rotB[i % 2][0:r, :], ROT[cols(t), :]).then_inc(S(f"q_in{i % 2}"), 16)
                    if i >= 2:
                        sp.wait_ge(S("pv"), V(l, last_swa[q_order[i - 2]]) + 1)
                    sp.dma_start(f(sqT[i % 2][:, 0:SWA_H * r]), SQT[t, :, 0:SWA_H * r]).then_inc(S(f"sq_in{i % 2}"), 16)
                for b in range(NB):
                    if b == 0:
                        sp.wait_ge(S("qc"), QN(l, "qc", N_Q["qc"] - 1) + 1)
                    if b == 1:
                        barrier(sp, phase_no(l, "B"))
                    s = l * NB + b
                    r0 = SAMPLE + NS * b
                    i = b % 2
                    if b >= 2:
                        sp.wait_ge(S("dm_lo"), s - 1)
                    sp.dma_start(dkraw[i][:, :], CKVT[l, b]).then_inc(S(f"dm_in{i}"), 16)
                    for j in range(4):
                        sp.dma_start(drraw[i][ROPE * j:ROPE * (j + 1), :], KRT[l, b]).then_inc(S(f"dm_in{i}"), 16)
                    if b >= 2:
                        sp.wait_ge(S("ds_lo"), s - 1)
                    sp.dma_start(dvraw[i][:, :].rearrange("p (j n) -> p j n", n=P),
                                 CKV[l, b, 0:PAST, :].rearrange("(j p) n -> p j n", p=P)).then_inc(S(f"ds_in{i}"), 16)
                    sp.dma_start(dtraw[i][0:META, :], CKV[l, b, PAST:CKEYS, :]).then_inc(S(f"ds_in{i}"), 16)
                    sp.dma_start(dtraw[i][META:META + NS, :], KVS[l, r0:r0 + NS, 0:LAT]).then_inc(S(f"ds_in{i}"), 16)
                    for j in range(2):
                        sp.dma_start(dsraw[i][HD * j:HD * (j + 1), :].rearrange("d (g n) -> d g n", g=KVH),
                                     SKT[l, b].rearrange("(g d) n -> d g n", d=HD)).then_inc(S(f"ds_in{i}"), 16)
                    sp.dma_start(duraw[i][:, 0:P], SV[l, b, 0:P, :]).then_inc(S(f"ds_in{i}"), 16)
                    sp.dma_start(duraw[i][0:META, P:2 * P], SV[l, b, P:WKEYS, :]).then_inc(S(f"ds_in{i}"), 16)
                    sp.dma_start(duraw[i][META:META + NS, P:2 * P],
                                 KVS[l, r0:r0 + NS, LAT + ROPE + KVH * HD:KVW]).then_inc(S(f"ds_in{i}"), 16)
                barrier(sp, phase_no(l, "E"))
                load_params(sp, l, "C")
                sp.dma_start(mt[:, :], MIX[cols(0), :]).then_inc(S("mt_in"), 16)
                sp.dma_start(hc[:, :], H[l, cols(0), :]).then_inc(S("hc_in"), 16)
                for t in range(1, TILES + 1):
                    load_split(sp, l, "C", slice(0, 4) if t == 1 else slice(4, 8) if t == 2 else slice(0))
                    if t < TILES:
                        sp.wait_ge(S("c_mixn"), A(l, t))
                        sp.dma_start(mt[0:rows(t), :], MIX[cols(t), :]).then_inc(S("mt_in"), 16)
                    if t >= 2:
                        sp.wait_ge(S("c_res"), A(l, t - 1))
                        sp.dma_start(hc[0:rows(t - 1), :], H[l, cols(t - 1), :]).then_inc(S("hc_in"), 16)
                def w_load(c, which, slot):
                    sp.dma_start(fraw[slot], W_FF[l, c, which].rearrange("p (k f) -> p k f", f=P))\
                      .then_inc(S(f"fraw_in{slot}"), 16)

                sp.wait_ge(S("split_lo"), first[l, "C"] + KD)
                for k in range(4):
                    if k == 2:
                        barrier(sp, phase_no(l, "C"))
                    if W_ITEMS * l + k >= 3:
                        sp.wait_ge(S("f_lo"), W_ITEMS * l + k - 2)
                    w_load(k // 2, k % 2, k % 3)

                def turn(j, items):
                    for k, (ahead, c, which) in enumerate(items):
                        sp.wait_ge(S("f_lo"), j * 6 + (W_ITEMS * l + 4 + k - 3 + 1))
                        w_load((j + ahead) * 2 + c, which, (4 + k) % 3)

                with sp.Fori(0, TURNS - 1) as j:
                    turn(j, TURN_ITEMS)
                turn(TURNS - 1, LAST_ITEMS)
                barrier(sp, phase_no(l, "F"))
                load_params(sp, l, "D")
                if l + 1 < L:
                    load_split(sp, l + 1, "A")
                barrier(sp, phase_no(l, "D"))

        def store_q(pool, l, t):
            r = rows(t)
            pool.wait_ge(S("a_post_lo"), A(l, t) + 1)
            for a in range(2):
                pool.dma_start(CQT[t].rearrange("p (a k n) -> p a k n", a=2, k=2)[:, a, :, 0:r],
                               f(cqTs[:, a, :, 0:r])).then_inc(S("cqT_out"), 16)
            pool.wait_ge(S("a_sqT"), A(l, t) + 1)
            w = SWA_H * r
            pool.dma_start(SQT[t, :, 0:w], f(sqTs[:, 0:w])).then_inc(S("sqT_out"), 16)

        def store_swa(pool, l, u):
            src = mixs[u["w"] % 2]
            pool.wait_ge(S("out_read"), V(l, u["v"]) + 1)
            name = f"mixs_out{u['w'] % 2}"
            if u["kind"] == "swa":
                c = u["arg"]
                for hh in range(2):
                    dst = MIX[CH * c:CH * c + CH, 512:1024].rearrange("q (j h d) -> q j h d", h=2, d=HD)[:, :, hh, :]
                    pool.dma_start(dst, src[CH * hh:CH * hh + CH, :, :]).then_inc(S(name), 16)
            else:
                r0 = METAROW if u["kind"] == "swa_m" else SAMPLE + NS * u["arg"]
                dst = MIX[r0:r0 + NS, 512:1024].rearrange("t (h d) -> h t d", d=HD)
                pool.dma_start(dst, src[:, 0, :]).then_inc(S(name), 16)

        @block.gpsimd
        def _(pool):
            pool.memset(half[:, :], -0.5).then_inc(S("half_set"), 1)
            pool.memset(ident[:, :], 0.0).then_inc(S("ident_zero"), 1)
            pool.wait_ge(S("ident_zero"), 1)
            pool.affine_select(out=ident[:, :], in_=ident[:, :], compare_op=ALU.not_equal, fill=1.0,
                               base=0, pattern=[[-1, P]], channel_multiplier=1).then_inc(S("ident"), 1)
            for t in range(TILES):
                ln_root(pool, q0(t), rows(t))
                pool.wait_ge(S("ln_out"), q0(t) + 1)
                pool.dma_start(H[0, cols(t), :], y0[t % 2][0:rows(t), :]).then_inc(S(f"y0_out{t % 2}"), 16)
            pool.wait_ge(S("y0_out0"), 16 * (TILES // 2))
            pool.wait_ge(S("y0_out1"), 16 * (TILES // 2))
            barrier(pool, 1)
            for l in range(L):
                for t in range(TILES):
                    r = rows(t)
                    pool.wait_ge(S("a_mse"), A(l, t) + 1)
                    pool.tensor_tensor(mrs[t % 2][0:r, :], mse[t % 2][0:r, :], half[0:r, 0:1].to_broadcast([r, 2]),
                                       ALU.pow).then_inc(S("a_root"), 1)
                    pool.wait_ge(S("a_rope"), A(l, t) + 1)
                    pool.dma_start(KVS[l, cols(t), 0:LAT + ROPE], kv1[0:r, :]).then_inc(S("kv_out"), 16)
                    pool.dma_start(KVS[l, cols(t), LAT + ROPE:LAT + ROPE + KVH * HD],
                                   zr[0:r, 8:10, :]).then_inc(S("kv_out"), 16)
                    pool.dma_start(KVS[l, cols(t), LAT + ROPE + KVH * HD:KVW],
                                   zs[0:r, SV0:INW]).then_inc(S("kv_out"), 16)
                    if t >= 1:
                        store_q(pool, l, t - 1)
                store_q(pool, l, TILES - 1)
                pool.wait_ge(S("cqT_out"), 16 * (2 * TILES * (l + 1)))
                pool.wait_ge(S("sqT_out"), 16 * (TILES * (l + 1)))
                pool.wait_ge(S("kv_out"), 16 * (3 * TILES * (l + 1)))
                barrier(pool, phase_no(l, "A"))
                for part, units in (("B", UB), ("E", UE)):
                    prev = None
                    for u in units + [None]:
                        if prev is not None and (prev["kind"].startswith("swa")):
                            store_swa(pool, l, prev)
                        if u is not None and u["kind"] == "oa":
                            t = u["arg"]
                            pool.wait_ge(S("oa_out"), QN(l, "oa", u["i"]) + 1)
                            pool.dma_start(MIX[cols(t), 0:512], mixo[0:rows(t), :]).then_inc(S("mixo_out"), 16)
                        prev = u
                    if part == "B":
                        pool.wait_ge(S("mixo_out"), 16 * (10 * l + 9))
                    else:
                        pool.wait_ge(S("mixo_out"), 16 * (10 * l + 10))
                        for i in range(2):
                            pool.wait_ge(S(f"mixs_out{i}"), 16 * (per_slot[i] * (l + 1)))
                        for src, dst, c0 in ((SK, NSK, LAT + ROPE), (SV, NSV, LAT + ROPE + KVH * HD)):
                            pool.dma_start(dst[l, :, 0:META, :], src[l, :, 0:META, :]).then_inc(S("cache_out"), 16)
                            pool.dma_start(dst[l, :, META:WIN, :], src[l, :, META + NS:WKEYS, :])\
                                .then_inc(S("cache_out"), 16)
                            pool.dma_start(dst[l, :, WIN:WKEYS, :],
                                           KVS[l, SAMPLE:METAROW, c0:c0 + KVH * HD].rearrange("(b t) n -> b t n", t=NS))\
                                .then_inc(S("cache_out"), 16)
                    barrier(pool, phase_no(l, part))
                for t in range(TILES):
                    r = rows(t)
                    pool.wait_ge(S("c_mse"), A(l, t) + 1)
                    pool.tensor_tensor(mrs[t % 2][0:r, :], mse[t % 2][0:r, :], half[0:r, 0:1].to_broadcast([r, 2]),
                                       ALU.pow).then_inc(S("c_root"), 1)
                    if t >= 2:
                        ln_root(pool, qC(l, t - 2), rows(t - 2))
                for t in (TILES - 2, TILES - 1):
                    ln_root(pool, qC(l, t), rows(t))
                barrier(pool, phase_no(l, "C"))

                def w_lo(n_wait, slot, dst):
                    pool.wait_ge(S("f_hi"), n_wait)
                    pool.tensor_tensor(fwl[dst][:, :, :], fraw[slot], f(fwh[dst][:, :, :]), ALU.subtract)\
                        .then_inc(S("f_lo"), 1)

                pool.wait_ge(S("f_lo"), W_ITEMS * l + 4)

                def turn(j, items):
                    for k, (ahead, c, which) in enumerate(items):
                        w_lo(j * 6 + (W_ITEMS * l + 4 + k + 1), (4 + k) % 3, 4 + c if which == 2 else 2 * c + which)

                with pool.Fori(0, TURNS - 1) as j:
                    turn(j, TURN_ITEMS)
                turn(TURNS - 1, LAST_ITEMS)
                barrier(pool, phase_no(l, "F"))
                for t in range(TILES):
                    ln_root(pool, qD(l, t), rows(t))
                    pool.wait_ge(S("ln_out"), qD(l, t) + 1)
                    pool.dma_start(H[l + 1, cols(t), :], yo[t % 2][0:rows(t), :]).then_inc(S(f"yo_out{t % 2}"), 16)
                for i in range(2):
                    pool.wait_ge(S(f"yo_out{i}"), 16 * ((l + 1) * TILES // 2))
                barrier(pool, phase_no(l, "D"))
            pool.wait_ge(S("cache_out"), 16 * (6 * L))

        def w_hi(act, l, item, slot, dst, total):
            act.wait_ge(S(f"fraw_in{slot}"), 16 * (total // 3 + 1))
            act.activation(fwh[dst][:, :, :], fraw[slot], ACT.Copy).then_inc(S("f_hi"), 1)

        def z_bank(i):
            return Sb[0][:, BANK * i:BANK * i + Z_BLOCKS[i][1] - Z_BLOCKS[i][0]]

        def g_bank(i):
            return Sb[0][:, 512 * i:512 * i + NT[i]]

        def u_bank(i):
            return Sb[1][:, 512 * i:512 * i + NT[i]]

        @block.scalar
        def _(act):
            split_hi(act, 0, "A")
            barrier(act, 1)
            for l in range(L):

                def x_hi(t):
                    r = rows(t)
                    act.wait_ge(S("a_xT"), A(l, t) + 1)
                    if t >= 2:
                        act.wait_ge(S("a_z"), 3 * A(l, t - 1))
                    act.activation(xTh[t % 2][:, :, 0:r],
                                   Sb[1][:, 0:1024].rearrange("p (k n) -> p k n", n=P)[:, :, 0:r], ACT.Copy)\
                       .then_inc(S("a_xh"), 1)

                def z_out(t, i):
                    r = rows(t)
                    if i == 0 and t >= 1:
                        act.wait_ge(S("a_rope"), A(l, t - 1) + 1)
                        act.wait_ge(S("kv_out"), 16 * (3 * A(l, t)))
                    act.wait_ge(S("a_z"), 3 * A(l, t) + i + 1)
                    c = slice(*Z_BLOCKS[i])
                    ins = act.activation(zs[0:r, c], z_bank(i)[0:r, :], ACT.Copy)
                    if i == 0:
                        act.activation(junkA[0:r, 0:QL], Sb[0][0:r, 0:QL], ACT.Square, scale=QL ** -0.5,
                                       accum_out=ms[t % 2][0:r, 0:1])
                        ins = act.activation(junkA[0:r, QL:QL + LAT], Sb[0][0:r, QL:QL + LAT], ACT.Square,
                                             scale=LAT ** -0.5, accum_out=ms[t % 2][0:r, 1:2])
                    ins.then_inc(S("a_zs"), 1)

                def stack_hi(t):
                    r = rows(t)
                    act.wait_ge(S("a_rope"), A(l, t) + 1)
                    if t >= 1:
                        act.wait_ge(S("a_post2"), A(l, t - 1) + 1)
                    act.activation(vh[0:r, t, :], kv1[0:r, 0:LAT], ACT.Copy)
                    kr = kv1[0:r, LAT:LAT + ROPE]
                    for i in (0, 1):
                        act.activation(krs[0:r, i, :], kr, ACT.Copy)
                    for i in range(2):
                        act.activation(kss[0:r, :, 0, i, :], zr[0:r, 8:10, :], ACT.Copy)
                    act.activation(sqs[0:r, :, 0, :], zr[0:r, 0:8, :], ACT.Copy).then_inc(S("a_stack_hi"), 1)

                def post_hi(t):
                    r = rows(t)
                    act.wait_ge(S("a_post1"), A(l, t) + 1)
                    if t >= 1:
                        act.wait_ge(S("cqT_out"), 16 * (2 * A(l, t)))
                        act.wait_ge(S("sqT_out"), 16 * (A(l, t)))
                    b5 = Sb[1][:, 1024:1536].rearrange("p (k n) -> p k n", n=P)
                    act.activation(cqTs[:, 0, :, 0:r], b5[:, 0:2, 0:r], ACT.Copy)
                    act.activation(ckvTh[:, key_cols(t)], b5[:, 2, 0:r], ACT.Copy)
                    act.activation(krT[:, key_cols(t)], b5[:, 3, 0:r], ACT.Copy).then_inc(S("a_post_hi"), 1)
                    act.activation(q_to(sqTs, t, True)[:, 0:4], q_from(Tb[1], t, True), ACT.Copy)\
                       .then_inc(S("a_sqT1"), 1)

                def post_sq(t):
                    act.wait_ge(S("a_post2"), A(l, t) + 1)
                    act.activation(q_to(sqTs, t, True)[:, 4:8], q_from(Sb[1][:, 1024:1536], t, True), ACT.Copy)\
                       .then_inc(S("a_sqT"), 1)

                x_hi(0)
                for n in range(TILES + 1):
                    if n + 1 < TILES:
                        x_hi(n + 1)
                    if n < TILES:
                        z_out(n, 0)
                        z_out(n, 1)
                    if n >= 1:
                        post_hi(n - 1)
                    if n < TILES:
                        z_out(n, 2)
                    if n >= 1:
                        post_sq(n - 1)
                    if n < TILES:
                        stack_hi(n)
                barrier(act, phase_no(l, "A"))

                split_hi(act, l, "B", slice(0, B_FIRST))

                def soft(u):
                    a = u["a"]
                    i = a % 2
                    act.wait_ge(S("bias"), AT(l, a) + 1)
                    if a >= 2:
                        act.wait_ge(S("rinv"), AT(l, a - 2) + 1)
                    if a >= 2:
                        pu = att_units[a - 2]
                        act.wait_ge(S("probsT"), G(l, pu["g0"] + len(pu["sizes"]) - 1) + 1)
                    k, sbuf = u["kind"], Sb[u["buf"]]
                    if k == "mla2":
                        n = key_count(u)
                        for h in range(2):
                            ins = act.activation(Pb[i][:, n * h:n * h + n], sbuf[:, BANK * h:BANK * h + n], ACT.Exp,
                                                 bias=nb[i][:, h:h + 1], scale=MLA_SCALE, accum_out=sm[i][:, h:h + 1])
                        ins.then_inc(S("probs"), 1)
                        return
                    if k.startswith("mla"):
                        act.activation(Pb[i][:, 0:key_count(u)], score_view(u), ACT.Exp, bias=nb[i][:, 0:1], scale=MLA_SCALE,
                                       accum_out=sm[i][:, 0:1]).then_inc(S("probs"), 1)
                        return
                    if k == "swa":
                        n = min(u["arg"], 2) * CH + CH + META
                        act.activation(ee[i][:, 0:4], es[i][:, 0:4], ACT.Exp)
                        for j in range(4):
                            ins = act.activation(Pb[i][:, 256 * j:256 * j + n], sbuf[:, 256 * j:256 * j + n], ACT.Exp,
                                                 bias=nb[i][:, j:j + 1], scale=SWA_SCALE, accum_out=sm[i][:, j:j + 1])
                    else:
                        n = WKEYS + NS if k == "swa_d" else META
                        act.activation(ee[i][:, 0:1], es[i][:, 0:1], ACT.Exp)
                        for g in range(KVH):
                            p = slice(CH * g, CH * g + CH)
                            ins = act.activation(Pb[i][p, 0:n], sbuf[p, 256 * g:256 * g + n], ACT.Exp,
                                                 bias=nb[i][p, 0:1], scale=SWA_SCALE, accum_out=sm[i][p, 0:1])
                    ins.then_inc(S("probs"), 1)

                def unit_hi(u, groups):
                    for g in groups:
                        gg = G(l, u["g0"] + g)
                        act.wait_ge(S("probsT"), gg + 1)
                        if g == 0 and u["opens"] and u["v"] >= 2:
                            act.wait_ge(S("pv"), V(l, u["v"] - 2) + 1)
                        src, dst = turned(u, g, Tb[gg % 2], PTh[u["v"] % 2][:, :])
                        act.activation(dst, src, ACT.Copy).then_inc(S("probsT_hi"), 1)

                def out_hi(u):
                    if not u["kind"].startswith("mla"):
                        return
                    act.wait_ge(S("pv"), V(l, u["v"]) + 1)
                    if u["oa"]:
                        act.wait_ge(S("oa"), QN(l, "oa", u["oa"] - 1) + 1)
                    act.activation(out_view(olh, u), o_view(u), ACT.Copy).then_inc(S("ol_hi"), 1)

                def q_unit(u):
                    k, i, t = u["kind"], QN(l, u["kind"], u["i"]), u["arg"]
                    r, s, sbuf = rows(t), u["i"] % 2, Sb[u["buf"]]
                    act.wait_ge(S(k), i + 1)
                    if k == "qa":
                        if u["i"] >= 1:
                            act.wait_ge(S("qb"), QN(l, "qb", u["i"] - 1) + 1)
                        act.activation(qnh[:, :, 0:r], sbuf[:, 0:512].rearrange("p (k n) -> p k n", n=P)[:, :, 0:r],
                                       ACT.Copy).then_inc(S("qa_hi"), 1)
                    elif k == "qb":
                        act.activation(q_to(qlh[s], t), q_from(sbuf[:, 0:1024], t), ACT.Copy).then_inc(S("qb_hi"), 1)
                    else:
                        act.activation(q_to(qrT[s], t), q_from(sbuf[:, 0:1024], t), ACT.Copy).then_inc(S("qc_out"), 1)

                def rope_hi(u):
                    r = rows(u["arg"])
                    act.wait_ge(S("qa_rope"), QN(l, "qa", u["i"]) + 1)
                    if u["i"] >= 1:
                        act.wait_ge(S("qc"), QN(l, "qc", u["i"] - 1) + 1)
                    for i in range(2):
                        ins = act.activation(qrs[0:r, :, 2 * i, :], qr_raw[0:r, :, :], ACT.Copy)
                    ins.then_inc(S("qrs_hi"), 1)

                def attend(units):
                    for n in range(len(units) + 2):
                        u = units[n] if n < len(units) else None
                        v = units[n - 1] if 1 <= n <= len(units) else None
                        w = units[n - 2] if n >= 2 else None
                        if v is not None and "a" in v:
                            unit_hi(v, range(1))
                        if u is not None:
                            if "a" in u:
                                soft(u)
                            elif u["kind"] != "oa":
                                q_unit(u)
                        if v is not None and "a" in v:
                            unit_hi(v, range(1, len(v["sizes"])))
                        if w is not None and "a" in w and w["closes"]:
                            out_hi(w)
                        if units is UB and B_FIRST + n < B_ITEMS:
                            split_hi(act, l, "B", slice(B_FIRST + n, B_FIRST + n + 1))
                        if u is not None:
                            if u["kind"] == "mla_d" and u["arg"] + 1 < NB:
                                keys_hi(u["arg"] + 1)
                            if u["kind"] == "swa_d" and u["arg"] + 1 < NB:
                                values_hi(u["arg"] + 1)
                            if u["kind"] == "qa":
                                rope_hi(u)

                def keys_hi(b):
                    s = b % 2
                    act.wait_ge(S(f"dm_in{s}"), 16 * 5 * (l * NB // 2 + b // 2 + 1))
                    if b >= 2:
                        act.wait_ge(S("pv"), V(l, dec["mla_d", b - 2]) + 1)
                    act.activation(dkh[s][:, :], dkraw[s][:, :], ACT.Copy)
                    act.activation(drs[s][:, :], drraw[s][:, :], ACT.Copy).then_inc(S("dm_hi"), 1)

                def values_hi(b):
                    s = b % 2
                    act.wait_ge(S(f"ds_in{s}"), 16 * 8 * (l * NB // 2 + b // 2 + 1))
                    if b >= 2:
                        act.wait_ge(S("pv"), V(l, dec["swa_d", b - 2]) + 1)
                    act.activation(dvh[s][:, 0:8, :], dvraw[s][:, :].rearrange("p (j n) -> p j n", n=P), ACT.Copy)
                    act.activation(dvh[s][0:32, 8, :], dtraw[s][0:32, :], ACT.Copy)
                    act.activation(dsh[s][:, :, 0, :], dsraw[s][:, :].rearrange("p (g n) -> p g n", g=KVH), ACT.Copy)
                    act.activation(duh[s][:, 0, :], duraw[s][:, 0:P], ACT.Copy)
                    act.activation(duh[s][0:32, 1, :], duraw[s][0:32, P:2 * P], ACT.Copy).then_inc(S("ds_hi"), 1)

                attend(UB)
                barrier(act, phase_no(l, "B"))
                keys_hi(0)
                values_hi(0)
                attend(UE)
                barrier(act, phase_no(l, "E"))

                def mix_sq(t):
                    r = rows(t)
                    act.wait_ge(S("mt_in"), 16 * (A(l, t) + 1))
                    for i in range(2):
                        ins = act.activation(junkC[0:r, 512 * i:512 * i + 512], mt[0:r, 512 * i:512 * i + 512], ACT.Square,
                                             scale=512 ** -0.5, accum_out=ms[t % 2][0:r, i:i + 1])
                    ins.then_inc(S("c_ms"), 1)

                def mix_hi(t):
                    r = rows(t)
                    act.wait_ge(S("c_mT"), A(l, t) + 1)
                    if t >= 2:
                        act.wait_ge(S("c_y"), A(l, t - 2) + 1)
                    act.activation(mTh[t % 2][:, :, 0:r],
                                   Sb[0][:, 0:1024].rearrange("p (k n) -> p k n", n=P)[:, :, 0:r], ACT.Copy)\
                       .then_inc(S("c_mh"), 1)

                def h1_hi(t):
                    r = rows(t)
                    act.wait_ge(S("c_hT"), A(l, t) + 1)
                    for i in range(2):
                        ins = act.activation(xh[:, 4 * i:4 * i + 4, cols(t)],
                                             Tb[i][:, :].rearrange("p (k n) -> p k n", n=P)[:, :, 0:r], ACT.Copy)
                    ins.then_inc(S("c_xh"), 1)

                mix_sq(0)
                mix_hi(0)
                mix_sq(1)
                split_hi(act, l, "C")
                for n in range(TILES + 2):
                    if n + 1 < TILES:
                        mix_hi(n + 1)
                    if n >= 2:
                        h1_hi(n - 2)
                    if n + 2 < TILES:
                        mix_sq(n + 2)
                barrier(act, phase_no(l, "C"))

                for k in range(KD):
                    if k < 4:
                        w_hi(act, l, k, k % 3, k, W_ITEMS * l + k)
                    act.activation(acc[:, k, :], f(xh[:, k, :]), ACT.Copy, scale=ALPHA).then_inc(S("f_acc0"), 1)

                def silu(j, c, first_turn):
                    for i in range(3):
                        act.wait_ge(S("f_gate"), j * 6 + (6 * TURNS * l + 3 * c + i + 1))
                        if not (first_turn and c == 0):
                            act.wait_ge(S("f_hidl"), j * 6 + (6 * TURNS * l + 3 * c - 3 + i + 1))
                        act.activation(gate[:, N0[i]:N0[i] + NT[i]], g_bank(i), ACT.Silu).then_inc(S("f_silu"), 1)

                def hid_hi(j, c):
                    for i in range(3):
                        act.wait_ge(S("f_hid"), j * 6 + (6 * TURNS * l + 3 * c + i + 1))
                        act.activation(hidh[c][:, N0[i]:N0[i] + NT[i]], gate[:, N0[i]:N0[i] + NT[i]], ACT.Copy)\
                           .then_inc(S("f_hidh"), 1)

                def weights_hi(j, items, k, first_turn):
                    _, c, which = items[k]
                    slot = (4 + k) % 3
                    item = W_ITEMS * l + 4 + k
                    act.wait_ge(S(f"fraw_in{slot}"), j * 32 + 16 * (item // 3 + 1))
                    if which < 2:
                        act.wait_ge(S("f_up" if which else "f_gate"), j * 6 + (6 * TURNS * l + 3 * c + 3))
                        act.activation(fwh[2 * c + which][:, :, :], fraw[slot], ACT.Copy).then_inc(S("f_hi"), 1)
                    else:
                        if not first_turn:
                            act.wait_ge(S("f_down"), j * 24 + 24 * TURNS * l)
                        act.activation(fwh[4 + c][:, :, :], fraw[slot], ACT.Copy).then_inc(S("f_hi"), 1)

                def turn(j, first_turn):
                    silu(j, 0, first_turn)
                    weights_hi(j, TURN_ITEMS, 0, first_turn)
                    hid_hi(j, 0)
                    for k in range(1, 4):
                        weights_hi(j, TURN_ITEMS, k, first_turn)
                    silu(j, 1, first_turn)
                    weights_hi(j, TURN_ITEMS, 4, first_turn)
                    hid_hi(j, 1)
                    weights_hi(j, TURN_ITEMS, 5, first_turn)

                turn(0, True)
                with act.Fori(1, TURNS - 1) as j:
                    turn(j, False)
                j = TURNS - 1
                silu(j, 0, False)
                hid_hi(j, 0)
                weights_hi(j, LAST_ITEMS, 0, False)
                weights_hi(j, LAST_ITEMS, 1, False)
                silu(j, 1, False)
                hid_hi(j, 1)
                barrier(act, phase_no(l, "F"))
                for t in range(TILES):
                    r = rows(t)
                    q = A(l, t)
                    act.wait_ge(S("d_T"), q + 1)
                    if t >= 2:
                        act.wait_ge(S("ln_norm"), qD(l, t - 2) + 1)
                    act.activation(xo[t % 2][0:r, :], Sb[t % 2][0:r, 0:1024], ACT.Copy).then_inc(S("d_xo"), 1)
                    if l + 1 < L:
                        split_hi(act, l + 1, "A", slice(t, t + 1))
                barrier(act, phase_no(l, "D"))

        @block.vector
        def _(dve):
            for i in range(2):
                dve.memset(Tb[i][:, :], 0.0).then_inc(S("t_zero"), 1)
            params(dve, "0")
            for t in range(TILES + 1):
                if t < TILES:
                    dve.wait_ge(S(f"x0_in{t % 2}"), 16 * (t // 2 + 1))
                    ln_stats(dve, q0(t), x0[t % 2], rows(t))
                if t >= 1:
                    if t >= 3:
                        dve.wait_ge(S(f"y0_out{(t - 1) % 2}"), 16 * ((t - 1) // 2))
                    ln_apply(dve, q0(t - 1), x0[(t - 1) % 2], y0[(t - 1) % 2], lnp, rows(t - 1))
                if t >= 1:
                    split_lo(dve, 0, "A", slice(t - 1, t))
            barrier(dve, 1)
            for l in range(L):
                params(dve, (l, "A"))

                def x_lo(t):
                    r = rows(t)
                    dve.wait_ge(S("a_xh"), A(l, t) + 1)
                    dve.tensor_tensor(xTl[t % 2][:, :, 0:r], heads(Sb[1][:, 0:1024], r), f(xTh[t % 2][:, :, 0:r]),
                                      ALU.subtract).then_inc(S("a_xl"), 1)

                def rotate(out, x, ta, tb, cs, sn, r, n, half_n, sems, items):
                    w = 2 * half_n
                    c = cs.rearrange("p (a w) -> p a w", a=1).to_broadcast([r, n, w])
                    s1 = sn[:, 0:half_n].rearrange("p (a w) -> p a w", a=1).to_broadcast([r, n, half_n])
                    s2 = sn[:, half_n:w].rearrange("p (a w) -> p a w", a=1).to_broadcast([r, n, half_n])
                    dve.tensor_tensor(ta, x, c, ALU.mult)
                    dve.tensor_tensor(tb[:, :, 0:half_n], x[:, :, half_n:w], s1, ALU.mult)
                    dve.tensor_tensor(tb[:, :, half_n:w], x[:, :, 0:half_n], s2, ALU.mult).then_inc(S(sems[0]), 1)
                    dve.wait_ge(S(sems[0]), items + 1)
                    dve.tensor_tensor(out, ta, tb, ALU.add).then_inc(S(sems[1]), 1)

                def norm_rope(t):
                    r, q = rows(t), A(l, t)
                    dve.wait_ge(S("a_zs"), 3 * q + 1)
                    if t >= 2:
                        dve.wait_ge(S("a_root"), q - 1)
                    dve.tensor_scalar(mse[t % 2][0:r, :], ms[t % 2][0:r, :], RMS_EPS, None, ALU.add)\
                       .then_inc(S("a_mse"), 1)
                    if t >= 1:
                        dve.wait_ge(S("kv_out"), 16 * (3 * q))
                        dve.wait_ge(S("a_stack_hi"), q)
                        dve.wait_ge(S("a_stack_lo"), q)
                        dve.wait_ge(S("a_post1"), q)
                    dve.wait_ge(S(f"rot_in{t % 2}"), 16 * (5 * l + t // 2 + 1))
                    dve.wait_ge(S("a_zs"), 3 * q + 3)
                    ro = rot[t % 2]
                    z10 = zs[0:r, SQ0:SV0].rearrange("p (h d) -> p h d", d=HD)
                    rotate(zr[0:r, :, :], z10, rta[0:r, :, :], rtb[0:r, :, :], ro[0:r, 0:64], ro[0:r, 64:128],
                           r, 10, HD // 2, ("a_rot1", "a_rot2"), q)
                    k1 = zs[0:r, KR0:SQ0].rearrange("p (h d) -> p h d", h=1)
                    dve.wait_ge(S("a_rot2"), q + 1)
                    rotate(kv1[0:r, LAT:LAT + ROPE].rearrange("p (h d) -> p h d", h=1), k1,
                           rta[0:r, 0:1, 0:ROPE], rtb[0:r, 0:1, 0:ROPE], ro[0:r, 128:160], ro[0:r, 160:192],
                           r, 1, ROPE // 2, ("a_rot3", "a_rot4"), q)
                    dve.wait_ge(S("a_root"), q + 1)
                    dve.scalar_tensor_tensor(out=cqn[0:r, :], in0=zs[0:r, 0:QL], scalar=mrs[t % 2][0:r, 0:1],
                                             in1=qkvg[0:r, 0:QL], op0=ALU.mult, op1=ALU.mult)
                    dve.scalar_tensor_tensor(out=kv1[0:r, 0:LAT], in0=zs[0:r, QL:KR0], scalar=mrs[t % 2][0:r, 1:2],
                                             in1=qkvg[0:r, QL:QL + LAT], op0=ALU.mult, op1=ALU.mult)\
                       .then_inc(S("a_rope"), 1)

                def stack_lo(t):
                    r = rows(t)
                    dve.wait_ge(S("a_stack_hi"), A(l, t) + 1)
                    dve.tensor_tensor(vl[0:r, t, :], kv1[0:r, 0:LAT], f(vh[0:r, t, :]), ALU.subtract)
                    for i in (2, 3):
                        dve.tensor_tensor(krs[0:r, i, :], kv1[0:r, LAT:LAT + ROPE], f(krs[0:r, 0, :]), ALU.subtract)
                    for i in range(2):
                        dve.tensor_tensor(kss[0:r, :, 1, i, :], zr[0:r, 8:10, :], f(kss[0:r, :, 0, 0, :]), ALU.subtract)
                    dve.tensor_tensor(sqs[0:r, :, 1, :], zr[0:r, 0:8, :], f(sqs[0:r, :, 0, :]), ALU.subtract)\
                       .then_inc(S("a_stack_lo"), 1)

                def post_lo(t):
                    r = rows(t)
                    dve.wait_ge(S("a_post_hi"), A(l, t) + 1)
                    b5 = Sb[1][:, 1024:1536].rearrange("p (k n) -> p k n", n=P)
                    dve.tensor_tensor(cqTs[:, 1, :, 0:r], b5[:, 0:2, 0:r], f(cqTs[:, 0, :, 0:r]), ALU.subtract)
                    dve.tensor_tensor(ckvTl[:, key_cols(t)], b5[:, 2, 0:r], f(ckvTh[:, key_cols(t)]), ALU.subtract)
                    dve.tensor_copy(skT[:, :, :, cols(t)].rearrange("p g a n -> p (g a) n"), heads(Tb[0][:, :], r))\
                       .then_inc(S("a_post_lo"), 1)

                x_lo(0)
                for n in range(TILES + 1):
                    if n + 1 < TILES:
                        x_lo(n + 1)
                    if n >= 1:
                        post_lo(n - 1)
                    if n < TILES:
                        norm_rope(n)
                        stack_lo(n)
                barrier(dve, phase_no(l, "A"))

                split_lo(dve, l, "B", slice(0, B_FIRST))
                params(dve, (l, "B"))
                dve.tensor_scalar(nsink[:, :], sinkT[:, :], -1.0, None, ALU.mult)
                dve.memset(f(maskq[:, :]), 0.0)
                dve.memset(f(maskk[:, :]), MASKED).then_inc(S("mask_zero"), 1)
                dve.wait_ge(S("mask_zero"), l + 1)
                dve.memset(f(maskq[0:1, 0:CH]), 1.0).then_inc(S("mask"), 1)

                def bias(u):
                    a = u["a"]
                    i, q = a % 2, AT(l, a)
                    dve.wait_ge(S("s_done"), q + 1)
                    if a >= 2:
                        dve.wait_ge(S("probs"), q - 1)
                    k, sbuf = u["kind"], Sb[u["buf"]]
                    if k == "mla2":
                        dve.tensor_reduce(mx[i][:, 0:2],
                                          sbuf[:, 0:2 * BANK].rearrange("p (h n) -> p h n", n=BANK)[:, :, 0:key_count(u)],
                                          AX.X, ALU.max, negate=True).then_inc(S("mx"), 1)
                        dve.wait_ge(S("mx"), q + 1)
                        dve.tensor_scalar(nb[i][:, 0:2], mx[i][:, 0:2], MLA_SCALE, None, ALU.mult)\
                           .then_inc(S("bias"), 1)
                        return
                    if k.startswith("mla"):
                        dve.tensor_reduce(mx[i][:, 0:1], score_view(u), AX.X, ALU.max, negate=True).then_inc(S("mx"), 1)
                        dve.wait_ge(S("mx"), q + 1)
                        dve.tensor_scalar(nb[i][:, 0:1], mx[i][:, 0:1], MLA_SCALE, None, ALU.mult)\
                           .then_inc(S("bias"), 1)
                        return
                    if k == "swa":
                        n, js, sk = min(u["arg"], 2) * CH + CH + META, 4, slice(0, 4)
                        dve.tensor_reduce(mx[i][:, 0:4], sbuf[:, 0:1024].rearrange("p (j n) -> p j n", n=256)[:, :, 0:n],
                                          AX.X, ALU.max, negate=True).then_inc(S("mx"), 1)
                    else:
                        n, js, sk = (WKEYS + NS if k == "swa_d" else META), 1, slice(4, 5)
                        for g in range(KVH):
                            p = slice(CH * g, CH * g + CH)
                            ins = dve.tensor_reduce(mx[i][p, 0:1], sbuf[p, 256 * g:256 * g + n], AX.X, ALU.max,
                                                    negate=True)
                        ins.then_inc(S("mx"), 1)
                    dve.wait_ge(S("mx"), q + 1)
                    dve.scalar_tensor_tensor(out=nb[i][:, 0:js], in0=mx[i][:, 0:js], scalar=SWA_SCALE,
                                             in1=nsink[:, sk], op0=ALU.mult, op1=ALU.min).then_inc(S("nbs"), 1)
                    dve.wait_ge(S("nbs"), l * N_SWA + u["w"] + 1)
                    dve.tensor_tensor(es[i][:, 0:js], nb[i][:, 0:js], sinkT[:, sk], ALU.add).then_inc(S("bias"), 1)

                def inverse(u):
                    a = u["a"]
                    i, q = a % 2, AT(l, a)
                    dve.wait_ge(S("probs"), q + 1)
                    k = u["kind"]
                    if k in ("mla", "mla2"):
                        if u["oa"] >= 2:
                            dve.wait_ge(S("oa_out"), QN(l, "oa", u["oa"] - 2) + 1)
                        n = 2 if k == "mla2" else 1
                        h = head_at(u["h"])
                        dve.reciprocal(ri[u["oa"] % 2][:, h:h + 2 * n - 1:2], sm[i][:, 0:n]).then_inc(S("rinv"), 1)
                        return
                    if k.startswith("mla"):
                        n = META if k == "mla_m" else CKEYS + NS
                        dve.reciprocal(rin[u["a"] % 4][:, 0:1], sm[i][:, 0:1]).then_inc(S("rinv"), 1)
                        dve.wait_ge(S("rinv"), q + 1)
                        dve.tensor_scalar(Pb[i][:, 0:n], Pb[i][:, 0:n], rin[u["a"] % 4][:, 0:1], None, ALU.mult)\
                           .then_inc(S("pnorm"), 1)
                        return
                    js = 4 if k == "swa" else 1
                    dve.tensor_tensor(den[i][:, 0:js], sm[i][:, 0:js], ee[i][:, 0:js], ALU.add).then_inc(S("den"), 1)
                    dve.wait_ge(S("den"), l * N_SWA + u["w"] + 1)
                    dve.reciprocal(rin[u["a"] % 4][:, 0:js], den[i][:, 0:js]).then_inc(S("rinv"), 1)

                def unit_lo(u):
                    for g in range(len(u["sizes"])):
                        gg = G(l, u["g0"] + g)
                        dve.wait_ge(S("probsT_hi"), gg + 1)
                        src, hi = turned(u, g, Tb[gg % 2], f(PTh[u["v"] % 2][:, :]))
                        _, lo = turned(u, g, Tb[gg % 2], PTl[u["v"] % 2][:, :])
                        dve.tensor_tensor(lo, src, hi, ALU.subtract).then_inc(S("probsT_lo"), 1)

                def out_lo(u):
                    q = AT(l, u["a"])
                    if u["kind"].startswith("mla"):
                        dve.wait_ge(S("ol_hi"), mla_ord(l, u) + 1)
                        dve.tensor_tensor(out_view(oll, u), o_view(u), f(out_view(olh, u)), ALU.subtract)\
                           .then_inc(S("out_read"), 1)
                        return
                    dve.wait_ge(S("pv"), V(l, u["v"]) + 1)
                    if per_slot[u["w"] % 2] * l + u["before_dmas"] > 0:
                        dve.wait_ge(S(f"mixs_out{u['w'] % 2}"), 16 * (per_slot[u["w"] % 2] * l + u["before_dmas"]))
                    dve.wait_ge(S("rinv"), q + 1)
                    dst = mixs[u["w"] % 2]
                    if u["kind"] == "swa":
                        dve.tensor_tensor(dst[:, :, :], OB[:, 0:4 * HD].rearrange("p (j d) -> p j d", d=HD),
                                          rin[u["a"] % 4][:, 0:4].rearrange("p (j d) -> p j d", d=1).to_broadcast([P, 4, HD]),
                                          ALU.mult).then_inc(S("out_read"), 1)
                        return
                    for g in range(KVH):
                        p = slice(CH * g, CH * g + CH)
                        ins = dve.tensor_scalar(dst[p, 0, :], OB[p, HD * g:HD * g + HD], rin[u["a"] % 4][p, 0:1],
                                                None, ALU.mult)
                    ins.then_inc(S("out_read"), 1)

                def q_unit(u):
                    k, q, t = u["kind"], QN(l, u["kind"], u["i"]), u["arg"]
                    r, s, sbuf = rows(t), u["i"] % 2, Sb[u["buf"]]
                    if k == "qa":
                        dve.wait_ge(S("qa_hi"), q + 1)
                        if u["i"] >= 1:
                            dve.wait_ge(S("qb"), q)
                        dve.tensor_tensor(qnl[:, :, 0:r], heads(sbuf[:, 0:512], r), f(qnh[:, :, 0:r]), ALU.subtract)\
                           .then_inc(S("qa_lo"), 1)
                        dve.wait_ge(S(f"q_in{s}"), 16 * (3 * (l * N_Q["qa"] // 2 + u["i"] // 2 + 1)))
                        if u["i"] >= 1:
                            dve.wait_ge(S("qrs_hi"), q)
                            dve.wait_ge(S("qrs_lo"), q)
                        x = sbuf[0:r, 512:768].rearrange("p (h d) -> p h d", d=ROPE)
                        ro = rotB[s]
                        rotate(qr_raw[0:r, :, :], x, qra[0:r, :, :], qrb[0:r, :, :], ro[0:r, 128:160],
                               ro[0:r, 160:192], r, HEADS, ROPE // 2, ("qa_rot", "qa_rope"), q)
                    elif k == "qb":
                        dve.wait_ge(S("qb_hi"), q + 1)
                        dve.tensor_tensor(q_to(qll[s], t), q_from(sbuf[:, 0:1024], t), q_to(f(qlh[s][:, :]), t),
                                          ALU.subtract).then_inc(S("qb_lo"), 1)
                    elif k == "oa":
                        dve.wait_ge(S("oa"), q + 1)
                        if q >= 1:
                            dve.wait_ge(S("mixo_out"), 16 * q)
                        if t < 8:
                            dve.tensor_tensor(mixo[:, :].rearrange("p (h d) -> p h d", d=HD),
                                              sbuf[:, 0:512].rearrange("p (h d) -> p h d", d=HD),
                                              ri[u["i"] % 2][:, :].rearrange("p (h d) -> p h d", d=1)
                                              .to_broadcast([P, HEADS, HD]), ALU.mult).then_inc(S("oa_out"), 1)
                        else:
                            dve.tensor_copy(mixo[0:r, :], sbuf[0:r, 0:512]).then_inc(S("oa_out"), 1)

                def rope_lo(u):
                    r, q = rows(u["arg"]), QN(l, "qa", u["i"])
                    dve.wait_ge(S("qrs_hi"), q + 1)
                    for i in range(2):
                        ins = dve.tensor_tensor(qrs[0:r, :, 2 * i + 1, :], qr_raw[0:r, :, :], f(qrs[0:r, :, 0, :]),
                                                ALU.subtract)
                    ins.then_inc(S("qrs_lo"), 1)

                def attend(units):
                    for n in range(len(units) + 2):
                        u = units[n] if n < len(units) else None
                        v = units[n - 1] if 1 <= n <= len(units) else None
                        w = units[n - 2] if n >= 2 else None
                        if u is not None:
                            if "a" in u:
                                bias(u)
                            elif u["kind"] != "oa":
                                q_unit(u)
                        if v is not None and "a" in v:
                            unit_lo(v)
                        if u is not None and u["kind"] == "mla_d":
                            inverse(u)
                        if w is not None and "a" in w and w["closes"]:
                            out_lo(w)
                        if units is UB and B_FIRST + n < B_ITEMS:
                            split_lo(dve, l, "B", slice(B_FIRST + n, B_FIRST + n + 1))
                        if u is not None:
                            if "a" in u and u["kind"] != "mla_d":
                                inverse(u)
                            if u["kind"] == "mla_d" and u["arg"] + 1 < NB:
                                keys_lo(u["arg"] + 1)
                            if u["kind"] == "swa_d" and u["arg"] + 1 < NB:
                                values_lo(u["arg"] + 1)
                            if u["kind"] == "qa":
                                rope_lo(u)
                            if u["kind"] == "oa":
                                q_unit(u)

                def keys_lo(b):
                    s = b % 2
                    dve.wait_ge(S("dm_hi"), l * NB + b + 1)
                    dve.tensor_tensor(dkl[s][:, :], dkraw[s][:, :], f(dkh[s][:, :]), ALU.subtract)
                    p = slice(2 * ROPE, 4 * ROPE)
                    dve.tensor_tensor(drs[s][p, :], drraw[s][p, :], f(drs[s][p, :]), ALU.subtract)\
                       .then_inc(S("dm_lo"), 1)

                def values_lo(b):
                    s = b % 2
                    dve.wait_ge(S("ds_hi"), l * NB + b + 1)
                    dve.tensor_tensor(dvl[s][:, 0:8, :], dvraw[s][:, :].rearrange("p (j n) -> p j n", n=P),
                                      f(dvh[s][:, 0:8, :]), ALU.subtract)
                    dve.tensor_tensor(dvl[s][0:32, 8, :], dtraw[s][0:32, :], f(dvh[s][0:32, 8, :]), ALU.subtract)
                    dve.tensor_tensor(dsh[s][:, :, 1, :], dsraw[s][:, :].rearrange("p (g n) -> p g n", g=KVH),
                                      f(dsh[s][:, :, 0, :]), ALU.subtract)
                    dve.tensor_tensor(dul[s][:, 0, :], duraw[s][:, 0:P], f(duh[s][:, 0, :]), ALU.subtract)
                    dve.tensor_tensor(dul[s][0:32, 1, :], duraw[s][0:32, P:2 * P], f(duh[s][0:32, 1, :]), ALU.subtract)\
                       .then_inc(S("ds_lo"), 1)

                attend(UB)
                barrier(dve, phase_no(l, "B"))
                keys_lo(0)
                values_lo(0)
                attend(UE)
                barrier(dve, phase_no(l, "E"))

                params(dve, (l, "C"))

                def mix_norm(t):
                    r, q = rows(t), A(l, t)
                    dve.wait_ge(S("c_ms"), q + 1)
                    if t >= 2:
                        dve.wait_ge(S("c_root"), q - 1)
                    dve.tensor_scalar(mse[t % 2][0:r, :], ms[t % 2][0:r, :], RMS_EPS, None, ALU.add)\
                       .then_inc(S("c_mse"), 1)
                    dve.wait_ge(S("c_root"), q + 1)
                    if t >= 1:
                        dve.wait_ge(S("c_mT"), q)
                    for i in range(2):
                        ins = dve.scalar_tensor_tensor(out=mn[0:r, 512 * i:512 * i + 512],
                                                       in0=mt[0:r, 512 * i:512 * i + 512],
                                                       scalar=mrs[t % 2][0:r, i:i + 1],
                                                       in1=mixg[0:r, 512 * i:512 * i + 512],
                                                       op0=ALU.mult, op1=ALU.mult)
                    ins.then_inc(S("c_mixn"), 1)

                def mix_lo(t):
                    r = rows(t)
                    dve.wait_ge(S("c_mh"), A(l, t) + 1)
                    dve.tensor_tensor(mTl[t % 2][:, :, 0:r], heads(Sb[0][:, 0:1024], r), f(mTh[t % 2][:, :, 0:r]),
                                      ALU.subtract).then_inc(S("c_ml"), 1)

                def residual(t):
                    r, q = rows(t), A(l, t)
                    dve.wait_ge(S("c_y"), q + 1)
                    dve.wait_ge(S("hc_in"), 16 * (q + 1))
                    dve.scalar_tensor_tensor(out=x1[0:r, :], in0=hc[0:r, :], scalar=ALPHA, in1=YB[t % 2][0:r, :],
                                             op0=ALU.mult, op1=ALU.add).then_inc(S("c_res"), 1)
                    dve.wait_ge(S("c_res"), q + 1)
                    ln_stats(dve, qC(l, t), x1, r)
                    if t >= 1:
                        dve.wait_ge(S("c_hT"), q)
                    ln_apply(dve, qC(l, t), x1, h1, ln1, r)

                def h1_lo(t):
                    r = rows(t)
                    dve.wait_ge(S("c_xh"), A(l, t) + 1)
                    for i in range(2):
                        ins = dve.tensor_tensor(xl[:, 4 * i:4 * i + 4, cols(t)], heads(Tb[i][:, :], r),
                                                f(xh[:, 4 * i:4 * i + 4, cols(t)]), ALU.subtract)
                    ins.then_inc(S("c_xl"), 1)

                mix_norm(0)
                mix_lo(0)
                split_lo(dve, l, "C")
                mix_norm(1)
                for n in range(TILES + 2):
                    if n + 1 < TILES:
                        mix_lo(n + 1)
                    if n >= 2:
                        h1_lo(n - 2)
                    if 1 <= n <= TILES:
                        residual(n - 1)
                    if n + 2 < TILES:
                        mix_norm(n + 2)
                barrier(dve, phase_no(l, "C"))

                for k in range(KD):
                    if k < 4:
                        dve.wait_ge(S("f_hi"), W_ITEMS * l + k + 1)
                        dve.tensor_tensor(fwl[k][:, :, :], fraw[k % 3], f(fwh[k][:, :, :]), ALU.subtract)\
                            .then_inc(S("f_lo"), 1)
                    dve.wait_ge(S("f_acc0"), KD * l + k + 1)
                    dve.scalar_tensor_tensor(out=acc[:, k, :], in0=f(xl[:, k, :]), scalar=ALPHA, in1=acc[:, k, :],
                                             op0=ALU.mult, op1=ALU.add).then_inc(S("f_acc"), 1)

                def hidden(j, c):
                    for i in range(3):
                        g = gate[:, N0[i]:N0[i] + NT[i]]
                        dve.wait_ge(S("f_silu"), j * 6 + (6 * TURNS * l + 3 * c + i + 1))
                        dve.wait_ge(S("f_up"), j * 6 + (6 * TURNS * l + 3 * c + i + 1))
                        dve.tensor_tensor(g, u_bank(i), g, ALU.mult).then_inc(S("f_hid"), 1)
                    for i in range(3):
                        g = gate[:, N0[i]:N0[i] + NT[i]]
                        dve.wait_ge(S("f_hidh"), j * 6 + (6 * TURNS * l + 3 * c + i + 1))
                        dve.tensor_tensor(hidl[c][:, N0[i]:N0[i] + NT[i]], g, f(hidh[c][:, N0[i]:N0[i] + NT[i]]),
                                          ALU.subtract).then_inc(S("f_hidl"), 1)

                def add_down(j):
                    for e in range(24):
                        k, i = e // 3, e % 3
                        a = acc[:, k, N0[i]:N0[i] + NT[i]]
                        dve.wait_ge(S("f_down"), j * 24 + (24 * TURNS * l + e + 1))
                        dve.tensor_tensor(a, a, Tb[e % 2][:, 0:NT[i]], ALU.add).then_inc(S("f_y"), 1)

                dve.wait_ge(S("f_acc"), KD * l + KD)
                hidden(0, 0)
                hidden(0, 1)
                with dve.Fori(1, TURNS) as j:
                    add_down(j - 1)
                    hidden(j, 0)
                    hidden(j, 1)
                add_down(TURNS - 1)
                barrier(dve, phase_no(l, "F"))

                params(dve, (l, "D"))
                for t in range(TILES + 1):
                    if t < TILES:
                        dve.wait_ge(S("d_xo"), A(l, t) + 1)
                        ln_stats(dve, qD(l, t), xo[t % 2], rows(t))
                    if t >= 1:
                        v = t - 1
                        if 5 * l + v // 2 >= 1:
                            dve.wait_ge(S(f"yo_out{v % 2}"), 16 * (5 * l + v // 2))
                        ln_apply(dve, qD(l, v), xo[v % 2], yo[v % 2], lnd, rows(v))
                        if l + 1 < L:
                            split_lo(dve, l + 1, "A", slice(v, v + 1))
                barrier(dve, phase_no(l, "D"))

        @block.tensor
        def _(pe):
            def three(out, wh, wl, mh, ml, start, stop):
                pe.matmul(out, wh, mh, start=start, stop=False)
                pe.matmul(out, wh, ml, start=False, stop=False)
                return pe.matmul(out, wl, mh, start=False, stop=stop)

            pe.wait_ge(S("ident"), 1)
            pe.wait_ge(S("t_zero"), 2)
            barrier(pe, 1)
            for l in range(L):
                def x_T(t):
                    r = rows(t)
                    pe.wait_ge(S(f"ht_in{t % 2}"), 16 * (5 * l + t // 2 + 1))
                    if t >= 1:
                        pe.wait_ge(S("a_xl"), A(l, t - 1) + 1)
                    for k in range(KD):
                        ins = pe.transpose(Sb[1][:, k * P:k * P + r], ht[t % 2][0:r, k * P:k * P + P], ident[0:r, 0:r])
                    ins.then_inc(S("a_xT"), 1)

                def z(t, i):
                    r = rows(t)
                    if i == 0:
                        pe.wait_ge(S("a_xl"), A(l, t) + 1)
                    if t >= 1:
                        pe.wait_ge(S("a_zs"), 3 * A(l, t - 1) + i + 1)
                    c0, c1 = Z_BLOCKS[i]
                    for k in range(KD):
                        ins = three(z_bank(i)[0:r, :], xTh[t % 2][:, k, 0:r], xTl[t % 2][:, k, 0:r],
                                    winh[:, k, c0:c1], winl[:, k, c0:c1], k == 0, k == KD - 1)
                    ins.then_inc(S("a_z"), 1)

                def post(t):
                    r = rows(t)
                    i = ident[0:r, 0:r]
                    pe.wait_ge(S("a_rope"), A(l, t) + 1)
                    pe.wait_ge(S("a_stack_lo"), A(l, t) + 1)
                    if t >= 1:
                        pe.wait_ge(S("a_post_lo"), A(l, t - 1) + 1)
                        pe.wait_ge(S("a_sqT"), A(l, t - 1) + 1)
                    for k in range(2):
                        pe.transpose(Sb[1][:, 1024 + k * P:1024 + k * P + r], cqn[0:r, k * P:k * P + P], i)
                    pe.transpose(Sb[1][:, 1280:1280 + r], kv1[0:r, 0:LAT], i)
                    pe.transpose(Sb[1][:, 1408:1408 + r], f(krs[0:r, :, :]).rearrange("p a d -> p (a d)"), i)
                    for k in range(4):
                        pe.transpose(Tb[0][:, k * P:k * P + r],
                                     f(kss[0:r, k // 2, k % 2, :, :]).rearrange("p a d -> p (a d)"), i)
                    for k in range(4):
                        ins = pe.transpose(Tb[1][:, k * P:k * P + r],
                                           f(sqs[0:r, k, :, :]).rearrange("p a d -> p (a d)"), i)
                    ins.then_inc(S("a_post1"), 1)

                def post_queries(t):
                    r = rows(t)
                    pe.wait_ge(S("a_post_lo"), A(l, t) + 1)
                    for k in range(4):
                        ins = pe.transpose(Sb[1][:, 1024 + k * P:1024 + k * P + r],
                                           f(sqs[0:r, 4 + k, :, :]).rearrange("p a d -> p (a d)"), ident[0:r, 0:r])
                    ins.then_inc(S("a_post2"), 1)

                x_T(0)
                all_split(pe, l, "A")
                for n in range(TILES + 1):
                    if n + 1 < TILES:
                        x_T(n + 1)
                    if n < TILES:
                        z(n, 0)
                        z(n, 1)
                    if n >= 1:
                        post(n - 1)
                    if n < TILES:
                        z(n, 2)
                    if n >= 1:
                        post_queries(n - 1)
                barrier(pe, phase_no(l, "A"))

                pe.wait_ge(S("split_lo"), first[l, "B"] + B_FIRST)
                pe.wait_ge(S("mask"), l + 1)

                def scores(u):
                    k, n, t = u["kind"], u["n"], u["arg"]
                    sbuf = Sb[u["buf"]]
                    free_scores(pe, l, u)
                    if k in ("qa", "qb", "qc", "oa"):
                        q_scores(u, sbuf)
                        return
                    tt = t if k in ("mla", "mla2") else (9 if k.endswith("_m") else (8 if k.endswith("_d") else t // 2))
                    i = q_index[tt]
                    s = i % 2
                    if k.startswith("mla"):
                        pe.wait_ge(S("qb_lo"), QN(l, "qb", i) + 1)
                        pe.wait_ge(S("qc_out"), QN(l, "qc", i) + 1)
                        if k in ("mla", "mla2"):
                            at = P * u["h"]
                        else:
                            at = 0 if k == "mla_m" else P * t
                        a, b, c = (x[s][:, at:at + P] for x in (qlh, qll, qrT))

                        def keys(out, kh, kl, kr, more=False):
                            pe.matmul(out, a, kh, start=True, stop=False)
                            pe.matmul(out, a, kl, start=False, stop=False)
                            pe.matmul(out, b, kh, start=False, stop=False)
                            return pe.matmul(out, c, kr, start=False, stop=not more)

                        if k == "mla2":
                            n = key_count(u)
                            for h in range(2):
                                out = sbuf[:, BANK * h:BANK * (h + 1)]
                                a, b, c = (x[s][:, at + P * h:at + P * h + P] for x in (qlh, qll, qrT))
                                keys(out[:, 0:n], ckvTh[:, 0:n], ckvTl[:, 0:n], krT[:, 0:n], more=True)
                                ins = pe.matmul(out[:, n - CH:n], maskq[:, :], maskk[:, :], start=False, stop=True)
                            ins.then_inc(S("s_done"), 1)
                            return
                        if k == "mla":
                            n, out = key_count(u), score_view(u)
                            cuts = [0] + [c for c in ((u["tail"], u["tail"] + BANK) if u["buf"] else (BANK, 2 * BANK))
                                          if 0 < c < n] + [n]
                            spans = list(zip(cuts, cuts[1:]))
                            if u["tail"] and u["buf"]:
                                spans = spans[1:] + spans[:1]
                            for c0, c1 in spans:
                                if u["tail"] and (c0, c1) == spans[-1] and u["tail_before"] is not None:
                                    pe.wait_ge(S("probs"), AT(l, u["tail_before"]["a"]) + 1)
                                m0 = max(c0, n - CH)
                                ins = keys(out[:, c0:c1], ckvTh[:, c0:c1], ckvTl[:, c0:c1], krT[:, c0:c1], more=m0 < c1)
                                if m0 < c1:
                                    ins = pe.matmul(out[:, m0:c1], maskq[:, :], maskk[:, 0:c1 - m0], start=False,
                                                    stop=True)
                            ins.then_inc(S("s_done"), 1)
                            return
                        if k == "mla_d":
                            pe.wait_ge(S("dm_lo"), l * NB + t + 1)
                            for c0, c1 in ((0, 512), (512, 1024), (1024, CKEYS)):
                                if c0 == 1024 and u["tail_before"] is not None:
                                    pe.wait_ge(S("probs"), AT(l, u["tail_before"]["a"]) + 1)
                                keys(sbuf[:, c0:c1] if c0 < 1024 else tail_view(u)[:, 0:META],
                                     dkh[t % 2][:, c0:c1], dkl[t % 2][:, c0:c1], drs[t % 2][:, c0:c1])
                            last = tail_view(u)[:, META:META + NS]
                        else:
                            last = sbuf[:, 0:META]
                        o = META + SEQ + NS * t if k == "mla_d" else 0
                        ins = keys(last, ckvTh[:, o:o + NS], ckvTl[:, o:o + NS], krT[:, o:o + NS])
                    elif k == "swa":
                        pe.wait_ge(S(f"sq_in{s}"), 16 * (l * N_Q["qa"] // 2 + i // 2 + 1))
                        q0_ = SWA_H * CH * (t % 2)
                        k0, k1 = CH * max(t - 2, 0), CH * (t + 1)
                        for j in range(4):
                            q = sqT[s][:, q0_ + P * j:q0_ + P * j + P]
                            c0 = 256 * j
                            for (s0, s1), at in (((k0, k1), c0), ((METAROW, TOK), c0 + k1 - k0)):
                                for a in range(2):
                                    ins = pe.matmul(sbuf[:, at:at + s1 - s0], q, skT[:, j // 2, a, s0:s1],
                                                    start=a == 0, stop=a == 1)
                    else:
                        pe.wait_ge(S(f"sq_in{s}"), 16 * (l * N_Q["qa"] // 2 + i // 2 + 1))
                        at = 0 if k == "swa_m" else P * t
                        q = sqT[s][:, at:at + P]
                        if k == "swa_d":
                            pe.wait_ge(S("ds_lo"), l * NB + t + 1)
                        for g in range(KVH):
                            c0, o = 256 * g, METAROW
                            if k == "swa_d":
                                for a in range(2):
                                    pe.matmul(sbuf[:, c0:c0 + WKEYS], q, dsh[t % 2][:, g, a, :], start=a == 0, stop=a == 1)
                                c0, o = c0 + WKEYS, SAMPLE + NS * t
                            for a in range(2):
                                ins = pe.matmul(sbuf[:, c0:c0 + NS], q, skT[:, g, a, o:o + NS],
                                                start=a == 0, stop=a == 1)
                    ins.then_inc(S("s_done"), 1)

                def q_scores(u, sbuf):
                    k, t, i = u["kind"], u["arg"], u["i"]
                    r, s, q = rows(t), i % 2, QN(l, k, i)
                    if k == "qa":
                        pe.wait_ge(S(f"q_in{s}"), 16 * (3 * (l * N_Q["qa"] // 2 + i // 2 + 1)))
                        for m in range(4):
                            for kk in range(2):
                                three(sbuf[:, m * P:m * P + r], wuqh[:, kk, m * P:m * P + P], wuql[:, kk, m * P:m * P + P],
                                      cq[s][:, 0, kk, 0:r], cq[s][:, 1, kk, 0:r], kk == 0, kk == 1)
                        for kk in range(2):
                            ins = three(sbuf[0:r, 512:768], cq[s][:, 0, kk, 0:r], cq[s][:, 1, kk, 0:r],
                                        wuqh[:, kk, 512:768], wuql[:, kk, 512:768], kk == 0, kk == 1)
                    elif k == "qb":
                        pe.wait_ge(S("qa_lo"), q + 1)
                        for h in range(HEADS):
                            p = slice(64 * (h % 2), 64 * (h % 2) + 64)
                            c0 = P * place_of(h)
                            ins = three(sbuf[:, c0:c0 + r], wukh[p, h // 2, :], wukl[p, h // 2, :],
                                        qnh[p, h // 2, 0:r], qnl[p, h // 2, 0:r], True, True)
                    elif k == "qc":
                        pe.wait_ge(S("qrs_lo"), q + 1)
                        for h in range(HEADS):
                            c0 = P * place_of(h)
                            ins = pe.transpose(sbuf[:, c0:c0 + r],
                                               f(qrs[0:r, h, :, :]).rearrange("p a d -> p (a d)"), ident[0:r, 0:r])
                    else:
                        last = u["last_mla"]
                        pe.wait_ge(S("split_lo"), first[l, "B"] + 6)
                        pe.wait_ge(S("out_read"), V(l, last) + 1)
                        for h in range(HEADS):
                            ins = three(sbuf[0:r, h * HD:h * HD + HD], olh[:, place_of(h), 0:r], oll[:, place_of(h), 0:r],
                                        wuvh[:, h * HD:h * HD + HD], wuvl[:, h * HD:h * HD + HD], True, True)
                    ins.then_inc(S(k), 1)

                def blocks_of(u):
                    k, t = u["kind"], u["arg"]
                    if k == "mla2":
                        n = key_count(u)
                        return [(n * h, META) for h in range(2)] + \
                            [(n * h + META + P * j, P) for j in range(t + 1) for h in range(2)]
                    if k == "mla":
                        return [(0, META)] + [(META + P * j, P) for j in range(t + 1)]
                    if k == "mla_d":
                        at = u["tail"] * u["buf"]
                        return [(at + P * j, P) for j in range(8)] + [(0 if at else PAST, META + NS)]
                    if k == "swa":
                        w = min(t, 2) * CH
                        return [(256 * j, w) for j in range(4 if w else 0)] + \
                            [(256 * j + w, CH + META) for j in range(4)]
                    if k == "swa_d":
                        return [(0, P), (P, META + NS)]
                    return [(0, META)]

                def turn_probs(u, groups):
                    for g in groups:
                        if g == 0:
                            if u["kind"] in ("mla_m", "mla_d"):
                                pe.wait_ge(S("pnorm"), norm_ord(l, u) + 1)
                            else:
                                pe.wait_ge(S("probs"), AT(l, u["a"]) + 1)
                        gg = G(l, u["g0"] + g)
                        if gg >= 2:
                            pe.wait_ge(S("probsT_lo"), gg - 1)
                        for b in range(u["sizes"][g]):
                            c0, w = blocks_of(u)[sum(u["sizes"][:g]) + b]
                            ins = pe.transpose(Tb[gg % 2][0:w, b * P:b * P + P], Pb[u["a"] % 2][:, c0:c0 + w],
                                               ident[:, :])
                        ins.then_inc(S("probsT"), 1)

                def values(u):
                    k, v, t = u["kind"], u["v"], u["arg"]
                    blocks = blocks_of(u)
                    pe.wait_ge(S("probsT_lo"), G(l, u["g0"] + len(u["sizes"]) - 1) + 1)
                    if V(l, v) >= 1:
                        pe.wait_ge(S("out_read"), V(l, v))
                    if k == "mla_d":
                        pe.wait_ge(S("ds_lo"), l * NB + t + 1)
                    th, tl = PTh[v % 2], PTl[v % 2]
                    if k in ("mla", "mla2"):
                        for b in range(t + 2):
                            w, tile = (P, b - 1) if b else (META, 9)
                            c = slice(2 * P * b, 2 * P * (b + 1))
                            ins = three(OB[:, 0:2 * P], vh[0:w, tile, :], vl[0:w, tile, :], th[0:w, c], tl[0:w, c],
                                        b == 0, b == t + 1)
                    elif k.startswith("mla"):
                        out = OB[:, 0:P]
                        for b, (c0, w) in enumerate(blocks):
                            if k == "mla_d":
                                v1, v2 = dvh[t % 2][0:w, b, :], dvl[t % 2][0:w, b, :]
                            else:
                                v1, v2 = vh[0:w, 9, :], vl[0:w, 9, :]
                            ins = three(out, v1, v2, th[0:w, b * P:b * P + P], tl[0:w, b * P:b * P + P],
                                        b == 0, b == len(blocks) - 1)
                    elif k == "swa":
                        if t == 0:
                            all_split(pe, l, "B")
                        w = min(t, 2) * CH
                        for j in range(4):
                            out, d = OB[:, HD * j:HD * j + HD], slice(HD * (j // 2), HD * (j // 2) + HD)
                            if w:
                                three(out, th[0:w, j * P:j * P + P], tl[0:w, j * P:j * P + P],
                                      VFh[0:w, t, d], VFl[0:w, t, d], True, False)
                            e = 512 + j * P
                            ins = three(out, th[0:CH + META, e:e + P], tl[0:CH + META, e:e + P],
                                        VXh[0:CH + META, t, d], VXl[0:CH + META, t, d], not w, True)
                    else:
                        if k == "swa_m":
                            pe.wait_ge(S("split_lo"), first[l, "B"] + 7)
                        out = OB[:, 0:P]
                        for b, (c0, w) in enumerate(blocks):
                            v1, v2 = (duh[t % 2][0:w, b, :], dul[t % 2][0:w, b, :]) if k == "swa_d" else (svmh[:, :], svml[:, :])
                            ins = three(out, th[0:w, b * P:b * P + P], tl[0:w, b * P:b * P + P], v1, v2,
                                        b == 0, b == len(blocks) - 1)
                    ins.then_inc(S("pv"), 1)

                def attend(units):
                    for n in range(len(units) + 2):
                        u = units[n] if n < len(units) else None
                        v = units[n - 1] if 1 <= n <= len(units) else None
                        w = units[n - 2] if n >= 2 else None
                        if u is not None and u["kind"] != "oa":
                            scores(u)
                        if v is not None and "a" in v:
                            turn_probs(v, range(min(2, len(v["sizes"]))))
                        if w is not None and "a" in w and w["closes"]:
                            values(w)
                        if v is not None and "a" in v:
                            turn_probs(v, range(2, len(v["sizes"])))
                        if u is not None and u["kind"] == "oa":
                            scores(u)

                attend(UB)
                barrier(pe, phase_no(l, "B"))
                attend(UE)
                barrier(pe, phase_no(l, "E"))

                def mix_T(t):
                    r = rows(t)
                    pe.wait_ge(S("c_mixn"), A(l, t) + 1)
                    if t >= 1:
                        pe.wait_ge(S("c_ml"), A(l, t - 1) + 1)
                    for k in range(KD):
                        ins = pe.transpose(Sb[0][:, k * P:k * P + r], mn[0:r, k * P:k * P + P], ident[0:r, 0:r])
                    ins.then_inc(S("c_mT"), 1)

                def w_out(t):
                    r = rows(t)
                    pe.wait_ge(S("c_ml"), A(l, t) + 1)
                    if t >= 2:
                        pe.wait_ge(S("c_res"), A(l, t - 2) + 1)
                    for k in range(KD):
                        if t == 0:
                            pe.wait_ge(S("split_lo"), first[l, "C"] + k + 1)
                        for c0 in (0, 512):
                            ins = three(YB[t % 2][0:r, c0:c0 + 512], mTh[t % 2][:, k, 0:r], mTl[t % 2][:, k, 0:r],
                                        wouth[:, k, c0:c0 + 512], woutl[:, k, c0:c0 + 512], k == 0, k == KD - 1)
                    ins.then_inc(S("c_y"), 1)

                def h1_T(t):
                    r = rows(t)
                    pe.wait_ge(S("ln_out"), qC(l, t) + 1)
                    if t >= 1:
                        pe.wait_ge(S("c_xl"), A(l, t - 1) + 1)
                    for k in range(KD):
                        ins = pe.transpose(Tb[k // 4][:, (k % 4) * P:(k % 4) * P + r], h1[0:r, k * P:k * P + P],
                                           ident[0:r, 0:r])
                    ins.then_inc(S("c_hT"), 1)

                mix_T(0)
                for n in range(TILES + 1):
                    if n + 1 < TILES:
                        mix_T(n + 1)
                    if n < TILES:
                        w_out(n)
                    if n >= 1:
                        h1_T(n - 1)
                barrier(pe, phase_no(l, "C"))

                def up_or_gate(j, c, which, first_turn):
                    k0 = TURN_ITEMS.index((1, c, which)) if not first_turn else None
                    slot = 2 * c + which
                    if first_turn:
                        pe.wait_ge(S("f_lo"), W_ITEMS * l + slot + 1)
                    else:
                        pe.wait_ge(S("f_lo"), j * 6 + (W_ITEMS * l + 4 - 6 + k0 + 1))
                    bank = u_bank if which else g_bank
                    for i in range(3):
                        if not (first_turn and c == 0):
                            pe.wait_ge(S("f_hid" if which else "f_silu"),
                                       j * 6 + (6 * TURNS * l + 3 * c + i - 3 + 1))
                        for k in range(KD):
                            ins = three(bank(i), fwh[slot][:, k, :], fwl[slot][:, k, :],
                                        xh[:, k, N0[i]:N0[i] + NT[i]], xl[:, k, N0[i]:N0[i] + NT[i]],
                                        k == 0, k == KD - 1)
                        ins.then_inc(S("f_up" if which else "f_gate"), 1)

                def down(j, last):
                    items = LAST_ITEMS if last else TURN_ITEMS
                    pe.wait_ge(S("f_lo"), j * 6 + (W_ITEMS * l + 4 + items.index((0, 1, 2)) + 1))
                    pe.wait_ge(S("f_hidl"), j * 6 + (6 * TURNS * l + 6))
                    for e in range(24):
                        k, i = e // 3, e % 3
                        if e >= 2:
                            pe.wait_ge(S("f_y"), j * 24 + (24 * TURNS * l + e - 1))
                        for c in range(2):
                            ins = three(Tb[e % 2][:, 0:NT[i]], fwh[4 + c][:, k, :], fwl[4 + c][:, k, :],
                                        hidh[c][:, N0[i]:N0[i] + NT[i]], hidl[c][:, N0[i]:N0[i] + NT[i]],
                                        c == 0, c == 1)
                        ins.then_inc(S("f_down"), 1)

                for c in range(2):
                    for which in range(2):
                        up_or_gate(0, c, which, True)
                with pe.Fori(1, TURNS) as j:
                    up_or_gate(j, 0, 0, False)
                    down(j - 1, False)
                    up_or_gate(j, 0, 1, False)
                    up_or_gate(j, 1, 0, False)
                    up_or_gate(j, 1, 1, False)
                down(TURNS - 1, True)
                barrier(pe, phase_no(l, "F"))

                for t in range(TILES):
                    r = rows(t)
                    if t >= 2:
                        pe.wait_ge(S("d_xo"), A(l, t - 2) + 1)
                    for k in range(KD):
                        ins = pe.transpose(Sb[t % 2][0:r, k * P:k * P + P], acc[:, k, cols(t)], ident[:, :])
                    ins.then_inc(S("d_T"), 1)
                barrier(pe, phase_no(l, "D"))


def kernel(x_prompt, x_sample, cache_mla_ckv, cache_mla_krope, cache_swa_k, cache_swa_v,
           meta_tokens, in_ln_g, in_ln_b, w_in, mla_q_norm_g, mla_w_uq, mla_kv_norm_g,
           mla_w_uk, mla_w_uv, swa_sinks, out_norm_mla_g, out_norm_swa_g, w_out,
           ln1_g, ln1_b, ffn_w_gate, ffn_w_up, ffn_w_down, ln2_g, ln2_b):
    import concourse.bacc as bacc
    from concourse.bass_utils import run_bass_kernel_spmd

    def C(a):
        return np.ascontiguousarray(a)

    def pair(g, b):
        return np.concatenate([g, b], axis=-1)

    pos = np.concatenate([META + np.arange(SEQ), np.tile(META + PAST + np.arange(NS), NB), np.arange(META)])
    parts = []
    for d in (HD, ROPE):
        inv = np.power(np.float32(10000.0), -(np.arange(d // 2, dtype=np.float32) * np.float32(2.0 / d)))
        ang = pos.astype(np.float32)[:, None] * inv[None, :].astype(np.float32)
        c, s = np.cos(ang), np.sin(ang)
        parts += [c, c, -s, s]
    rot = C(np.concatenate(parts, axis=1).astype(np.float32))

    sk = np.asarray(cache_swa_k).reshape(L, NB, WKEYS, KVH * HD)
    sinks = np.asarray(swa_sinks)
    lanes = np.arange(P)
    sink_rows = np.stack([sinks[:, 2 * j + lanes // CH] for j in range(4)] + [sinks[:, lanes // NS]], axis=-1)
    uq = np.asarray(mla_w_uq)
    gu = [np.asarray(w).reshape(L, KD, P, FC, P).transpose(0, 3, 2, 1, 4).reshape(L, FC, P, D)
          for w in (ffn_w_gate, ffn_w_up)]
    w_ff = np.stack(gu + [np.asarray(ffn_w_down).reshape(L, FC, P, D)], axis=2)
    arrays = {
        "X": np.concatenate([np.asarray(x_prompt)[0], np.asarray(x_sample).reshape(NB * NS, D),
                             np.asarray(meta_tokens)], axis=0),
        "LNP": np.concatenate([pair(in_ln_g, in_ln_b)[None], pair(ln2_g, ln2_b)], axis=0),
        "ROT": rot,
        "W_IN": np.asarray(w_in),
        "QKVG": pair(mla_q_norm_g, mla_kv_norm_g),
        "W_UQ": np.concatenate([uq[..., 0:64].reshape(L, QL, 512), uq[..., 64:96].reshape(L, QL, 256)], axis=-1),
        "W_UK": np.asarray(mla_w_uk).transpose(0, 2, 3, 1).reshape(L, HEADS * 64, LAT),
        "W_UV": np.asarray(mla_w_uv).reshape(L, LAT, HEADS * 64),
        "SINKS": sink_rows,
        "MIXG": pair(out_norm_mla_g, out_norm_swa_g),
        "W_OUT": np.asarray(w_out),
        "LN1": pair(ln1_g, ln1_b),
        "W_FF": w_ff,
        "CKVT": np.asarray(cache_mla_ckv).transpose(0, 1, 3, 2),
        "CKV": np.asarray(cache_mla_ckv),
        "KRT": np.asarray(cache_mla_krope).transpose(0, 1, 3, 2),
        "SKT": sk.transpose(0, 1, 3, 2),
        "SK": sk,
        "SV": np.asarray(cache_swa_v).reshape(L, NB, WKEYS, KVH * HD),
    }
    outs = {"H": (L + 1, TOK, D), "KVS": (L, TOK, KVW), "NSK": (L, NB, WKEYS, KVH * HD), "NSV": (L, NB, WKEYS, KVH * HD)}
    nc = bacc.Bacc("TRN2", target_bir_lowering=False, num_devices=1)
    feed, args = {}, []
    for name, a in arrays.items():
        feed[f"in_{name}"] = C(a)
        args.append(nc.dram_tensor(f"in_{name}", a.shape, F32, kind="ExternalInput").ap())
    for name, shape in outs.items():
        args.append(nc.dram_tensor(f"out_{name}", shape, F32, kind="ExternalOutput").ap())
    program(nc, *args)
    got = run_bass_kernel_spmd(nc, [feed], core_ids=[0]).results[0]
    h, kv, nk, nv = (np.asarray(got[f"out_{n}"]) for n in outs)

    meta, seq, smp = slice(METAROW, TOK), slice(0, SEQ), slice(SAMPLE, METAROW)
    k0, v0 = LAT + ROPE, LAT + ROPE + KVH * HD

    def prompt(c0, c1, n):
        return np.concatenate([kv[:, meta, c0:c1], kv[:, SEQ - n:SEQ, c0:c1]], axis=1)[:, None]

    def sample(c0, c1):
        return kv[:, smp, c0:c1].reshape(L, NB, NS, c1 - c0)

    def kvh(a):
        return a.reshape(a.shape[:-1] + (KVH, HD))

    return (h[L, seq][None], h[L, smp].reshape(NB, NS, D),
            prompt(0, LAT, SEQ), prompt(LAT, k0, SEQ), kvh(prompt(k0, v0, WIN)), kvh(prompt(v0, KVW, WIN)),
            sample(0, LAT), sample(LAT, k0), kvh(nk), kvh(nv))
```
